# Optimizing a Trainium2 kernel written in Bass

```python
import jax, jax.numpy as jnp
from jax import lax
import numpy as np

D_MODEL = 1024
BATCH = 1
SEQ = 256
DEPTH = 1

D_MIX = D_MODEL
ATTN_HEADS = 8
HEAD_DIM = 64
D_ATTN = ATTN_HEADS * HEAD_DIM
CONV_GROUPS = 8
D_CONV = D_MIX - D_ATTN
CONV_WIDTH = 3
IDX_HEADS = 8
IDX_DIM = 64
MAX_TOPK = 256
Q_BLOCK = 128
PEER_HEADS = 8
PEER_KEYS = 128
PEER_EXPERTS = PEER_KEYS * PEER_KEYS
PEER_HALF = 128
PEER_QDIM = 2 * PEER_HALF
PEER_TOPK = 16
EPS = 1e-6

SPLITS = [D_ATTN, D_ATTN, D_ATTN, D_CONV, D_CONV, D_CONV, IDX_HEADS * IDX_DIM, IDX_DIM, IDX_HEADS]
D_IN = sum(SPLITS)


def rms_norm(x, w):
    xf = x.astype(jnp.float32)
    y = xf * lax.rsqrt(jnp.mean(xf * xf, axis=-1, keepdims=True) + EPS)
    return (y * w.astype(jnp.float32)).astype(x.dtype)

def _gather_rows(t, idx):
    return jax.vmap(lambda tb, ib: tb[ib])(t, idx)

def dsa_attention(q, k, v, iq, ik, iw):
    B, L = q.shape[0], q.shape[1]
    topk = min(MAX_TOPK, L // 4)
    n_blocks = L // Q_BLOCK
    s_pos = jnp.arange(L)
    att_scale = HEAD_DIM ** -0.5
    idx_scale = (IDX_DIM ** -0.5) * (IDX_HEADS ** -0.5)

    def block_fn(blk):
        start = blk * Q_BLOCK
        qb = lax.dynamic_slice_in_dim(q, start, Q_BLOCK, axis=1)
        iqb = lax.dynamic_slice_in_dim(iq, start, Q_BLOCK, axis=1)
        iwb = lax.dynamic_slice_in_dim(iw, start, Q_BLOCK, axis=1)
        t_pos = start + jnp.arange(Q_BLOCK)
        rel = jax.nn.relu(jnp.einsum('bqhd,bsd->bqhs', iqb, ik).astype(jnp.float32))
        score = jnp.einsum('bqhs,bqh->bqs', rel, iwb.astype(jnp.float32)) * idx_scale
        causal = s_pos[None, None, :] <= t_pos[None, :, None]
        score = jnp.where(causal, score, -jnp.inf)
        _, sel = lax.top_k(score, topk)
        k_sel = _gather_rows(k, sel)
        v_sel = _gather_rows(v, sel)
        logits = jnp.einsum('bqhd,bqkhd->bhqk', qb, k_sel).astype(jnp.float32) * att_scale
        valid = (sel <= t_pos[None, :, None])[:, None, :, :]
        logits = jnp.where(valid, logits, -jnp.inf)
        p = jax.nn.softmax(logits, axis=-1).astype(v.dtype)
        o = jnp.einsum('bhqk,bqkhd->bqhd', p, v_sel)
        return o.reshape(B, Q_BLOCK, ATTN_HEADS * HEAD_DIM)

    out = lax.map(block_fn, jnp.arange(n_blocks))
    return out.transpose(1, 0, 2, 3).reshape(B, L, ATTN_HEADS * HEAD_DIM)

def short_conv(b_gate, c_gate, xc, conv_w, conv_b):
    L = xc.shape[1]
    u = c_gate * xc
    up = jnp.pad(u, ((0, 0), (CONV_WIDTH - 1, 0), (0, 0)))
    y = conv_b
    for j in range(CONV_WIDTH):
        y = y + conv_w[j] * up[:, j:j + L]
    return b_gate * y

def peer_ffn(h, peer_wq, peer_subkeys, peer_u, peer_v):
    B, L, D = h.shape
    n_blocks = L // Q_BLOCK
    hb_all = h.reshape(B, n_blocks, Q_BLOCK, D).transpose(1, 0, 2, 3)

    def block_fn(hb):
        q = (hb @ peer_wq).reshape(B, Q_BLOCK, PEER_HEADS, 2, PEER_HALF)
        s = jnp.einsum('bqhpd,hpnd->bqhpn', q, peer_subkeys).astype(jnp.float32)
        vals, idx = lax.top_k(s, PEER_TOPK)
        combo = vals[..., 0, :, None] + vals[..., 1, None, :]
        ids = idx[..., 0, :, None] * PEER_KEYS + idx[..., 1, None, :]
        combo = combo.reshape(B, Q_BLOCK, PEER_HEADS, PEER_TOPK * PEER_TOPK)
        ids = ids.reshape(B, Q_BLOCK, PEER_HEADS, PEER_TOPK * PEER_TOPK)
        top_s, pos = lax.top_k(combo, PEER_TOPK)
        expert = jnp.take_along_axis(ids, pos, axis=-1)
        g = jax.nn.softmax(top_s, axis=-1).astype(hb.dtype)
        u_sel = peer_u[expert]
        a = jax.nn.gelu(jnp.einsum('bqhkd,bqd->bqhk', u_sel, hb))
        v_sel = peer_v[expert]
        return jnp.einsum('bqhk,bqhkd->bqd', g * a, v_sel)

    out = lax.map(block_fn, hb_all)
    return out.transpose(1, 0, 2, 3).reshape(B, L, D)

def first_inputs(seed: int = 0) -> dict:
    key = jax.random.key(seed)
    ks = jax.random.split(key, 20)
    f32 = jnp.float32
    nrm = lambda k, shape, s: jax.random.normal(k, shape, f32) * s
    return {
        "x": nrm(ks[0], (BATCH, SEQ, D_MODEL), 1.0),
        "c": nrm(ks[1], (BATCH, D_MODEL), 1.0),
        "norm1_w": 1.0 + nrm(ks[2], (D_MODEL,), 0.02),
        "norm2_w": 1.0 + nrm(ks[3], (D_MODEL,), 0.02),
        "w_ada": nrm(ks[4], (D_MODEL, 6 * D_MODEL), D_MODEL ** -0.5),
        "b_ada": nrm(ks[5], (6 * D_MODEL,), 0.02),
        "w_in": nrm(ks[6], (D_MODEL, D_IN), D_MODEL ** -0.5),
        "q_norm_w": 1.0 + nrm(ks[7], (HEAD_DIM,), 0.02),
        "k_norm_w": 1.0 + nrm(ks[8], (HEAD_DIM,), 0.02),
        "conv_w": nrm(ks[9], (CONV_WIDTH, D_CONV), CONV_WIDTH ** -0.5),
        "conv_b": nrm(ks[10], (D_CONV,), 0.01),
        "attn_out_norm_w": 1.0 + nrm(ks[11], (D_ATTN,), 0.02),
        "conv_out_norm_w": 1.0 + nrm(ks[12], (D_CONV,), 0.02),
        "w_out": nrm(ks[13], (D_MIX, D_MODEL), D_MIX ** -0.5),
        "peer_wq": nrm(ks[14], (D_MODEL, PEER_HEADS * PEER_QDIM), D_MODEL ** -0.5),
        "peer_subkeys": nrm(ks[15], (PEER_HEADS, 2, PEER_KEYS, PEER_HALF), PEER_HALF ** -0.5),
        "peer_u": nrm(ks[16], (PEER_EXPERTS, D_MODEL), D_MODEL ** -0.5),
        "peer_v": nrm(ks[17], (PEER_EXPERTS, D_MODEL), PEER_HEADS ** -0.5),
    }

def first_block(x, c, norm1_w, norm2_w, w_ada, b_ada, w_in, q_norm_w, k_norm_w,
              conv_w, conv_b, attn_out_norm_w, conv_out_norm_w, w_out,
              peer_wq, peer_subkeys, peer_u, peer_v):
    B, L, _ = x.shape
    mod = jax.nn.silu(c) @ w_ada + b_ada
    shift1, scale1, gate1, shift2, scale2, gate2 = [m[:, None, :] for m in jnp.split(mod, 6, axis=-1)]

    for _ in range(DEPTH):
        h = rms_norm(x, norm1_w) * (1.0 + scale1) + shift1
        proj = h @ w_in
        offs = np.cumsum(SPLITS)[:-1].tolist()
        q, k, v, cb, cc, cx, iq, ik, iw = jnp.split(proj, offs, axis=-1)
        q = rms_norm(q.reshape(B, L, ATTN_HEADS, HEAD_DIM), q_norm_w)
        k = rms_norm(k.reshape(B, L, ATTN_HEADS, HEAD_DIM), k_norm_w)
        v = v.reshape(B, L, ATTN_HEADS, HEAD_DIM)
        iq = iq.reshape(B, L, IDX_HEADS, IDX_DIM)
        y_attn = dsa_attention(q, k, v, iq, ik, iw)
        y_conv = short_conv(cb, cc, cx, conv_w, conv_b)
        y_mix = jnp.concatenate([rms_norm(y_attn, attn_out_norm_w),
                                 rms_norm(y_conv, conv_out_norm_w)], axis=-1)
        x = x + gate1 * (y_mix @ w_out)
        h2 = rms_norm(x, norm2_w) * (1.0 + scale2) + shift2
        x = x + gate2 * peer_ffn(h2, peer_wq, peer_subkeys, peer_u, peer_v)
    return x


GRID_W = 64
CTX_LEN = 256
RET_HEADS = 4
RET_DK = 256
RET_DV = 512
RET_CHUNK = 128
FOURIER_GROUPS = 4
FOURIER_DG = 256
D_FF = 2816
ROPE_BASE = 10000.0
N_MOD = 9

RET_QK = RET_HEADS * RET_DK
RET_V = RET_HEADS * RET_DV
FOURIER_W = FOURIER_GROUPS * FOURIER_DG
IN_COLS = 2 * RET_QK + 2 * RET_V + FOURIER_W + 2 * D_MODEL
SPLITS_2 = (RET_QK, 2 * RET_QK, 2 * RET_QK + RET_V, 2 * RET_QK + 2 * RET_V,
          2 * RET_QK + 2 * RET_V + FOURIER_W, 2 * RET_QK + 2 * RET_V + FOURIER_W + D_MODEL)


def rmsnorm(x, w):
    xf = x.astype(jnp.float32)
    y = xf * lax.rsqrt(jnp.mean(xf * xf, axis=-1, keepdims=True) + EPS)
    return (y * w.astype(jnp.float32)).astype(x.dtype)

def modulate(h, shift, scale):
    return h * (1 + scale) + shift

def swiglu(h, w13, w2):
    a, b = jnp.split(h @ w13, 2, axis=-1)
    return (jax.nn.silu(a) * b) @ w2

def heads(a, dh):
    B, L, _ = a.shape
    return a.reshape(B, L, -1, dh).transpose(0, 2, 1, 3)

def project(h, w_in):
    u = h @ w_in
    q, k, v, g, f, ga, gf = jnp.split(u, SPLITS_2, axis=-1)
    q = heads(q, RET_DK).astype(jnp.float32) * (RET_DK ** -0.5)
    k = heads(k, RET_DK).astype(jnp.float32)
    v = heads(v, RET_DV).astype(jnp.float32)
    return q, k, v, g, f, ga, gf

def rope_2d(a, rows):
    row = jnp.repeat(jnp.arange(rows, dtype=jnp.float32), GRID_W)
    col = jnp.tile(jnp.arange(GRID_W, dtype=jnp.float32), rows)
    n_freq = RET_DK // 4
    inv = ROPE_BASE ** (-jnp.arange(n_freq, dtype=jnp.float32) / n_freq)
    ang = jnp.concatenate([row[:, None] * inv, col[:, None] * inv], axis=-1)
    cos, sin = jnp.cos(ang), jnp.sin(ang)
    a1, a2 = a[..., 0::2], a[..., 1::2]
    return jnp.stack([a1 * cos - a2 * sin, a1 * sin + a2 * cos], axis=-1).reshape(a.shape)

def retention_scan(q, k, v, log_gamma, s0):
    B, H, L, dk = q.shape
    dv = v.shape[-1]
    C = RET_CHUNK
    n = L // C
    idx = jnp.arange(C, dtype=jnp.float32)
    lg = log_gamma[:, None]
    diff = idx[:, None] - idx[None, :]
    decay_intra = jnp.where(diff >= 0, jnp.exp(lg[:, :, None] * jnp.maximum(diff, 0.0)), 0.0)
    xi = jnp.exp(lg * (idx + 1.0))
    zeta = jnp.exp(lg * (C - 1.0 - idx))
    g_chunk = jnp.exp(log_gamma * C)

    def to_chunks(a):
        return jnp.moveaxis(a.reshape(B, H, n, C, a.shape[-1]), 2, 0)

    def step(s, qkv):
        qc, kc, vc = qkv
        sc = jnp.einsum('bhid,bhjd->bhij', qc, kc) * decay_intra
        o = (jnp.einsum('bhij,bhjv->bhiv', sc, vc)
             + jnp.einsum('bhid,bhdv->bhiv', qc, s) * xi[None, :, :, None])
        s = s * g_chunk[None, :, None, None] + jnp.einsum('bhjd,bhjv->bhdv', kc * zeta[None, :, :, None], vc)
        return s, o

    s, o = lax.scan(step, s0, (to_chunks(q), to_chunks(k), to_chunks(v)))
    o = jnp.moveaxis(o, 0, 2).reshape(B, H, L, dv)
    return o, s

def bidir_retention(q, k, v, lg_f, lg_b, s_f0, s_b0):
    o_f, s_f = retention_scan(q, k, v, lg_f, s_f0)
    flip = lambda a: jnp.flip(a, axis=2)
    o_b, s_b = retention_scan(flip(q), flip(k), flip(v), lg_b, s_b0)
    return o_f + flip(o_b), s_f, s_b

def retention_out(o, g, gn_w, p_ret):
    mu = jnp.mean(o, axis=-1, keepdims=True)
    var = jnp.mean(jnp.square(o - mu), axis=-1, keepdims=True)
    on = (o - mu) * lax.rsqrt(var + EPS)
    B, H, L, dv = o.shape
    on = on.transpose(0, 2, 1, 3).reshape(B, L, H * dv).astype(g.dtype) * gn_w
    return (jax.nn.silu(g) * on) @ p_ret

def fourier_branch(f, p_four):
    B, L, _ = f.shape
    fg = f.reshape(B, L, FOURIER_GROUPS, FOURIER_DG).astype(jnp.float32)
    mixed = jnp.fft.fft2(fg, axes=(1, 3), norm="ortho").real
    return mixed.reshape(B, L, FOURIER_W).astype(f.dtype) @ p_four

def merge(r, fo, ga, gf, w_out):
    return (jax.nn.sigmoid(ga) * r + jax.nn.sigmoid(gf) * fo) @ w_out

def second_inputs(seed: int = 0) -> dict:
    key = jax.random.key(seed)
    ks = jax.random.split(key, 24)

    def w(k, shape, fan_in, scale=1.0):
        return jax.random.normal(k, shape, jnp.float32) * (scale * fan_in ** -0.5)

    def gain(k, shape):
        return 1.0 + 0.02 * jax.random.normal(k, shape, jnp.float32)

    decay_base = jnp.asarray(np.log(2.0 ** (5 + np.arange(RET_HEADS)) - 1.0).astype(np.float32))
    return {
        "x": jax.random.normal(ks[0], (BATCH, SEQ, D_MODEL), jnp.float32),
        "c": jax.random.normal(ks[1], (BATCH, D_MODEL), jnp.float32),
        "ctx": jax.random.normal(ks[2], (BATCH, CTX_LEN, D_MODEL), jnp.float32),
        "c_ctx": 0.5 * jax.random.normal(ks[3], (D_MODEL,), jnp.float32),
        "w_ada": w(ks[4], (DEPTH, D_MODEL, N_MOD * D_MODEL), D_MODEL, 0.5),
        "b_ada": 0.02 * jax.random.normal(ks[5], (DEPTH, N_MOD * D_MODEL), jnp.float32),
        "norm_ffn1": gain(ks[6], (DEPTH, D_MODEL)),
        "w13_ffn1": w(ks[7], (DEPTH, D_MODEL, 2 * D_FF), D_MODEL),
        "w2_ffn1": w(ks[8], (DEPTH, D_FF, D_MODEL), D_FF),
        "norm_mix": gain(ks[9], (DEPTH, D_MODEL)),
        "w_in": w(ks[10], (DEPTH, D_MODEL, IN_COLS), D_MODEL),
        "decay_fwd": decay_base[None, :] + 0.05 * jax.random.normal(ks[11], (DEPTH, RET_HEADS), jnp.float32),
        "decay_bwd": decay_base[None, :] + 0.05 * jax.random.normal(ks[12], (DEPTH, RET_HEADS), jnp.float32),
        "ret_gn_w": gain(ks[13], (DEPTH, RET_V)),
        "p_ret": w(ks[14], (DEPTH, RET_V, D_MODEL), RET_V),
        "p_four": w(ks[15], (DEPTH, FOURIER_W, D_MODEL), FOURIER_W),
        "w_out": w(ks[16], (DEPTH, D_MODEL, D_MODEL), D_MODEL),
        "norm_ffn2": gain(ks[17], (DEPTH, D_MODEL)),
        "w13_ffn2": w(ks[18], (DEPTH, D_MODEL, 2 * D_FF), D_MODEL),
        "w2_ffn2": w(ks[19], (DEPTH, D_FF, D_MODEL), D_FF),
        "norm_final": gain(ks[20], (D_MODEL,)),
    }

def second_block(x, c, ctx, c_ctx, w_ada, b_ada, norm_ffn1, w13_ffn1, w2_ffn1, norm_mix, w_in,
              decay_fwd, decay_bwd, ret_gn_w, p_ret, p_four, w_out, norm_ffn2, w13_ffn2, w2_ffn2,
              norm_final):
    B, L, _ = x.shape
    rows = L // GRID_W
    for l in range(DEPTH):
        last = l == DEPTH - 1
        mod_x = (jax.nn.silu(c) @ w_ada[l] + b_ada[l])[:, None, :]
        mod_c = (jax.nn.silu(c_ctx) @ w_ada[l] + b_ada[l])[None, None, :]
        sh1x, sc1x, g1x, sh2x, sc2x, g2x, sh3x, sc3x, g3x = jnp.split(mod_x, N_MOD, axis=-1)
        sh1c, sc1c, g1c, sh2c, sc2c, g2c, sh3c, sc3c, g3c = jnp.split(mod_c, N_MOD, axis=-1)

        x = x + 0.5 * g1x * swiglu(modulate(rmsnorm(x, norm_ffn1[l]), sh1x, sc1x), w13_ffn1[l], w2_ffn1[l])
        ctx = ctx + 0.5 * g1c * swiglu(modulate(rmsnorm(ctx, norm_ffn1[l]), sh1c, sc1c), w13_ffn1[l], w2_ffn1[l])

        lg_f = jax.nn.log_sigmoid(decay_fwd[l].astype(jnp.float32))
        lg_b = jax.nn.log_sigmoid(decay_bwd[l].astype(jnp.float32))

        qc, kc, vc, gc, fc, gac, gfc = project(modulate(rmsnorm(ctx, norm_mix[l]), sh2c, sc2c), w_in[l])
        zero = jnp.zeros((ctx.shape[0], RET_HEADS, RET_DK, RET_DV), jnp.float32)
        o_c, s_f, s_b = bidir_retention(qc, kc, vc, lg_f, lg_b, zero, zero)

        qx, kx, vx, gx, fx, gax, gfx = project(modulate(rmsnorm(x, norm_mix[l]), sh2x, sc2x), w_in[l])
        qx = rope_2d(qx, rows)
        kx = rope_2d(kx, rows)
        o_x, _, _ = bidir_retention(qx, kx, vx, lg_f, lg_b, s_f, s_b)
        y_x = merge(retention_out(o_x, gx, ret_gn_w[l], p_ret[l]), fourier_branch(fx, p_four[l]), gax, gfx, w_out[l])
        x = x + g2x * y_x

        x = x + 0.5 * g3x * swiglu(modulate(rmsnorm(x, norm_ffn2[l]), sh3x, sc3x), w13_ffn2[l], w2_ffn2[l])

        if not last:
            y_c = merge(retention_out(o_c, gc, ret_gn_w[l], p_ret[l]), fourier_branch(fc, p_four[l]), gac, gfc, w_out[l])
            ctx = ctx + g2c * y_c
            ctx = ctx + 0.5 * g3c * swiglu(modulate(rmsnorm(ctx, norm_ffn2[l]), sh3c, sc3c), w13_ffn2[l], w2_ffn2[l])
    return rmsnorm(x, norm_final)


def setup_inputs(seed=0):
    out = dict(first_inputs(seed))
    for name, value in second_inputs(seed + 1).items():
        if name != "x":
            out[name + "_2"] = value
    return out


def reference(
    x, c, norm1_w, norm2_w, w_ada, b_ada, w_in, q_norm_w, k_norm_w, conv_w, conv_b,
    attn_out_norm_w, conv_out_norm_w, w_out, peer_wq, peer_subkeys, peer_u, peer_v, c_2, ctx_2,
    c_ctx_2, w_ada_2, b_ada_2, norm_ffn1_2, w13_ffn1_2, w2_ffn1_2, norm_mix_2, w_in_2,
    decay_fwd_2, decay_bwd_2, ret_gn_w_2, p_ret_2, p_four_2, w_out_2, norm_ffn2_2, w13_ffn2_2,
    w2_ffn2_2, norm_final_2,
):
    x = first_block(
        x, c, norm1_w, norm2_w, w_ada, b_ada, w_in, q_norm_w, k_norm_w, conv_w, conv_b,
        attn_out_norm_w, conv_out_norm_w, w_out, peer_wq, peer_subkeys, peer_u, peer_v,
    )
    return second_block(
        x, c_2, ctx_2, c_ctx_2, w_ada_2, b_ada_2, norm_ffn1_2, w13_ffn1_2, w2_ffn1_2,
        norm_mix_2, w_in_2, decay_fwd_2, decay_bwd_2, ret_gn_w_2, p_ret_2, p_four_2, w_out_2,
        norm_ffn2_2, w13_ffn2_2, w2_ffn2_2, norm_final_2,
    )


_drawn_inputs = setup_inputs


def setup_inputs(seed=0):
    import zlib

    import numpy as np

    out = dict(_drawn_inputs(seed))
    spreads = {}
    factors = {'norm2_w': 3.5,
     'q_norm_w': 8.0,
     'k_norm_w': 8.0,
     'conv_b': 8.0,
     'attn_out_norm_w': 3.962,
     'conv_out_norm_w': 4.451,
     'c_ctx_2': 5.199,
     'b_ada_2': 3.814,
     'norm_ffn1_2': 8.0,
     'norm_mix_2': 8.0,
     'decay_bwd_2': 21.36,
     'ret_gn_w_2': 26.01,
     'norm_ffn2_2': 30.93,
     'norm_final_2': 7.905}
    for name, (base, spread) in spreads.items():
        noise = np.random.default_rng([zlib.crc32(name.encode()), seed]).standard_normal(out[name].shape)
        drawn = base * np.exp(spread * noise) if base else spread * noise
        out[name] = __import__('jax').numpy.asarray(drawn.astype(out[name].dtype))
    for name, factor in factors.items():
        out[name] = (out[name] * factor).astype(out[name].dtype)
    return out
```

```python
from contextlib import ExitStack

import numpy as np

import concourse.bass as bass
from concourse import mybir

ALU = mybir.AluOpType
ACT = mybir.ActivationFunctionType
F32 = mybir.dt.float32
U32 = mybir.dt.uint32
AX_X = mybir.AxisListType.X

P = 128
D = 1024
KD = D // P
L = 256
NT = L // P
EPS = 1e-6
BANKS = 8
BANK = 512

HEADS, HD = 8, 64
ATT = HEADS * HD
KA = ATT // P
TOPK = L // 4
PH, PK, PSEL = 8, 128, 16
EXPERTS = PK * PK
SLOTS = PH * PSEL
ATT_SCALE = HD ** -0.5
IDX_SCALE = (64 ** -0.5) * (8 ** -0.5)
FILL, TAKEN = -3.0e38, -3.2e38
MASKED = -1.0e30

RH, DK, DV = 4, 256, 512
FF = 2816
KF = FF // P
FG = 4
RING = 4
SLAB = 4096
GBUF = 8
ROW = 2 * D
BATCH = 2
ROUND = 16

PARAMS = [("c", 8), ("c2", 16), ("b_ada", 48), ("b_ada_2", 72), ("norm1_w", 8), ("norm2_w", 8), ("q_norm_w", 1),
          ("k_norm_w", 1), ("conv_w", 12), ("conv_b", 4), ("attn_out_norm_w", 4), ("conv_out_norm_w", 4),
          ("norm_ffn1_2", 8), ("norm_mix_2", 8), ("ret_gn_w_2", 16), ("norm_ffn2_2", 8), ("norm_final_2", 8),
          ("decay", 8)]
EARLY = [("ident", P), ("pair", P), ("causal", NT * L), ("iota16", PSEL), ("age", 2 * NT)]
LATE_DECAY = 2 * NT * L * 2
LATE_DFT = 2 * 2 * 256
LATE_ROPE = 2 * L
LATE_XI = 2 * L


def offsets(table):
    at, out = 0, {}
    for name, width in table:
        out[name] = (at, width)
        at += width
    return out, at


PARAM_AT, PARAM_W = offsets(PARAMS)
EARLY_AT, EARLY_W = offsets(EARLY)


def shape_constants():
    tok = np.arange(L)
    causal = (tok[None, :] <= tok[:, None]).astype(np.float32).reshape(NT, P, L).transpose(1, 0, 2)
    pair = (np.arange(P)[:, None] // HD == np.arange(P)[None, :] // HD).astype(np.float32)
    age = np.stack([L - 1 - tok.reshape(NT, P), tok.reshape(NT, P)]).transpose(2, 0, 1).astype(np.float32)
    iota16 = np.broadcast_to(np.arange(PSEL, dtype=np.float32), (P, PSEL))
    early = np.concatenate([np.eye(P, dtype=np.float32), pair, causal.reshape(P, -1), iota16, age.reshape(P, -1)], 1)
    diff = (tok[None, :] - tok[:, None]).astype(np.float32)
    decay = np.stack([np.maximum(diff, 0), np.maximum(-diff, 0), diff >= 0, diff <= 0]).astype(np.float32)
    decay = decay.reshape(4, NT, P, L).transpose(2, 0, 1, 3).reshape(P, -1)
    ang = 2 * np.pi * (np.outer(np.arange(256), np.arange(256)) % 256) / 256
    dft = (np.concatenate([np.cos(ang), np.sin(ang)], 1) / 16).astype(np.float32)
    dft = dft.reshape(2, P, 512).transpose(1, 0, 2).reshape(P, -1)
    inv = (np.float32(10000.0) ** (-np.arange(64, dtype=np.float32) / 64)).astype(np.float32)
    row, col = (tok // 64).astype(np.float32), (tok % 64).astype(np.float32)
    turn = np.concatenate([inv[:, None] * row[None, :], inv[:, None] * col[None, :]], 0).astype(np.float32)
    rope = np.concatenate([np.cos(turn), np.sin(turn)], 1).astype(np.float32)
    xi = np.broadcast_to(np.concatenate([tok + 1, L - tok]).astype(np.float32), (P, 2 * L))
    late = np.concatenate([decay, dft, rope, xi], 1)
    return np.ascontiguousarray(early), np.ascontiguousarray(late)


def slab_order():
    ada = [("w_ada", i, SLAB) for i in range(12)]
    ffn = lambda n: [(f"w13_ffn{n}", i, SLAB) for i in range(11)] + [(f"w2_ffn{n}", i, KF * P) for i in range(8)]
    w_in_2 = {"q": (0, 2), "k": (2, 4), "v": (4, 8), "g": (8, 12), "f": (12, 14), "ga": (14, 16), "gf": (16, 18)}
    proj = lambda n: [("w_in_2", i, SLAB) for i in range(*w_in_2[n])]
    first = (ada[:4] + [("w_idx", 0, KD * 136)] + [("w_in", i, SLAB) for i in range(7)] + ada[4:]
             + [("w_out", i, SLAB) for i in range(2)] + [("peer_wq", i, SLAB) for i in range(4)]
             + [("subkeys", 0, 2 * PH * PK)])
    context = [("w_ada_2", i, SLAB) for i in range(18)] + ffn(1) + proj("k") + proj("v")
    second = (ffn(1) + proj("gf") + proj("f") + [("p_four", i, SLAB) for i in range(2)] + proj("ga") + proj("q")
              + proj("k") + proj("v") + proj("g") + [("p_ret", i, SLAB) for i in range(4)]
              + [("w_out_2", i, SLAB) for i in range(2)] + ffn(2))
    return first + context + second, len(first) + len(context)


def program(nc, dram, out):
    slabs, second_at = slab_order()
    with ExitStack() as ctx:
        def sb(name, width, dt=F32):
            return ctx.enter_context(nc.sbuf_tensor(name, [P, width], dt))

        sems = {}

        def sem(name):
            if name not in sems:
                sems[name] = ctx.enter_context(nc.semaphore(name))
            return sems[name]

        psum = ctx.enter_context(nc.psum_tensor("psum", [P, BANKS, BANK], F32))
        ring = sb("ring", RING * SLAB)
        x_t = sb("x_t", KD * L)[:].rearrange("p (k t) -> p k t", k=KD)
        h_t = sb("h_t", KD * L)[:].rearrange("p (k t) -> p k t", k=KD)
        prm = sb("prm", PARAM_W)
        early = sb("early", EARLY_W)
        ones = sb("ones", P)
        mod1 = sb("mod1", 48)
        mod2 = sb("mod2", 144)
        mod2_v = mod2[:].rearrange("p (m k s) -> p m k s", m=9, s=2)
        cols = sb("cols", 160)
        rstd = sb("rstd", L)
        arena = sb("arena", 27648)
        small = sb("small", 2600)
        ids = sb("ids", NT * SLOTS, U32)
        idx_stage = sb("idx_stage", ROUND, U32)
        found = sb("found", 2 * PH * PSEL, U32)
        place = sb("place", SLOTS, U32)

        def param(name):
            at, w = PARAM_AT[name]
            return prm[:, at:at + w]

        def const(name):
            at, w = EARLY_AT[name]
            return early[:, at:at + w]

        ident = const("ident")

        silu_c, silu_c2 = cols[:, 0:8], cols[:, 8:24]
        scale_of = {}
        for i, key in enumerate(("n1", "n2", "ctx1", "ctx2", "x1", "x2", "x3")):
            scale_of[key] = cols[:, 24 + 8 * i:32 + 8 * i]
        half_gate = {"ctx1": cols[:, 80:88], "x1": cols[:, 88:96], "x3": cols[:, 96:104]}
        lg = cols[:, 104:112]
        lg_e, lg_z, lg_z2, lg_s = (cols[:, 112 + 8 * i:120 + 8 * i] for i in range(4))
        fade = cols[:, 144:160]

        ctx_t = arena[:, 0:2048].rearrange("p (k t) -> p k t", k=KD)
        h2 = arena[:, 2048:4096].rearrange("p (t d) -> p t d", t=NT)
        y_acc = arena[:, 4096:5120]
        y_of = [y_acc, h2[:, 0, :]]
        F0, G0 = 5120, 11264
        iq_t = arena[:, G0:G0 + 1024].rearrange("p (j t) -> p j t", j=4)
        ik_t = arena[:, G0 + 1024:G0 + 1280]
        idx = arena[:, G0 + 1280:G0 + 1792].rearrange("p (t s) -> p t s", t=NT)
        fill = arena[:, G0 + 1792:G0 + 2304].rearrange("p (t s) -> p t s", t=NT)
        bias = arena[:, G0 + 2304:G0 + 2816].rearrange("p (t s) -> p t s", t=NT)
        relu = arena[:, G0 + 2816:G0 + 3840].rearrange("p (b s) -> p b s", b=4)
        q_t = arena[:, G0 + 3840:G0 + 4864].rearrange("p (j t) -> p j t", j=KA)
        k_t = arena[:, G0 + 4864:G0 + 5888].rearrange("p (j t) -> p j t", j=KA)
        raw = arena[:, G0 + 5888:G0 + 7936].rearrange("p (a j t) -> p a j t", a=2, j=KA)
        raw_sq = arena[:, G0 + 7936:G0 + 9984].rearrange("p (a j t) -> p a j t", a=2, j=KA)
        y_mix = arena[:, G0 + 5888:G0 + 7936].rearrange("p (k t) -> p k t", k=KD)
        v_n = arena[:, G0 + 9984:G0 + 11008].rearrange("p (t d) -> p t d", t=NT)
        padded = arena[:, G0 + 11008:G0 + 12040].rearrange("p (j t) -> p j t", j=KA)
        y_conv = arena[:, G0 + 12040:G0 + 13064].rearrange("p (j t) -> p j t", j=KA)
        sq1 = arena[:, G0 + 13064:G0 + 15112].rearrange("p (k t) -> p k t", k=KD)
        gate_c = arena[:, 4096:5120].rearrange("p (j t) -> p j t", j=KA)
        p_t0 = arena[:, F0:F0 + 1024].rearrange("p (h q) -> p h q", h=HEADS)
        p_t1 = arena[:, F0 + 1024:F0 + 3072].rearrange("p (h s q) -> p h s q", h=HEADS, s=2)
        probs = arena[:, F0 + 3072:F0 + 5120].rearrange("p (h s) -> p h s", h=HEADS)
        y_att = arena[:, F0 + 5120:F0 + 6144].rearrange("p (j t) -> p j t", j=KA)
        pq_t = arena[:, G0:G0 + 4096].rearrange("p (h t) -> p h t", h=2 * PH)
        key_s = arena[:, F0:F0 + 4096].rearrange("p (t h n) -> p t h n", t=NT, h=2 * PH)
        combo = arena[:, F0 + 4096:F0 + 6144].rearrange("p (h n) -> p h n", h=PH)
        pick = h_t
        rows = [arena[:, G0 + i * ROW:G0 + (i + 1) * ROW] for i in range(GBUF)]
        top_v = small[:, 0:256].rearrange("p (h n) -> p h n", h=2 * PH)
        top_i = small[:, 256:512].rearrange("p (h n) -> p h n", h=2 * PH)
        best = small[:, 512:768].rearrange("p (t h n) -> p t h n", t=NT, h=PH)
        half_i = small[:, 768:1024]
        half_id = small[:, 1024:1280]
        id_f = small[:, 1280:1408]
        hsum = small[:, 1408:1424]
        dots = small[:, 1424:1424 + 16].rearrange("p (b n) -> p b n", b=8)
        acts = small[:, 1440:1456].rearrange("p (b n) -> p b n", b=8)
        weights = small[:, 1456:1472].rearrange("p (b n) -> p b n", b=8)
        max8 = small[:, 1472:1480]
        stat = small[:, 1480:1496]
        mxs = small[:, 1496:1504]
        iw = small[:, 1504:1520].rearrange("p (t h) -> p t h", t=NT)
        xi = small[:, 1536:2048].rearrange("p (a t) -> p a t", a=2)
        rope_tmp = small[:, 2048:2560].rearrange("p (b t) -> p b t", b=2)
        hid = arena[:, F0:F0 + KF * L].rearrange("p (k t) -> p k t", k=KF)
        kc = arena[:, F0:F0 + 2048].rearrange("p (t n) -> p t n", t=NT)
        vc = arena[:, F0 + 2048:F0 + 6144].rearrange("p (t n) -> p t n", t=NT)
        k_fade = [h_t[:, 2 * i:2 * i + 2, :] for i in range(4)]
        state = arena[:, G0 + 8192:G0 + 16384].rearrange("p (h a b v) -> p h a b v", h=RH, a=2, b=2)
        late_decay = arena[:, G0 + 2048:G0 + 4096].rearrange("p (m t i) -> p m t i", m=4, t=NT)
        decay_t = arena[:, 0:2048].rearrange("p (h t i) -> p h t i", h=RH, t=NT)
        sq2 = arena[:, G0:G0 + 2048].rearrange("p (k t) -> p k t", k=KD)
        sig = arena[:, 2048:4096].rearrange("p (k t) -> p k t", k=KD)
        rope = arena[:, 4096:4608].rearrange("p (a t) -> p a t", a=2)
        late_xi = arena[:, 4608:5120].rearrange("p (a t) -> p a t", a=2)
        f_t = arena[:, F0:F0 + 2048].rearrange("p (k t) -> p k t", k=KD)
        mixed = arena[:, F0 + 2048:F0 + 4096].rearrange("p (k t) -> p k t", k=KD)
        m_t = arena[:, F0 + 4096:F0 + 6144].rearrange("p (k t) -> p k t", k=KD)
        dft_z = arena[:, G0:G0 + 4096].rearrange("p (t g a c) -> p t g a c", t=NT, g=FG, a=2)
        dft = arena[:, G0 + 4096:G0 + 5120].rearrange("p (k a c) -> p k a c", k=2, a=2)
        rq_t = arena[:, G0:G0 + 2048].rearrange("p (k t) -> p k t", k=KD)
        rk_t = arena[:, G0 + 2048:G0 + 4096].rearrange("p (k t) -> p k t", k=KD)
        rv = arena[:, F0:F0 + 4096].rearrange("p (t n) -> p t n", t=NT)
        rg_t = arena[:, G0 + 4096:G0 + 8192].rearrange("p (k t) -> p k t", k=16)
        q_faded = h_t[:, 0:4, :].rearrange("p (a k) t -> p a k t", a=2)
        sc_t = h_t[:, 4:6, :]
        o_n = h_t[:, 6:8, :].rearrange("p a t -> p (a t)")

        group_done = sem("group_done")
        drained = {"act": sem("act_drained"), "dve": sem("dve_drained")}
        landed = [sem(f"slab_landed{i}") for i in range(RING)]
        row_landed = [sem(f"row_landed{i}") for i in range(GBUF)]

        groups, index, turn = [], {}, {"act": 0, "dve": 0}
        slab_free = []

        def emptied(name):
            _, who, count = groups[index[name]]
            return drained[who], count

        block = ctx.enter_context(nc.Block())

        @block.tensor
        def _(pe):
            def begin(name, who):
                i = len(groups)
                if i >= BANKS:
                    pe.wait_ge(drained[groups[i - BANKS][1]], groups[i - BANKS][2])
                count = 1 + sum(g[1] == who for g in groups)
                groups.append((name, who, count))
                index[name] = i
                return psum[:, i % BANKS, :]

            def end(ins):
                ins.then_inc(group_done, 1)

            used = [0]

            def next_slab(name, i):
                n = used[0]
                assert slabs[n][:2] == (name, i), (slabs[n], name, i)
                used[0] += 1
                pe.wait_ge(landed[n % RING], 16 * (n // RING + 1))
                at = (n % RING) * SLAB
                return ring[:, at:at + slabs[n][2]]

            def release():
                slab_free.append(len(groups))

            def mm(o, a, b, first, last):
                return nc.tensor.matmul(o, a, b, start=first, stop=last)

            def by_feature(tag, array, ids_, src, who, kb=KD, after=None):
                n = 0
                for i in ids_:
                    w = next_slab(array, i).rearrange("p (k n) -> p k n", k=kb)
                    width = w.shape[2]
                    for b in range(0, width // P, 2):
                        o = begin(f"{tag}{n}", who(n) if callable(who) else who)
                        n += 1
                        for j in range(2):
                            for k in range(kb):
                                last = mm(o[:, j * L:(j + 1) * L], w[:, k, (b + j) * P:(b + j + 1) * P], src[:, k, :],
                                          k == 0, k == kb - 1)
                        end(last)
                    release()

            def by_token(tag, array, ids_, src, who):
                n = 0
                for i in ids_:
                    w = next_slab(array, i).rearrange("p (k n) -> p k n", k=KD)
                    for t in range(NT):
                        o = begin(f"{tag}{n}", who)
                        n += 1
                        for k in range(KD):
                            last = mm(o[:, 0:BANK], src[:, k, t * P:(t + 1) * P], w[:, k, :], k == 0, k == KD - 1)
                        end(last)
                    release()

            def squares(tag, sq, kb):
                pe.wait_ge(sem("sq_" + tag), 1)
                o = begin("ss_" + tag, "dve")
                for k in range(kb):
                    last = mm(o[:, 0:L], ones[:], sq[:, k, :], k == 0, k == kb - 1)
                end(last)

            def modulation(tag, array, ids_, src, width):
                for i in ids_:
                    w = next_slab(array, i).rearrange("p (k n) -> p k n", k=KD)
                    o = begin(f"{tag}{i}", "act")
                    for j in range(4):
                        for k in range(KD):
                            last = mm(o[:, j * width:(j + 1) * width], w[:, k, j * P:(j + 1) * P],
                                      src[:, k * width:(k + 1) * width], k == 0, k == KD - 1)
                    end(last)
                    release()

            def feed_forward(tag, n, src):
                for i in range(11):
                    w = next_slab(f"w13_ffn{n}", i).rearrange("p (k n) -> p k n", k=KD)
                    for half, who in ((0, "act"), (1, "dve")):
                        o = begin(f"{tag}_{'ab'[half]}{i}", who)
                        for j in range(2):
                            c = half * 256 + j * P
                            for k in range(KD):
                                last = mm(o[:, j * L:(j + 1) * L], w[:, k, c:c + P], src[:, k, :], k == 0, k == KD - 1)
                        end(last)
                    release()
                pe.wait_ge(*emptied(f"{tag}_b10"))
                for i in range(8):
                    w = next_slab(f"w2_ffn{n}", i).rearrange("p (k n) -> p k n", k=KF)
                    o = begin(f"{tag}_y{i}", "dve")
                    for k in range(KF):
                        last = mm(o[:, 0:L], w[:, k, :], hid[:, k, :], k == 0, k == KF - 1)
                    end(last)
                    release()

            pe.wait_ge(sem("ones"), 1)
            pe.wait_ge(sem("params"), 48)
            pe.wait_ge(sem("silu_c"), 2)
            modulation("ada", "w_ada", range(4), silu_c, 1)
            squares("n1", sq1, KD)
            pe.wait_ge(sem("h_n1"), 1)
            w = next_slab("w_idx", 0).rearrange("p (k n) -> p k n", k=KD)
            o = begin("ik", "act")
            for k in range(KD):
                last = mm(o[:, 0:L], w[:, k, 0:P], h_t[:, k, :], k == 0, k == KD - 1)
            end(last)
            o = begin("iw", "act")
            for t in range(NT):
                for k in range(KD):
                    last = mm(o[:, t * 8:t * 8 + 8], h_t[:, k, t * P:(t + 1) * P], w[:, k, P:P + 8], k == 0, k == KD - 1)
            end(last)
            release()
            by_feature("iq", "w_in", [0], h_t, "act")
            pe.wait_ge(*emptied("iq1"))
            for t in range(NT):
                for h in range(8):
                    r = 64 * (h % 2)
                    n = (t + 1) * P
                    o = begin(f"is{t}_{h}", "act")
                    end(mm(o[:, 0:n], iq_t[r:r + 64, h // 2, t * P:(t + 1) * P], ik_t[r:r + 64, 0:n], True, True))
            by_feature("q", "w_in", [1], h_t, "act")
            by_feature("k", "w_in", [2], h_t, "act")
            by_token("v", "w_in", [3], h_t, "act")
            for a, tag in ((0, "q"), (1, "k")):
                for i in range(2):
                    pe.wait_ge(*emptied(f"{tag}{i}"))
                    o = begin(f"{tag}ss{i}", "dve")
                    end(mm(o[:, 0:BANK], const("pair"), raw_sq[:, a, 2 * i:2 * i + 2, :].rearrange("p j t -> p (j t)"),
                           True, True))
            by_feature("cc", "w_in", [4], h_t, "act")
            by_feature("cx", "w_in", [5], h_t, "dve")
            by_feature("cb", "w_in", [6], h_t, "dve")
            modulation("ada", "w_ada", range(4, 12), silu_c, 1)
            squares("conv", sq1, KA)
            pe.wait_ge(sem("qk_ready"), 4)
            for t in range(NT):
                n = (t + 1) * P
                for h in range(HEADS):
                    r = 64 * (h % 2)
                    o = begin(f"at{t}_{h}", "dve")
                    end(mm(o[:, 0:n], q_t[r:r + 64, h // 2, t * P:(t + 1) * P], k_t[r:r + 64, h // 2, 0:n], True, True))
                pe.wait_ge(sem("probs"), t + 1)
                for i in range(2 * (t + 1)):
                    o = begin(f"pt{t}_{i}", "act")
                    for j in range(4):
                        h, s = divmod(4 * i + j, t + 1)
                        last = nc.tensor.transpose(o[:, j * P:(j + 1) * P], probs[:, h, s * P:(s + 1) * P], ident)
                    end(last)
            pe.wait_ge(*emptied("pt1_3"))
            for j in range(KA):
                o = begin(f"pv{j}", "act")
                for h in (2 * j, 2 * j + 1):
                    c = (h % 2) * L
                    last = mm(o[:, c:c + P], v_n[:, 0, j * P:(j + 1) * P], p_t0[:, h, :], True, True)
                    for s in range(2):
                        last = mm(o[:, c + P:c + L], v_n[:, s, j * P:(j + 1) * P], p_t1[:, h, s, :], s == 0, s == 1)
                end(last)
            squares("att", sq1, KA)
            pe.wait_ge(sem("y_mix"), 2)
            by_feature("wo", "w_out", range(2), y_mix, "dve")
            squares("n2", sq1, KD)
            pe.wait_ge(sem("h_n2"), 1)
            by_feature("pq", "peer_wq", range(4), h_t, "act")
            for t in range(NT):
                for i in range(2):
                    o = begin(f"ht{t}_{i}", "act")
                    for j in range(4):
                        last = nc.tensor.transpose(o[:, j * P:(j + 1) * P], h_t[:, 4 * i + j, t * P:(t + 1) * P], ident)
                    end(last)
            pe.wait_ge(*emptied("pq7"))
            w = next_slab("subkeys", 0).rearrange("p (h n) -> p h n", h=2 * PH)
            for t in range(NT):
                for i in range(4):
                    o = begin(f"ks{t}_{i}", "act")
                    for j in range(4):
                        hp = 4 * i + j
                        last = mm(o[:, j * P:(j + 1) * P], pq_t[:, hp, t * P:(t + 1) * P], w[:, hp, :], True, True)
                    end(last)
            release()

            modulation("ada2_", "w_ada_2", range(18), silu_c2, 2)
            squares("ctx1", hid, KD)
            pe.wait_ge(sem("h_ctx1"), 1)
            feed_forward("fc", 1, h_t)
            squares("ctx2", hid, KD)
            pe.wait_ge(sem("h_ctx2"), 1)
            by_token("kc", "w_in_2", range(2, 4), h_t, "act")
            by_token("vc", "w_in_2", range(4, 8), h_t, "act")

            for t in range(NT):
                pe.wait_ge(sem("experts"), t + 1)
                for i in range(2):
                    o = begin(f"yt{t}_{i}", "dve")
                    for j in range(4):
                        last = nc.tensor.transpose(o[:, j * P:(j + 1) * P],
                                                   y_of[t][:, (4 * i + j) * P:(4 * i + j + 1) * P], ident)
                    end(last)
            for h in range(RH):
                for a in range(2):
                    pe.wait_ge(sem("k_fade"), 2 * h + a + 1)
                    for b in range(2):
                        o = begin(f"st{h}_{a}_{b}", "act")
                        for t in range(NT):
                            last = mm(o[:, 0:DV], k_fade[(2 * h + a) % 4][:, t, b * P:(b + 1) * P],
                                      vc[:, t, h * DV:(h + 1) * DV], t == 0, t == 1)
                        end(last)
            squares("x1", sq2, KD)
            pe.wait_ge(sem("h_x1"), 1)
            feed_forward("f1", 1, h_t)
            squares("x2", sq2, KD)
            pe.wait_ge(sem("h_x2"), 1)
            by_feature("gf", "w_in_2", range(16, 18), h_t, "act")
            by_feature("f", "w_in_2", range(12, 14), h_t, "act")
            pe.wait_ge(*emptied("f3"))
            pe.wait_ge(sem("late"), 64)
            for t in range(NT):
                for g in range(FG):
                    o = begin(f"z{t}_{g}", "act")
                    for k in range(2):
                        last = mm(o[:, 0:BANK], f_t[:, 2 * g + k, t * P:(t + 1) * P],
                                  dft[:, k, :, :].rearrange("p a c -> p (a c)"), k == 0, k == 1)
                    end(last)
            pe.wait_ge(*emptied("z1_3"))
            for i in range(4):
                o = begin(f"mx{i}", "act")
                for j in range(2):
                    n = 0
                    for t in range(NT):
                        for a in range(2):
                            last = mm(o[:, j * L:(j + 1) * L], dft_z[:, t, i, a, j * P:(j + 1) * P], dft[:, t, a, :],
                                      n == 0, n == 3)
                            n += 1
                end(last)
            pe.wait_ge(*emptied("mx3"))
            by_feature("pf", "p_four", range(2), mixed, "dve")
            by_feature("ga", "w_in_2", range(14, 16), h_t, "act")
            by_feature("rq", "w_in_2", range(0, 2), h_t, "dve")
            by_feature("rk", "w_in_2", range(2, 4), h_t, "dve")
            by_token("rv", "w_in_2", range(4, 8), h_t, "act")
            by_feature("rg", "w_in_2", range(8, 12), h_t, "act")
            for h in range(RH):
                pe.wait_ge(sem("q_faded"), h + 1)
                o = begin(f"sc{h}", "dve")
                for t in range(NT):
                    for b in range(2):
                        last = mm(o[:, t * L:(t + 1) * L], rk_t[:, 2 * h + b, t * P:(t + 1) * P], rq_t[:, 2 * h + b, :],
                                  b == 0, b == 1)
                end(last)
                for t in range(NT):
                    o = begin(f"o{h}_{t}", "dve")
                    n = 0
                    for a in range(2):
                        for b in range(2):
                            mm(o[:, 0:DV], q_faded[:, a, b, t * P:(t + 1) * P], state[:, h, a, b, :], n == 0, False)
                            n += 1
                    pe.wait_ge(*emptied(f"sc{h}"))
                    for s in range(NT):
                        last = mm(o[:, 0:DV], sc_t[:, s, t * P:(t + 1) * P], rv[:, s, h * DV:(h + 1) * DV],
                                  False, s == 1)
                    end(last)
                for t in range(NT):
                    pe.wait_ge(*emptied(f"o{h}_{t}"))
                    o = begin(f"ot{h}_{t}", "dve")
                    for j in range(4):
                        last = nc.tensor.transpose(o[:, j * P:(j + 1) * P], o_n[:, j * P:(j + 1) * P], ident)
                    end(last)
            pe.wait_ge(*emptied(f"ot{RH - 1}_1"))
            by_feature("pr", "p_ret", range(4), rg_t, "dve", kb=16)
            pe.wait_ge(sem("merged"), 1)
            by_feature("w2o", "w_out_2", range(2), m_t, "dve")
            squares("x3", sq2, KD)
            pe.wait_ge(sem("h_x3"), 1)
            feed_forward("f2", 2, h_t)
            squares("fin", sq2, KD)
            assert used[0] == len(slabs)

        @block.sync
        def _(sp):
            for src, dst in (("params", prm), ("early", early), ("x", x_t)):
                d = dst[:] if src != "x" else x_t.rearrange("p k t -> p (k t)")
                sp.dma_start(d, dram[src]).then_inc(sem("params"), 16)
            for n, (name, i, words) in enumerate(slabs):
                if n == 8:
                    sp.dma_start(ctx_t.rearrange("p k t -> p (k t)"), dram["ctx"]).then_inc(sem("ctx_landed"), 16)
                if n >= RING:
                    sp.wait_ge(group_done, slab_free[n - RING])
                at = (n % RING) * SLAB
                sp.dma_start(ring[:, at:at + words], dram[name][i]).then_inc(landed[n % RING], 16)
                if n == second_at + RING:
                    sp.wait_ge(sem("experts_added"), 1)
                    at = 0
                    for dst, w in ((late_decay, LATE_DECAY), (dft, LATE_DFT), (rope, LATE_ROPE), (late_xi, LATE_XI)):
                        s = "p m t i -> p (m t i)" if w == LATE_DECAY else (
                            "p k a c -> p (k a c)" if w == LATE_DFT else "p a t -> p (a t)")
                        sp.dma_start(dst.rearrange(s), dram["late"][:, at:at + w]).then_inc(sem("late"), 16)
                        at += w
            sp.wait_ge(sem("out_ready"), 1)
            sp.dma_start(out, h_t.rearrange("p k t -> p (k t)")).then_inc(sem("stored"), 16)
            sp.wait_ge(sem("stored"), 16)

        @block.gpsimd
        def _(pool):
            staged = sem("staged")
            for t in range(NT):
                pool.wait_ge(sem("ids"), t + 1)
                with pool.Fori(0, SLOTS // ROUND) as r:
                    for half in range(2):
                        n = ROUND // 2
                        pool.wait_ge(sem("row_free"), r * ROUND + (t * SLOTS + half * n + 1))
                        nc.gpsimd.tensor_copy(idx_stage[:, half * n:(half + 1) * n],
                                              ids[:, bass.ds(r * ROUND + (t * SLOTS + half * n), n)]).then_inc(staged, 1)
                        pool.wait_ge(staged, r * 2 + (t * 2 * SLOTS // ROUND + half + 1))
                        for s in range(n):
                            slot = half * n + s
                            pool.wait_ge(sem("row_free"), r * ROUND + (t * SLOTS + slot + 1))
                            pool.sem_inc(sem("row_turn"), 1)
                            nc.gpsimd.indirect_dma_start(
                                rows[slot % GBUF], None, dram["experts"],
                                bass.IndirectOffsetOnAxis(ap=idx_stage[:, slot:slot + 1], axis=0),
                            ).then_inc(row_landed[slot % GBUF], 16)

        @block.scalar
        def _(act):
            taken, roots = [0], [0]

            def root(ap):
                roots[0] += 1
                act.wait_ge(sem("root_in"), roots[0])
                nc.scalar.activation(ap, ap, ACT.Sqrt).then_inc(sem("root_out"), 1)

            def take(name):
                _, who, count = groups[index[name]]
                taken[0] += 1
                assert who == "act" and count == taken[0], (name, who, count, taken[0])
                act.wait_ge(group_done, index[name] + 1)
                return psum[:, index[name] % BANKS, :]

            def drain(ins):
                ins.then_inc(drained["act"], 1)

            def flat(ap):
                return ap.rearrange("p a t -> p (a t)")

            def copy_out(name, dst, func=ACT.Copy, width=BANK, scale=1.0):
                drain(nc.scalar.activation(dst, take(name)[:, 0:width], func, scale=scale))

            def square(tag, dst, src, kb):
                nc.scalar.activation(flat(dst[:, 0:kb, :]), flat(src), ACT.Square).then_inc(sem("sq_" + tag), 1)

            def ff_act(tag):
                for i in range(11):
                    drain(nc.scalar.activation(flat(hid[:, 2 * i:2 * i + 2, :]), take(f"{tag}_a{i}"), ACT.Silu))
                    yield
                for i in range(8):
                    yield

            act.wait_ge(sem("params"), 48)
            nc.scalar.activation(silu_c, param("c"), ACT.Silu).then_inc(sem("silu_c"), 1)
            nc.scalar.activation(silu_c2, param("c2"), ACT.Silu).then_inc(sem("silu_c"), 1)
            square("n1", sq1, x_t, KD)
            for i in range(4):
                copy_out(f"ada{i}", mod1[:, 4 * i:4 * i + 4], width=4)
            root(rstd[:])
            act.wait_ge(sem("lg_abs"), 1)
            nc.scalar.activation(lg_e, lg_z, ACT.Exp, scale=-1.0).then_inc(sem("lg_exp"), 1)
            copy_out("ik", ik_t, width=L)
            copy_out("iw", iw.rearrange("p t h -> p (t h)"), width=16)
            for i in range(2):
                copy_out(f"iq{i}", flat(iq_t[:, 2 * i:2 * i + 2, :]))
            for t in range(NT):
                for h in range(8):
                    n = 8 * t + h
                    if n >= 4:
                        act.wait_ge(sem("relu_used"), n - 3)
                    copy_out(f"is{t}_{h}", relu[:, n % 4, 0:(t + 1) * P], ACT.Relu, (t + 1) * P)
            for a, tag in ((0, "q"), (1, "k")):
                for i in range(2):
                    o = take(f"{tag}{i}")
                    nc.scalar.activation(flat(raw[:, a, 2 * i:2 * i + 2, :]), o, ACT.Copy)
                    drain(nc.scalar.activation(flat(raw_sq[:, a, 2 * i:2 * i + 2, :]), o, ACT.Square))
            for t in range(NT):
                copy_out(f"v{t}", v_n[:, t, :])
            for i in range(2):
                copy_out(f"cc{i}", flat(gate_c[:, 2 * i:2 * i + 2, :]))
            for a in range(2):
                for i in range(2):
                    root(flat(raw_sq[:, a, 2 * i:2 * i + 2, :]))
            for i in range(4, 12):
                copy_out(f"ada{i}", mod1[:, 4 * i:4 * i + 4], width=4)
            act.wait_ge(sem("y_conv"), 1)
            square("conv", sq1, y_conv, KA)
            root(rstd[:])
            for t in range(NT):
                n = (t + 1) * P
                act.wait_ge(sem("shifted"), t + 1)
                nc.scalar.activation(probs[:, :, 0:n], probs[:, :, 0:n], ACT.Exp, scale=ATT_SCALE).then_inc(sem("exped"), 1)
                for i in range(2 * (t + 1)):
                    dst = p_t0[:, 4 * i:4 * i + 4, :] if t == 0 else p_t1[:, 2 * i:2 * i + 2, :, :]
                    s = "p h q -> p (h q)" if t == 0 else "p h s q -> p (h s q)"
                    copy_out(f"pt{t}_{i}", dst.rearrange(s))
            for j in range(KA):
                o = take(f"pv{j}")
                nc.scalar.activation(y_att[0:64, j, :], o[0:64, 0:L], ACT.Copy)
                drain(nc.scalar.activation(y_att[64:128, j, :], o[64:128, L:2 * L], ACT.Copy))
            act.wait_ge(sem("conv_mixed"), 1)
            act.wait_ge(drained["act"], taken[0])
            square("att", sq1, y_att, KA)
            root(rstd[:])
            act.wait_ge(*emptied("wo3"))
            square("n2", sq1, x_t, KD)
            root(rstd[:])
            for i in range(8):
                copy_out(f"pq{i}", flat(pq_t[:, 2 * i:2 * i + 2, :]))
            for t in range(NT):
                for i in range(2):
                    copy_out(f"ht{t}_{i}", h2[:, t, i * BANK:(i + 1) * BANK])
            for t in range(NT):
                for i in range(4):
                    copy_out(f"ks{t}_{i}", key_s[:, t, 4 * i:4 * i + 4, :].rearrange("p h n -> p (h n)"))

            def background():
                for i in range(28):
                    if i < 18:
                        copy_out(f"ada2_{i}", mod2[:, 8 * i:8 * i + 8], width=8)
                    yield
                act.wait_ge(sem("ctx_landed"), 16)
                act.wait_ge(sem("ids"), 2)
                square("ctx1", hid, ctx_t, KD)
                root(rstd[:])
                yield
                yield from ff_act("fc")
                act.wait_ge(*emptied("fc_y7"))
                square("ctx2", hid, ctx_t, KD)
                root(rstd[:])
                yield
                act.wait_ge(sem("h_ctx2"), 1)
                for i in range(12):
                    c, t = divmod(i, 2)
                    if c < 2:
                        copy_out(f"kc{i}", kc[:, t, c * BANK:(c + 1) * BANK])
                    else:
                        copy_out(f"vc{i - 4}", vc[:, t, (c - 2) * BANK:(c - 1) * BANK])
                    yield

            bg = background()
            for t in range(NT):
                act.wait_ge(sem("best"), t + 1)
                flat_best = best[:, t].rearrange("p h n -> p (h n)")
                nc.scalar.activation(flat_best, flat_best, ACT.Exp).then_inc(sem("best_exp"), 1)
                for b in range(SLOTS // BATCH):
                    n = t * (SLOTS // BATCH) + b
                    act.wait_ge(sem("dots"), BATCH * (n + 1))
                    nc.scalar.activation(acts[:, n % 8, :], dots[:, n % 8, :], ACT.Gelu_apprx_tanh).then_inc(sem("gelus"), 1)
                    if b % 2 == 1:
                        next(bg, None)
            for _ in bg:
                pass
            act.wait_ge(sem("lg"), 1)
            for a in range(2):
                for t in range(NT):
                    at = EARLY_AT["age"][0] + 2 * a + t
                    for h in range(RH):
                        c = (a * NT + t) * RH + h
                        last = nc.scalar.activation(fade[:, c:c + 1], early[:, at:at + 1], ACT.Exp,
                                                    scale=lg[:, 4 * a + h:4 * a + h + 1])
            last.then_inc(sem("fade"), 1)
            act.wait_ge(sem("experts_added"), 1)
            for h in range(RH):
                for a in range(2):
                    for b in range(2):
                        copy_out(f"st{h}_{a}_{b}", state[:, h, a, b, :])
            square("x1", sq2, x_t, KD)
            root(rstd[:])
            act.wait_ge(sem("late"), 64)
            for h in range(RH):
                for a in range(2):
                    n = 2 * h + a
                    if n >= 2:
                        act.wait_ge(sem("decay_used"), n - 1)
                    nc.scalar.activation((xi if a == 0 else rope_tmp).rearrange("p a t -> p (a t)"),
                                         late_decay[:, a].rearrange("p t i -> p (t i)"), ACT.Exp,
                                         scale=lg[:, 4 * a + h:4 * a + h + 1]).then_inc(sem("decay_exp"), 1)
            for _ in ff_act("f1"):
                pass
            act.wait_ge(*emptied("f1_y7"))
            square("x2", sq2, x_t, KD)
            root(rstd[:])
            for i in range(4):
                copy_out(f"gf{i}", flat(sig[:, 2 * i:2 * i + 2, :]), ACT.Sigmoid)
            for i in range(4):
                copy_out(f"f{i}", flat(f_t[:, 2 * i:2 * i + 2, :]))
            for t in range(NT):
                for g in range(FG):
                    o = take(f"z{t}_{g}")
                    nc.scalar.activation(dft_z[:, t, g, 0, :], o[:, 0:256], ACT.Copy)
                    drain(nc.scalar.activation(dft_z[:, t, g, 1, :], o[:, 256:512], ACT.Copy, scale=-1.0))
            for i in range(4):
                copy_out(f"mx{i}", flat(mixed[:, 2 * i:2 * i + 2, :]))
            act.wait_ge(*emptied("pf3"))
            for i in range(4):
                copy_out(f"ga{i}", flat(sig[:, 2 * i:2 * i + 2, :]), ACT.Sigmoid)
            for i in range(8):
                c, t = divmod(i, 2)
                copy_out(f"rv{i}", rv[:, t, c * BANK:(c + 1) * BANK])
            for i in range(8):
                copy_out(f"rg{i}", flat(rg_t[:, 2 * i:2 * i + 2, :]), ACT.Silu)
            for h in range(RH + 1):
                if h:
                    act.wait_ge(sem("q_faded"), h)
                if h < RH:
                    for a in range(2):
                        last = nc.scalar.activation(xi[:, a, :], late_xi[:, a, :], ACT.Exp,
                                                    scale=lg[:, 4 * a + h:4 * a + h + 1])
                    last.then_inc(sem("xi"), 1)
                if h:
                    for t in range(NT):
                        root(stat[:, 8:9])
            act.wait_ge(*emptied("w2o3"))
            square("x3", sq2, x_t, KD)
            root(rstd[:])
            for _ in ff_act("f2"):
                pass
            act.wait_ge(*emptied("f2_y7"))
            square("fin", sq2, x_t, KD)
            root(rstd[:])
            assert taken[0] == sum(g[1] == "act" for g in groups)

        @block.vector
        def _(v):
            taken, steps, roots = [0], {}, [0]
            chain = sem("dve_step")

            def step(ins, s=chain):
                ins.then_inc(s, 1)
                steps[s.name] = steps.get(s.name, 0) + 1
                v.wait_ge(s, steps[s.name])

            def take(name):
                _, who, count = groups[index[name]]
                taken[0] += 1
                assert who == "dve" and count == taken[0], (name, who, count, taken[0])
                v.wait_ge(group_done, index[name] + 1)
                return psum[:, index[name] % BANKS, :]

            def drain(ins):
                step(ins, drained["dve"])

            def flat(ap):
                return ap.rearrange("p a t -> p (a t)")

            TT, TS, STT = nc.vector.tensor_tensor, nc.vector.tensor_scalar, nc.vector.scalar_tensor_tensor

            def rooted(dst):
                roots[0] += 1
                step(nc.vector.reciprocal(dst, dst), sem("root_in"))
                v.wait_ge(sem("root_out"), roots[0])

            def root(name, dst, width, n):
                drain(TS(dst, take(name)[:, 0:width], 1.0 / n, EPS, ALU.mult, ALU.add))
                rooted(dst)

            def modulated(tag, src, dst, weight, scale, shift):
                step(STT(scale_of[tag], scale, 1.0, weight, ALU.add, ALU.mult))
                root("ss_" + tag, rstd[:], L, D)
                step(TT(dst, src, rstd[:].unsqueeze(1).to_broadcast([P, KD, L]), ALU.mult))
                for k in range(KD):
                    last = TS(dst[:, k, :], dst[:, k, :], scale_of[tag][:, k:k + 1], shift[:, k:k + 1], ALU.mult, ALU.add)
                    if k < KD - 1:
                        last.then_inc(chain, 1)
                        steps[chain.name] += 1
                step(last, sem("h_" + tag))

            def mix(src, dst, k0, weight):
                for j in range(KA):
                    step(STT(dst[:, k0 + j, :], src[:, j, :], weight[:, j:j + 1], rstd[:], ALU.mult, ALU.mult),
                         sem("y_mix") if j == KA - 1 else chain)

            def residual(names, dst, gate, per):
                n = 0
                for name in names:
                    o = take(name)
                    for j in range(per):
                        ins = STT(dst[:, n, :], o[:, j * L:(j + 1) * L], gate[:, n:n + 1], dst[:, n, :], ALU.mult, ALU.add)
                        n += 1
                        if j < per - 1:
                            step(ins)
                    drain(ins)

            def ff_dve(tag, dst, gate):
                for i in range(11):
                    o = take(f"{tag}_b{i}")
                    v.wait_ge(*emptied(f"{tag}_a{i}"))
                    hb = flat(hid[:, 2 * i:2 * i + 2, :])
                    drain(TT(hb, hb, o, ALU.mult))
                    yield
                for i in range(8):
                    drain(STT(dst[:, i, :], take(f"{tag}_y{i}")[:, 0:L], gate[:, i:i + 1], dst[:, i, :],
                              ALU.mult, ALU.add))
                    yield

            step(nc.vector.memset(ones[:], 1.0), sem("ones"))
            v.wait_ge(sem("params"), 48)
            step(STT(lg_z, param("decay"), -1.0, param("decay"), ALU.mult, ALU.max), sem("lg_abs"))
            step(nc.vector.memset(padded[:, :, 0:2], 0.0))
            step(TS(flat(fill), const("causal"), 1.0, -FILL, ALU.subtract, ALU.mult))
            v.wait_ge(*emptied("ada3"))
            step(TT(mod1[:, 0:16], mod1[:, 0:16], param("b_ada")[:, 0:16], ALU.add))
            modulated("n1", x_t, h_t, param("norm1_w"), mod1[:, 8:16], mod1[:, 0:8])
            v.wait_ge(sem("lg_exp"), 1)
            step(TS(lg_z, lg_e, 2.0, None, ALU.add))
            step(nc.vector.reciprocal(lg_z, lg_z))
            step(TT(lg_z, lg_z, lg_e, ALU.mult))
            step(TT(lg_z2, lg_z, lg_z, ALU.mult))
            step(TS(lg_s, lg_z2, 1.0 / 17, None, ALU.mult))
            for odd in (15, 13, 11, 9, 7, 5, 3):
                step(STT(lg_s, lg_s, 1.0 / odd, lg_z2, ALU.add, ALU.mult))
            step(STT(lg_s, lg_s, 1.0, lg_z, ALU.add, ALU.mult))
            step(TS(lg_e, param("decay"), 0.0, None, ALU.min))
            step(STT(lg, lg_s, -2.0, lg_e, ALU.mult, ALU.add), sem("lg"))
            v.wait_ge(*emptied("iw"))
            for t in range(NT):
                n = (t + 1) * P
                if t == 0:
                    step(nc.vector.memset(idx[:, 0, P:L], 0.0))
                for h in range(8):
                    v.wait_ge(*emptied(f"is{t}_{h}"))
                    if h == 0:
                        ins = TS(idx[:, t, 0:n], relu[:, (8 * t + h) % 4, 0:n], iw[:, t, 0:1], None, ALU.mult)
                    else:
                        ins = STT(idx[:, t, 0:n], relu[:, (8 * t + h) % 4, 0:n], iw[:, t, h:h + 1], idx[:, t, 0:n],
                                  ALU.mult, ALU.add)
                    step(ins, sem("relu_used"))
            causal = const("causal")
            step(STT(flat(idx), flat(idx), IDX_SCALE, causal, ALU.mult, ALU.mult))
            step(TT(flat(idx), flat(idx), flat(fill), ALU.add))
            for t in range(NT):
                n = (t + 1) * P
                for _ in range(TOPK // 8):
                    step(nc.vector.max(max8, idx[:, t, 0:n]))
                    step(nc.vector.match_replace(idx[:, t, 0:n], max8, idx[:, t, 0:n], TAKEN))
            step(STT(flat(bias), flat(idx), TAKEN, causal, ALU.is_equal, ALU.mult))
            step(TS(flat(bias), flat(bias), 1.0, -MASKED, ALU.subtract, ALU.mult))
            for a, tag, dst in ((0, "q", q_t), (1, "k", k_t)):
                for i in range(2):
                    rs = flat(raw_sq[:, a, 2 * i:2 * i + 2, :])
                    root(f"{tag}ss{i}", rs, BANK, HD)
                    step(STT(flat(dst[:, 2 * i:2 * i + 2, :]), flat(raw[:, a, 2 * i:2 * i + 2, :]),
                             param(f"{tag}_norm_w")[:, 0:1], rs, ALU.mult, ALU.mult), sem("qk_ready"))
            for i in range(2):
                o = take(f"cx{i}").rearrange("p (j t) -> p j t", j=2)
                v.wait_ge(*emptied(f"cc{i}"))
                drain(TT(padded[:, 2 * i:2 * i + 2, 2:2 + L], gate_c[:, 2 * i:2 * i + 2, :], o, ALU.mult))
            cw, cb = param("conv_w"), param("conv_b")
            for j in range(KA):
                step(TS(y_conv[:, j, :], padded[:, j, 0:L], cw[:, j:j + 1], cb[:, j:j + 1], ALU.mult, ALU.add))
                for i in (1, 2):
                    step(STT(y_conv[:, j, :], padded[:, j, i:i + L], cw[:, 4 * i + j:4 * i + j + 1], y_conv[:, j, :],
                             ALU.mult, ALU.add))
            for i in range(2):
                o = take(f"cb{i}")
                yc = flat(y_conv[:, 2 * i:2 * i + 2, :])
                drain(TT(yc, yc, o, ALU.mult))
            v.wait_ge(*emptied("ada11"))
            step(TT(mod1[:, 16:48], mod1[:, 16:48], param("b_ada")[:, 16:48], ALU.add), sem("y_conv"))
            root("ss_conv", rstd[:], L, ATT)
            mix(y_conv, y_mix, KA, param("conv_out_norm_w"))
            step(nc.vector.memset(stat[:, 0:1], 0.0), sem("conv_mixed"))
            for t in range(NT):
                n = (t + 1) * P
                pr = probs[:, :, 0:n]
                if t:
                    v.wait_ge(*emptied("pt0_1"))
                for h in range(HEADS):
                    drain(TT(probs[:, h, 0:n], take(f"at{t}_{h}")[:, 0:n], bias[:, t, 0:n], ALU.add))
                step(nc.vector.tensor_reduce(mxs, pr, AX_X, ALU.max))
                step(TT(pr, pr, mxs.unsqueeze(2).to_broadcast([P, HEADS, n]), ALU.subtract), sem("shifted"))
                v.wait_ge(sem("exped"), t + 1)
                step(nc.vector.tensor_reduce(mxs, pr, AX_X, ALU.add))
                step(nc.vector.reciprocal(mxs, mxs))
                step(TT(pr, pr, mxs.unsqueeze(2).to_broadcast([P, HEADS, n]), ALU.mult), sem("probs"))
            root("ss_att", rstd[:], L, ATT)
            mix(y_att, y_mix, 0, param("attn_out_norm_w"))
            residual([f"wo{i}" for i in range(4)], x_t, mod1[:, 16:24], 2)
            modulated("n2", x_t, h_t, param("norm2_w"), mod1[:, 32:40], mod1[:, 24:32])

            def top16(values, out_v, out_i):
                step(nc.vector.max(out_v[:, 0:8], values))
                step(nc.vector.max_index(out_i[:, 0:8], out_v[:, 0:8], values))
                step(nc.vector.match_replace(values, out_v[:, 0:8], values, FILL))
                step(nc.vector.max(out_v[:, 8:16], values))
                step(nc.vector.max_index(out_i[:, 8:16], out_v[:, 8:16], values))

            def choose_experts(t):
                fv = found[:].rearrange("p (h n) -> p h n", h=2 * PH)
                for hp in range(2 * PH):
                    v.wait_ge(*emptied(f"ks{t}_{hp // 4}"))
                    top16(key_s[:, t, hp, :], top_v[:, hp, :], fv[:, hp, :])
                    yield
                step(nc.vector.tensor_copy(flat(top_i), found[:]))
                tv = top_v.rearrange("p (h a) n -> p h a n", a=2)
                ti = top_i.rearrange("p (h a) n -> p h a n", a=2)
                wide = [P, PH, PSEL, PSEL]
                step(TT(combo.rearrange("p h (i j) -> p h i j", i=PSEL),
                        tv[:, :, 0, :].unsqueeze(3).to_broadcast(wide), tv[:, :, 1, :].unsqueeze(2).to_broadcast(wide),
                        ALU.add))
                yield
                pl = place[:].rearrange("p (h n) -> p h n", h=PH)
                for h in range(PH):
                    top16(combo[:, h, :], best[:, t, h, :], pl[:, h, :])
                    yield
                hi = half_i.rearrange("p (a n) -> p a n", a=2)
                hid_ = half_id.rearrange("p (a n) -> p a n", a=2)
                spare = found[:, 0:SLOTS]
                step(TS(spare, place[:], 4, None, ALU.logical_shift_right))
                step(nc.vector.tensor_copy(hi[:, 0, :], spare))
                step(TS(spare, place[:], 15, None, ALU.bitwise_and))
                step(nc.vector.tensor_copy(hi[:, 1, :], spare))
                hot = pick.rearrange("p k t -> p (k t)").rearrange("p (s n) -> p s n", n=PSEL)
                hot4 = pick.rearrange("p k t -> p (k t)").rearrange("p (h s n) -> p h s n", h=PH, s=PSEL)
                for a in range(2):
                    step(TT(hot, hi[:, a, :].unsqueeze(2).to_broadcast([P, SLOTS, PSEL]),
                            const("iota16").unsqueeze(1).to_broadcast([P, SLOTS, PSEL]), ALU.is_equal))
                    step(TT(hot4, hot4, ti[:, :, a, :].unsqueeze(2).to_broadcast(wide), ALU.mult))
                    step(nc.vector.tensor_reduce(hid_[:, a, :], hot, AX_X, ALU.add))
                    yield
                step(STT(id_f, hid_[:, 0, :], float(PK), hid_[:, 1, :], ALU.mult, ALU.add))
                step(nc.vector.tensor_copy(ids[:, t * SLOTS:(t + 1) * SLOTS], id_f), sem("ids"))
                bt = best[:, t]
                step(nc.vector.tensor_copy(hsum[:, 0:8], bt[:, :, 0]))
                step(TT(bt, bt, hsum[:, 0:8].unsqueeze(2).to_broadcast([P, PH, PSEL]), ALU.subtract), sem("best"))
                yield

            def gates(t):
                v.wait_ge(sem("best_exp"), t + 1)
                step(nc.vector.tensor_reduce(hsum[:, 0:8], best[:, t], AX_X, ALU.add))
                step(nc.vector.reciprocal(hsum[:, 0:8], hsum[:, 0:8]))
                step(TT(best[:, t], best[:, t], hsum[:, 0:8].unsqueeze(2).to_broadcast([P, PH, PSEL]), ALU.mult))

            def background():
                yield from choose_experts(1)
                v.wait_ge(*emptied("ada2_17"))
                b2 = param("b_ada_2").unsqueeze(2).to_broadcast([P, 72, 2])
                m2 = mod2[:].rearrange("p (j s) -> p j s", s=2)
                step(TT(m2, m2, b2, ALU.add))
                for key, row, s in (("ctx1", 2, 1), ("x1", 2, 0), ("x3", 8, 0)):
                    step(TS(half_gate[key], mod2_v[:, row, :, s], 0.5, None, ALU.mult))
                v.wait_ge(sem("ctx_landed"), 16)
                modulated("ctx1", ctx_t, h_t, param("norm_ffn1_2"), mod2_v[:, 1, :, 1], mod2_v[:, 0, :, 1])
                yield
                yield from ff_dve("fc", ctx_t, half_gate["ctx1"])
                modulated("ctx2", ctx_t, h_t, param("norm_mix_2"), mod2_v[:, 4, :, 1], mod2_v[:, 3, :, 1])
                yield

            for _ in choose_experts(0):
                pass
            v.wait_ge(*emptied("ks1_3"))
            v.sem_inc(sem("row_free"), GBUF)
            bg = background()
            per_tile = SLOTS // BATCH

            def dot_batch(n):
                for s in range(BATCH):
                    g = n * BATCH + s
                    v.wait_ge(row_landed[g % GBUF], 16 * (g // GBUF + 1))
                    u = rows[g % GBUF][:, 0:D]
                    step(nc.vector.tensor_tensor_reduce(u, u, h2[:, n // per_tile, :], 1.0, 0.0, ALU.mult, ALU.add,
                                                        dots[:, n % 8, s:s + 1]), sem("dots"))

            def sum_batch(n):
                t, b = divmod(n, per_tile)
                v.wait_ge(sem("gelus"), n + 1)
                gate = flat(best[:, t])[:, b * BATCH:(b + 1) * BATCH]
                step(TT(weights[:, n % 8, :], acts[:, n % 8, :], gate, ALU.mult))
                for s in range(BATCH):
                    g = n * BATCH + s
                    STT(y_of[t], rows[g % GBUF][:, D:2 * D], weights[:, n % 8, s:s + 1], y_of[t],
                        ALU.mult, ALU.add).then_inc(sem("row_free"), 1)
                    v.wait_ge(sem("row_free"), GBUF + g + 1)

            for t in range(NT):
                gates(t)
                step(nc.vector.memset(y_of[t], 0.0))
                dot_batch(t * per_tile)
                for b in range(per_tile):
                    n = t * per_tile + b
                    if b + 1 < per_tile:
                        dot_batch(n + 1)
                    sum_batch(n)
                    if b % 2 == 1:
                        next(bg, None)
                step(nc.vector.memset(stat[:, 0:1], 0.0), sem("experts"))
            for _ in bg:
                pass
            for t in range(NT):
                for i in range(2):
                    o = take(f"yt{t}_{i}")
                    for j in range(4):
                        k = 4 * i + j
                        xs = x_t[:, k, t * P:(t + 1) * P]
                        ins = STT(xs, o[:, j * P:(j + 1) * P], mod1[:, 40 + k:41 + k], xs, ALU.mult, ALU.add)
                        if j < 3:
                            step(ins)
                    drain(ins)
            step(nc.vector.memset(stat[:, 0:1], 0.0), sem("experts_added"))
            v.wait_ge(*emptied("kc3"))
            v.wait_ge(*emptied("vc7"))
            v.wait_ge(sem("fade"), 1)
            for h in range(RH):
                for a in range(2):
                    n = 2 * h + a
                    if n >= 4:
                        v.wait_ge(*emptied(f"st{(n - 4) // 2}_{(n - 4) % 2}_1"))
                    for t in range(NT):
                        c = (a * NT + t) * RH + h
                        step(TS(k_fade[n % 4][:, t, :], kc[:, t, h * DK:(h + 1) * DK], fade[:, c:c + 1], None, ALU.mult),
                             sem("k_fade") if t == NT - 1 else chain)
            v.wait_ge(*emptied(f"st{RH - 1}_1_1"))
            modulated("x1", x_t, h_t, param("norm_ffn1_2"), mod2_v[:, 1, :, 0], mod2_v[:, 0, :, 0])
            v.wait_ge(sem("late"), 64)
            for h in range(RH):
                for a in range(2):
                    v.wait_ge(sem("decay_exp"), 2 * h + a + 1)
                    mask = flat(late_decay[:, 2 + a])
                    if a == 0:
                        step(TT(flat(decay_t[:, h]), flat(xi), mask, ALU.mult), sem("decay_used"))
                    else:
                        step(TT(flat(rope_tmp), flat(rope_tmp), mask, ALU.mult))
                        step(TT(flat(decay_t[:, h]), flat(decay_t[:, h]), flat(rope_tmp), ALU.add), sem("decay_used"))
            for _ in ff_dve("f1", x_t, half_gate["x1"]):
                pass
            modulated("x2", x_t, h_t, param("norm_mix_2"), mod2_v[:, 4, :, 0], mod2_v[:, 3, :, 0])
            v.wait_ge(*emptied("gf3"))
            for i in range(4):
                drain(TT(flat(m_t[:, 2 * i:2 * i + 2, :]), flat(sig[:, 2 * i:2 * i + 2, :]), take(f"pf{i}"), ALU.mult))
            cos = rope[:, 0, :].unsqueeze(1).to_broadcast([P, 2, L])
            sin = rope[:, 1, :].unsqueeze(1).to_broadcast([P, 2, L])
            for tag, dst, scale in (("rq", rq_t, DK ** -0.5), ("rk", rk_t, 1.0)):
                for h in range(RH):
                    o = take(f"{tag}{h}").rearrange("p (b t) -> p b t", b=2)
                    d = dst[:, 2 * h:2 * h + 2, :]
                    step(STT(d, o, scale, cos, ALU.mult, ALU.mult))
                    drain(STT(rope_tmp, o, scale, sin, ALU.mult, ALU.mult))
                    step(TT(d[:, 0, :], d[:, 0, :], rope_tmp[:, 1, :], ALU.subtract))
                    step(TT(d[:, 1, :], d[:, 1, :], rope_tmp[:, 0, :], ALU.add))
            v.wait_ge(*emptied("rv7"))
            v.wait_ge(*emptied("rg7"))
            for h in range(RH):
                v.wait_ge(sem("xi"), h + 1)
                for a in range(2):
                    step(TT(q_faded[:, a], rq_t[:, 2 * h:2 * h + 2, :], xi[:, a, :].unsqueeze(1).to_broadcast([P, 2, L]),
                            ALU.mult), sem("q_faded") if a else chain)
                drain(TT(flat(sc_t), take(f"sc{h}"), flat(decay_t[:, h]), ALU.mult))
                for t in range(NT):
                    o = take(f"o{h}_{t}")
                    step(nc.vector.bn_stats(stat[:, 0:6], o))
                    step(nc.vector.bn_aggr(stat[:, 6:8], stat[:, 0:6]))
                    step(TS(stat[:, 8:9], stat[:, 7:8], EPS, None, ALU.add))
                    rooted(stat[:, 8:9])
                    if t:
                        v.wait_ge(group_done, index[f"ot{h}_0"] + 1)
                    drain(TS(o_n, o, stat[:, 6:7], stat[:, 8:9], ALU.subtract, ALU.mult))
                for t in range(NT):
                    o = take(f"ot{h}_{t}")
                    for j in range(4):
                        k = 4 * h + j
                        g = rg_t[:, k, t * P:(t + 1) * P]
                        ins = STT(g, o[:, j * P:(j + 1) * P], param("ret_gn_w_2")[:, k:k + 1], g, ALU.mult, ALU.mult)
                        if j < 3:
                            step(ins)
                    drain(ins)
            v.wait_ge(*emptied("ga3"))
            for i in range(4):
                s = flat(sig[:, 2 * i:2 * i + 2, :])
                m = flat(m_t[:, 2 * i:2 * i + 2, :])
                drain(TT(s, s, take(f"pr{i}"), ALU.mult))
                step(TT(m, m, s, ALU.add), sem("merged") if i == 3 else chain)
            residual([f"w2o{i}" for i in range(4)], x_t, mod2_v[:, 5, :, 0], 2)
            modulated("x3", x_t, h_t, param("norm_ffn2_2"), mod2_v[:, 7, :, 0], mod2_v[:, 6, :, 0])
            for _ in ff_dve("f2", x_t, half_gate["x3"]):
                pass
            root("ss_fin", rstd[:], L, D)
            for k in range(KD):
                step(STT(h_t[:, k, :], x_t[:, k, :], param("norm_final_2")[:, k:k + 1], rstd[:], ALU.mult, ALU.mult),
                     sem("out_ready") if k == KD - 1 else chain)
            assert taken[0] == sum(g[1] == "dve" for g in groups)




def _tiles(w, width):
    k, n = w.shape
    return np.ascontiguousarray(w.reshape(k // P, P, n // width, width).transpose(2, 1, 0, 3)).reshape(
        n // width, P, k // P * width)


def _columns(vec):
    return np.asarray(vec).reshape(-1, P).T


def _feature_major(x):
    return np.ascontiguousarray(np.asarray(x).reshape(L, KD, P).transpose(2, 1, 0)).reshape(P, KD * L)


def _ffn_pairs(w13):
    w = np.asarray(w13)[0]
    w = w.reshape(D, 2, FF // 256, 256).transpose(0, 2, 1, 3).reshape(D, 2 * FF)
    return _tiles(w, 512)


def _pairs_apart(w):
    return w.reshape(D, RH, DK // 2, 2).transpose(0, 1, 3, 2).reshape(D, RH * DK)


def kernel(**inputs):
    import concourse.bacc as bacc
    from concourse.bass_utils import run_bass_kernel_spmd

    a = {k: np.asarray(v) for k, v in inputs.items()}
    early, late = shape_constants()
    w_in = a["w_in"]
    w_in_2 = a["w_in_2"][0]
    order = [3072, 0, 512, 1024, 2048, 2560, 1536]
    ik, iw = w_in[:, 3584:3648], w_in[:, 3648:3656]
    parts = {
        "c": _columns(a["c"]),
        "c2": np.stack([_columns(a["c_2"]), _columns(a["c_ctx_2"])], 2).reshape(P, 16),
        "b_ada": _columns(a["b_ada"]), "b_ada_2": _columns(a["b_ada_2"]),
        "q_norm_w": np.tile(a["q_norm_w"], 2)[:, None], "k_norm_w": np.tile(a["k_norm_w"], 2)[:, None],
        "conv_w": a["conv_w"].reshape(3, KA, P).transpose(2, 0, 1).reshape(P, 12),
        "decay": np.broadcast_to(np.concatenate([a["decay_fwd_2"][0], a["decay_bwd_2"][0]]), (P, 8)),
    }
    params = np.concatenate([parts[n] if n in parts else _columns(a[n]) for n, _ in PARAMS], 1)
    arrays = {
        "params": params, "early": early, "late": late,
        "x": _feature_major(a["x"][0]), "ctx": _feature_major(a["ctx_2"][0]),
        "w_ada": _tiles(a["w_ada"], 512),
        "w_idx": _tiles(np.concatenate([ik, ik, iw], 1), 136),
        "w_in": np.concatenate([_tiles(w_in[:, o:o + 512], 512) for o in order]),
        "w_out": _tiles(a["w_out"], 512), "peer_wq": _tiles(a["peer_wq"], 512),
        "subkeys": a["peer_subkeys"].reshape(2 * PH, PK, P).transpose(2, 0, 1).reshape(1, P, 2 * PH * PK),
        "experts": np.concatenate([a["peer_u"], a["peer_v"]], 1),
        "w_ada_2": _tiles(a["w_ada_2"][0], 512),
        "w13_ffn1": _ffn_pairs(a["w13_ffn1_2"]), "w2_ffn1": _tiles(a["w2_ffn1_2"][0], P),
        "w13_ffn2": _ffn_pairs(a["w13_ffn2_2"]), "w2_ffn2": _tiles(a["w2_ffn2_2"][0], P),
        "w_in_2": _tiles(np.concatenate([_pairs_apart(w_in_2[:, 0:1024]), _pairs_apart(w_in_2[:, 1024:2048]),
                                         w_in_2[:, 2048:]], 1), 512),
        "p_ret": _tiles(a["p_ret_2"][0], 256), "p_four": _tiles(a["p_four_2"][0], 512),
        "w_out_2": _tiles(a["w_out_2"][0], 512),
    }
    nc = bacc.Bacc("TRN2", target_bir_lowering=False, num_devices=1)
    feeds, dram = {}, {}
    for name, array in arrays.items():
        feeds["in_" + name] = np.ascontiguousarray(array)
        dram[name] = nc.dram_tensor("in_" + name, array.shape, F32, kind="ExternalInput").ap()
    out = nc.dram_tensor("out_x", (P, KD * L), F32, kind="ExternalOutput").ap()
    program(nc, dram, out)
    got = run_bass_kernel_spmd(nc, [feeds], core_ids=[0]).results[0]["out_x"]
    return np.ascontiguousarray(np.asarray(got).reshape(P, KD, L).transpose(2, 1, 0)).reshape(1, L, D)
```

```python
from contextlib import ExitStack

import numpy as np

import concourse.bass as bass
from concourse import mybir

ALU = mybir.AluOpType
ACT = mybir.ActivationFunctionType
F32 = mybir.dt.float32
F32R = mybir.dt.float32r
U32 = mybir.dt.uint32
AX_X = mybir.AxisListType.X

P = 128
D = 1024
KD = D // P
L = 256
NT = L // P
EPS = 1e-6
BANKS = 8
BANK = 512

HEADS, HD = 8, 64
ATT = HEADS * HD
KA = ATT // P
TOPK = L // 4
PH, PK, PSEL = 8, 128, 16
EXPERTS = PK * PK
SLOTS = PH * PSEL
ATT_SCALE = HD ** -0.5
IDX_SCALE = (64 ** -0.5) * (8 ** -0.5)
FILL, TAKEN = -3.0e38, -3.2e38
MASKED = -1.0e30

RH, DK, DV = 4, 256, 512
FF = 2816
KF = FF // P
FG = 4
RING = 4
SLAB = 4096
SPLIT_RING = 3
PIECES = 4
PIECE = SLAB // PIECES
GBUF = 8
ROW = 2 * D
BATCH = 2
ROUND = 16

PARAMS = [("c", 8), ("c2", 16), ("b_ada", 48), ("b_ada_2", 72), ("norm1_w", 8), ("norm2_w", 8), ("q_norm_w", 1),
          ("k_norm_w", 1), ("conv_w", 12), ("conv_b", 4), ("attn_out_norm_w", 4), ("conv_out_norm_w", 4),
          ("norm_ffn1_2", 8), ("norm_mix_2", 8), ("ret_gn_w_2", 16), ("norm_ffn2_2", 8), ("norm_final_2", 8),
          ("decay", 8)]
EARLY = [("ident", P), ("pair", P), ("causal", NT * L), ("iota16", PSEL), ("age", 2 * NT)]
LATE_DECAY = 2 * NT * L * 2
LATE_DFT = 2 * 2 * 256
LATE_ROPE = 2 * L
LATE_XI = 2 * L


def offsets(table):
    at, out = 0, {}
    for name, width in table:
        out[name] = (at, width)
        at += width
    return out, at


PARAM_AT, PARAM_W = offsets(PARAMS)
EARLY_AT, EARLY_W = offsets(EARLY)


def shape_constants():
    tok = np.arange(L)
    causal = (tok[None, :] <= tok[:, None]).astype(np.float32).reshape(NT, P, L).transpose(1, 0, 2)
    pair = (np.arange(P)[:, None] // HD == np.arange(P)[None, :] // HD).astype(np.float32)
    age = np.stack([L - 1 - tok.reshape(NT, P), tok.reshape(NT, P)]).transpose(2, 0, 1).astype(np.float32)
    iota16 = np.broadcast_to(np.arange(PSEL, dtype=np.float32), (P, PSEL))
    early = np.concatenate([np.eye(P, dtype=np.float32), pair, causal.reshape(P, -1), iota16, age.reshape(P, -1)], 1)
    diff = (tok[None, :] - tok[:, None]).astype(np.float32)
    decay = np.stack([np.maximum(diff, 0), np.maximum(-diff, 0), diff >= 0, diff <= 0]).astype(np.float32)
    decay = decay.reshape(4, NT, P, L).transpose(2, 0, 1, 3).reshape(P, -1)
    ang = 2 * np.pi * (np.outer(np.arange(256), np.arange(256)) % 256) / 256
    dft = (np.concatenate([np.cos(ang), np.sin(ang)], 1) / 16).astype(np.float32)
    dft = dft.reshape(2, P, 512).transpose(1, 0, 2).reshape(P, -1)
    inv = (np.float32(10000.0) ** (-np.arange(64, dtype=np.float32) / 64)).astype(np.float32)
    row, col = (tok // 64).astype(np.float32), (tok % 64).astype(np.float32)
    turn = np.concatenate([inv[:, None] * row[None, :], inv[:, None] * col[None, :]], 0).astype(np.float32)
    rope = np.concatenate([np.cos(turn), np.sin(turn)], 1).astype(np.float32)
    xi = np.broadcast_to(np.concatenate([tok + 1, L - tok]).astype(np.float32), (P, 2 * L))
    late = np.concatenate([decay, dft, rope, xi], 1)
    return np.ascontiguousarray(early), np.ascontiguousarray(late)


def slab_order():
    ada = [("w_ada", i, SLAB) for i in range(12)]
    ffn = lambda n: [(f"w13_ffn{n}", i, SLAB) for i in range(11)] + [(f"w2_ffn{n}", i, KF * P) for i in range(8)]
    w_in_2 = {"q": (0, 2), "k": (2, 4), "v": (4, 8), "g": (8, 12), "f": (12, 14), "ga": (14, 16), "gf": (16, 18)}
    proj = lambda n: [("w_in_2", i, SLAB) for i in range(*w_in_2[n])]
    first = (ada[:4] + [("w_idx", 0, KD * 136)] + [("w_in", i, SLAB) for i in range(7)] + ada[4:]
             + [("w_out", i, SLAB) for i in range(2)] + [("peer_wq", i, SLAB) for i in range(4)]
             + [("subkeys", 0, 2 * PH * PK)])
    context = [("w_ada_2", i, SLAB) for i in range(18)] + ffn(1) + proj("k") + proj("v")
    second = (ffn(1) + proj("gf") + proj("f") + [("p_four", i, SLAB) for i in range(2)] + proj("ga") + proj("q")
              + proj("k") + proj("v") + proj("g") + [("p_ret", i, SLAB) for i in range(4)]
              + [("w_out_2", i, SLAB) for i in range(2)] + ffn(2))
    return first + context + second, len(first) + len(context)


def cuts(name, i):
    if name.startswith("w2_ffn"):
        return [(0, 8, 0, P), (8, 16, 0, P), (16, KF, 0, P)]
    if name == "p_ret":
        return [(8 * b, 8 * b + 8, c * P, (c + 1) * P) for c in range(2) for b in range(2)]
    if name == "w_in_2" and 4 <= i < 8:
        return [(2 * q, 2 * q + 2, 0, 4 * P) for q in range(4)]
    return [(0, KD, c * P, (c + 1) * P) for c in range(4)]


def slots_of(slabs, second_at):
    plan, users = [], {}
    for n in range(len(slabs)):
        slot = n % RING if n < second_at else (n - second_at) % SPLIT_RING
        users.setdefault(slot, []).append(n)
        plan.append((slot, len(users[slot]), users[slot][-2] if len(users[slot]) > 1 else None))
    return plan, [n for n in users[SPLIT_RING] if n < second_at][-1]


def program(nc, dram, out):
    slabs, second_at = slab_order()
    slots, last_in_split = slots_of(slabs, second_at)
    pieces = [(n,) + cut for n in range(second_at, len(slabs)) for cut in cuts(*slabs[n][:2])]
    with ExitStack() as ctx:
        def sb(name, width, dt=F32):
            return ctx.enter_context(nc.sbuf_tensor(name, [P, width], dt))

        def twin(name, width):
            plain = sb(name, width)
            return plain, nc.alloc_sbuf_tensor_at(name + "_r", [P, width], F32R, offset=nc.sbuf_base - 4 * width)

        sems = {}

        def sem(name):
            if name not in sems:
                sems[name] = ctx.enter_context(nc.semaphore(name))
            return sems[name]

        psum = ctx.enter_context(nc.psum_tensor("psum", [P, BANKS, BANK], F32))
        ring, ring_r = twin("ring", RING * SLAB)
        x_t = sb("x_t", KD * L)[:].rearrange("p (k t) -> p k t", k=KD)
        h_words, h_words_r = twin("h_t", KD * L)
        h_t, h_lo = (t[:].rearrange("p (k t) -> p k t", k=KD) for t in (h_words, h_words_r))
        prm = sb("prm", PARAM_W)
        early = sb("early", EARLY_W)
        ones = sb("ones", P)
        mod1 = sb("mod1", 48)
        mod2 = sb("mod2", 144)
        mod2_v = mod2[:].rearrange("p (m k s) -> p m k s", m=9, s=2)
        cols = sb("cols", 160)
        rstd = sb("rstd", L)
        arena, arena_r = twin("arena", 27648)
        small, small_r = twin("small", 2600)
        ids = sb("ids", NT * SLOTS, U32)
        idx_stage = sb("idx_stage", ROUND, U32)
        found = sb("found", 2 * PH * PSEL, U32)
        place = sb("place", SLOTS, U32)

        def param(name):
            at, w = PARAM_AT[name]
            return prm[:, at:at + w]

        def const(name):
            at, w = EARLY_AT[name]
            return early[:, at:at + w]

        ident = const("ident")

        silu_c, silu_c2 = cols[:, 0:8], cols[:, 8:24]
        scale_of = {}
        for i, key in enumerate(("n1", "n2", "ctx1", "ctx2", "x1", "x2", "x3")):
            scale_of[key] = cols[:, 24 + 8 * i:32 + 8 * i]
        half_gate = {"ctx1": cols[:, 80:88], "x1": cols[:, 88:96], "x3": cols[:, 96:104]}
        lg = cols[:, 104:112]
        lg_e, lg_z, lg_z2, lg_s = (cols[:, 112 + 8 * i:120 + 8 * i] for i in range(4))
        fade = cols[:, 144:160]

        ctx_t = arena[:, 0:2048].rearrange("p (k t) -> p k t", k=KD)
        h2 = arena[:, 2048:4096].rearrange("p (t d) -> p t d", t=NT)
        y_acc = arena[:, 4096:5120]
        y_of = [y_acc, h2[:, 0, :]]
        F0, G0 = 5120, 11264
        iq_t = arena[:, G0:G0 + 1024].rearrange("p (j t) -> p j t", j=4)
        ik_t = arena[:, G0 + 1024:G0 + 1280]
        idx = arena[:, G0 + 1280:G0 + 1792].rearrange("p (t s) -> p t s", t=NT)
        fill = arena[:, G0 + 1792:G0 + 2304].rearrange("p (t s) -> p t s", t=NT)
        bias = arena[:, G0 + 2304:G0 + 2816].rearrange("p (t s) -> p t s", t=NT)
        relu = arena[:, G0 + 2816:G0 + 3840].rearrange("p (b s) -> p b s", b=4)
        q_t = arena[:, G0 + 3840:G0 + 4864].rearrange("p (j t) -> p j t", j=KA)
        k_t = arena[:, G0 + 4864:G0 + 5888].rearrange("p (j t) -> p j t", j=KA)
        raw = arena[:, G0 + 5888:G0 + 7936].rearrange("p (a j t) -> p a j t", a=2, j=KA)
        raw_sq = arena[:, G0 + 7936:G0 + 9984].rearrange("p (a j t) -> p a j t", a=2, j=KA)
        y_mix = arena[:, G0 + 5888:G0 + 7936].rearrange("p (k t) -> p k t", k=KD)
        v_n = arena[:, G0 + 9984:G0 + 11008].rearrange("p (t d) -> p t d", t=NT)
        padded = arena[:, G0 + 11008:G0 + 12040].rearrange("p (j t) -> p j t", j=KA)
        y_conv = arena[:, G0 + 12040:G0 + 13064].rearrange("p (j t) -> p j t", j=KA)
        sq1 = arena[:, G0 + 13064:G0 + 15112].rearrange("p (k t) -> p k t", k=KD)
        gate_c = arena[:, 4096:5120].rearrange("p (j t) -> p j t", j=KA)
        p_t0 = arena[:, F0:F0 + 1024].rearrange("p (h q) -> p h q", h=HEADS)
        p_t1 = arena[:, F0 + 1024:F0 + 3072].rearrange("p (h s q) -> p h s q", h=HEADS, s=2)
        probs = arena[:, F0 + 3072:F0 + 5120].rearrange("p (h s) -> p h s", h=HEADS)
        y_att = arena[:, F0 + 5120:F0 + 6144].rearrange("p (j t) -> p j t", j=KA)
        pq_t = arena[:, G0:G0 + 4096].rearrange("p (h t) -> p h t", h=2 * PH)
        key_s = arena[:, F0:F0 + 4096].rearrange("p (t h n) -> p t h n", t=NT, h=2 * PH)
        combo = arena[:, F0 + 4096:F0 + 6144].rearrange("p (h n) -> p h n", h=PH)
        pick = h_t
        rows = [arena[:, G0 + i * ROW:G0 + (i + 1) * ROW] for i in range(GBUF)]
        top_v = small[:, 0:256].rearrange("p (h n) -> p h n", h=2 * PH)
        top_i = small[:, 256:512].rearrange("p (h n) -> p h n", h=2 * PH)
        best = small[:, 512:768].rearrange("p (t h n) -> p t h n", t=NT, h=PH)
        half_i = small[:, 768:1024]
        half_id = small[:, 1024:1280]
        id_f = small[:, 1280:1408]
        hsum = small[:, 1408:1424]
        dots = small[:, 1424:1424 + 16].rearrange("p (b n) -> p b n", b=8)
        acts = small[:, 1440:1456].rearrange("p (b n) -> p b n", b=8)
        weights = small[:, 1456:1472].rearrange("p (b n) -> p b n", b=8)
        max8 = small[:, 1472:1480]
        stat = small[:, 1480:1496]
        mxs = small[:, 1496:1504]
        iw = small[:, 1504:1520].rearrange("p (t h) -> p t h", t=NT)
        xi = small[:, 1536:2048].rearrange("p (a t) -> p a t", a=2)
        rope_tmp = small[:, 2048:2560].rearrange("p (b t) -> p b t", b=2)
        hid = arena[:, F0:F0 + KF * L].rearrange("p (k t) -> p k t", k=KF)
        kc = arena[:, F0:F0 + 2048].rearrange("p (t n) -> p t n", t=NT)
        vc = arena[:, F0 + 2048:F0 + 6144].rearrange("p (t n) -> p t n", t=NT)
        k_fade = [h_t[:, 2 * i:2 * i + 2, :] for i in range(4)]
        state = arena[:, G0 + 8192:G0 + 16384].rearrange("p (h a b v) -> p h a b v", h=RH, a=2, b=2)
        late_decay = arena[:, 2048:4096].rearrange("p (m t i) -> p m t i", m=4, t=NT)
        decay_t = arena[:, 0:2048].rearrange("p (h t i) -> p h t i", h=RH, t=NT)
        sq2 = small[:, 0:2048].rearrange("p (k t) -> p k t", k=KD)
        sig = arena[:, 2048:4096].rearrange("p (k t) -> p k t", k=KD)
        rope = arena[:, 4096:4608].rearrange("p (a t) -> p a t", a=2)
        late_xi = arena[:, 4608:5120].rearrange("p (a t) -> p a t", a=2)
        f_t = arena[:, F0:F0 + 2048].rearrange("p (k t) -> p k t", k=KD)
        mixed = arena[:, F0 + 2048:F0 + 4096].rearrange("p (k t) -> p k t", k=KD)
        m_t = arena[:, F0 + 4096:F0 + 6144].rearrange("p (k t) -> p k t", k=KD)
        dft_z = arena[:, G0:G0 + 4096].rearrange("p (t g a c) -> p t g a c", t=NT, g=FG, a=2)
        decay_tmp = arena[:, G0 + 5632:G0 + 6656].rearrange("p (a i) -> p a i", a=2)
        dft = arena[:, G0 + 6656:G0 + 7680].rearrange("p (k a c) -> p k a c", k=2, a=2)
        rq_t = arena[:, G0:G0 + 2048].rearrange("p (k t) -> p k t", k=KD)
        rk_t = arena[:, G0 + 2048:G0 + 4096].rearrange("p (k t) -> p k t", k=KD)
        rv = arena[:, F0:F0 + 4096].rearrange("p (t n) -> p t n", t=NT)
        rg_t = arena[:, G0 + 4096:G0 + 8192].rearrange("p (k t) -> p k t", k=16)
        q_faded = h_t[:, 0:4, :].rearrange("p (a k) t -> p a k t", a=2)
        sc_t = h_t[:, 4:6, :]
        o_n = h_t[:, 6:8, :].rearrange("p a t -> p (a t)")

        h_hi = small_r[:, 0:2048].rearrange("p (k t) -> p k t", k=KD)
        hid_lo = arena_r[:, F0:F0 + KF * L].rearrange("p (k t) -> p k t", k=KF)
        hid_hi = arena_r[:, G0:G0 + KF * L].rearrange("p (k t) -> p k t", k=KF)
        mixed_lo = arena_r[:, F0 + 2048:F0 + 4096].rearrange("p (k t) -> p k t", k=KD)
        mixed_hi = arena_r[:, F0:F0 + 2048].rearrange("p (k t) -> p k t", k=KD)
        m_lo = arena_r[:, F0 + 4096:F0 + 6144].rearrange("p (k t) -> p k t", k=KD)
        rg_lo = arena_r[:, G0 + 4096:G0 + 8192].rearrange("p (k t) -> p k t", k=16)
        rg_hi = arena_r[:, G0:G0 + 4096].rearrange("p (a h j t) -> p a h j t", a=2, h=RH, j=2)

        def whole(q, ring_of):
            n, k0, k1, c0, c1 = pieces[q]
            width = 512 if cuts(*slabs[n][:2])[-1][3] == 4 * P else slabs[n][2] // cuts(*slabs[n][:2])[-1][1]
            at = slots[n][0] * SLAB
            return ring_of[:, at:at + slabs[n][2]].rearrange("p (k n) -> p k n", n=width)[:, k0:k1, c0:c1]

        def upper(q):
            n, k0, k1, c0, c1 = pieces[q]
            at = SPLIT_RING * SLAB + (q % PIECES) * PIECE
            return ring_r[:, at:at + (k1 - k0) * (c1 - c0)].rearrange("p (k n) -> p k n", n=c1 - c0)

        group_done = sem("group_done")
        drained = {"act": sem("act_drained"), "dve": sem("dve_drained")}
        landed = [sem(f"slab_landed{i}") for i in range(RING)]
        row_landed = [sem(f"row_landed{i}") for i in range(GBUF)]

        groups, index, turn = [], {}, {"act": 0, "dve": 0}
        piece_read, piece_of = [], {}
        hi_made, lo_made, piece_done = sem("hi_made"), sem("lo_made"), sem("piece_done")
        slab_free = []

        def emptied(name):
            _, who, count = groups[index[name]]
            return drained[who], count

        block = ctx.enter_context(nc.Block())

        @block.tensor
        def _(pe):
            def begin(name, who):
                i = len(groups)
                if i >= BANKS:
                    pe.wait_ge(drained[groups[i - BANKS][1]], groups[i - BANKS][2])
                count = 1 + sum(g[1] == who for g in groups)
                groups.append((name, who, count))
                index[name] = i
                return psum[:, i % BANKS, :]

            def end(ins):
                ins.then_inc(group_done, 1)

            used = [0]

            def next_slab(name, i):
                n = used[0]
                assert slabs[n][:2] == (name, i), (slabs[n], name, i)
                used[0] += 1
                pe.wait_ge(landed[slots[n][0]], 16 * slots[n][1])
                at = slots[n][0] * SLAB
                return ring[:, at:at + slabs[n][2]]

            def release():
                slab_free.append(len(groups))

            def mm(o, a, b, first, last):
                return nc.tensor.matmul(o, a, b, start=first, stop=last)

            def by_feature(tag, array, ids_, src, who, kb=KD, after=None):
                n = 0
                for i in ids_:
                    w = next_slab(array, i).rearrange("p (k n) -> p k n", k=kb)
                    width = w.shape[2]
                    for b in range(0, width // P, 2):
                        o = begin(f"{tag}{n}", who(n) if callable(who) else who)
                        n += 1
                        for j in range(2):
                            for k in range(kb):
                                last = mm(o[:, j * L:(j + 1) * L], w[:, k, (b + j) * P:(b + j + 1) * P], src[:, k, :],
                                          k == 0, k == kb - 1)
                        end(last)
                    release()

            def by_token(tag, array, ids_, src, who):
                n = 0
                for i in ids_:
                    w = next_slab(array, i).rearrange("p (k n) -> p k n", k=KD)
                    for t in range(NT):
                        o = begin(f"{tag}{n}", who)
                        n += 1
                        for k in range(KD):
                            last = mm(o[:, 0:BANK], src[:, k, t * P:(t + 1) * P], w[:, k, :], k == 0, k == KD - 1)
                        end(last)
                    release()

            def squares(tag, sq, kb):
                pe.wait_ge(sem("sq_" + tag), 1)
                o = begin("ss_" + tag, "dve")
                for k in range(kb):
                    last = mm(o[:, 0:L], ones[:], sq[:, k, :], k == 0, k == kb - 1)
                end(last)

            def modulation(tag, array, ids_, src, width):
                for i in ids_:
                    w = next_slab(array, i).rearrange("p (k n) -> p k n", k=KD)
                    o = begin(f"{tag}{i}", "act")
                    for j in range(4):
                        for k in range(KD):
                            last = mm(o[:, j * width:(j + 1) * width], w[:, k, j * P:(j + 1) * P],
                                      src[:, k * width:(k + 1) * width], k == 0, k == KD - 1)
                    end(last)
                    release()

            def feed_forward(tag, n, src):
                for i in range(11):
                    w = next_slab(f"w13_ffn{n}", i).rearrange("p (k n) -> p k n", k=KD)
                    for half, who in ((0, "act"), (1, "dve")):
                        o = begin(f"{tag}_{'ab'[half]}{i}", who)
                        for j in range(2):
                            c = half * 256 + j * P
                            for k in range(KD):
                                last = mm(o[:, j * L:(j + 1) * L], w[:, k, c:c + P], src[:, k, :], k == 0, k == KD - 1)
                        end(last)
                    release()
                pe.wait_ge(*emptied(f"{tag}_b10"))
                for i in range(8):
                    w = next_slab(f"w2_ffn{n}", i).rearrange("p (k n) -> p k n", k=KF)
                    o = begin(f"{tag}_y{i}", "dve")
                    for k in range(KF):
                        last = mm(o[:, 0:L], w[:, k, :], hid[:, k, :], k == 0, k == KF - 1)
                    end(last)
                    release()

            def next_piece():
                q = len(piece_read)
                pe.wait_ge(lo_made, q + 1)
                return pieces[q][1:], upper(q), whole(q, ring_r)

            mid = [0]

            def piece_end(ins, name=None):
                if name:
                    end(ins)
                    piece_of[name] = len(piece_read)
                    piece_read.append((group_done, len(groups)))
                else:
                    mid[0] += 1
                    ins.then_inc(piece_done, 1)
                    piece_read.append((piece_done, mid[0]))
                n = pieces[len(piece_read) - 1][0]
                if len(piece_read) == len(pieces) or pieces[len(piece_read)][0] != n:
                    assert used[0] == n
                    used[0] += 1
                    release()

            def three(o, w_hi, w_lo, a_hi, a_lo, first, last):
                mm(o, w_hi, a_hi, first, False)
                mm(o, w_hi, a_lo, False, False)
                return mm(o, w_lo, a_hi, False, last)

            def split_feature(tag, count, hi, lo, who, kb=KD, need=None):
                need = need or {}
                for n in range(count):
                    o = begin(f"{tag}{n}", who)
                    for j in range(2):
                        for part in range(kb // KD):
                            (k0, k1, _, _), w_hi, w_lo = next_piece()
                            for k in range(k0, k1):
                                if k in need:
                                    pe.wait_ge(*need.pop(k))
                                last = three(o[:, j * L:(j + 1) * L], w_hi[:, k - k0, :], w_lo[:, k - k0, :],
                                             hi(k), lo[:, k, :], k == 0, k == kb - 1)
                            ends = j == 1 and part == kb // KD - 1
                            piece_end(last, f"{tag}{n}" if ends else None)

            def split_token(tag, count):
                for i in range(count):
                    o = [begin(f"{tag}{NT * i + t}", "act") for t in range(NT)]
                    for part in range(4):
                        (k0, k1, _, _), w_hi, w_lo = next_piece()
                        for t in range(NT):
                            ts = slice(t * P, (t + 1) * P)
                            for k in range(k0, k1):
                                mm(o[t], h_hi[:, k, ts], w_hi[:, k - k0, :], k == 0, False)
                                mm(o[t], h_lo[:, k, ts], w_hi[:, k - k0, :], False, False)
                                last = mm(o[t], h_hi[:, k, ts], w_lo[:, k - k0, :], False, k == KD - 1)
                            if part == 3 and t < NT - 1:
                                end(last)
                        piece_end(last, f"{tag}{NT * i + NT - 1}" if part == 3 else None)
                    piece_of[f"{tag}{NT * i}"] = piece_of[f"{tag}{NT * i + 1}"]

            def norm_need(m):
                return {k: (sem("h_split"), KD * m + k + 1) for k in range(KD)}

            def h_hi_of(k):
                return h_hi[:, k, :]

            def split_feed_forward(tag, m, f):
                need = norm_need(m)
                for i in range(11):
                    for half, who in ((0, "act"), (1, "dve")):
                        name = f"{tag}_{'ab'[half]}{i}"
                        o = begin(name, who)
                        for j in range(2):
                            _, w_hi, w_lo = next_piece()
                            for k in range(KD):
                                if k in need:
                                    pe.wait_ge(*need.pop(k))
                                last = three(o[:, j * L:(j + 1) * L], w_hi[:, k, :], w_lo[:, k, :], h_hi[:, k, :],
                                             h_lo[:, k, :], k == 0, k == KD - 1)
                            piece_end(last, name if j else None)
                for i in range(8):
                    o = begin(f"{tag}_y{i}", "dve")
                    for part in range(3):
                        (k0, k1, _, _), w_hi, w_lo = next_piece()
                        if i == 0:
                            pe.wait_ge(sem("hid_split"), 11 * f + k1 // 2)
                        for k in range(k0, k1):
                            last = three(o[:, 0:L], w_hi[:, k - k0, :], w_lo[:, k - k0, :], hid_hi[:, k, :],
                                         hid_lo[:, k, :], k == 0, k == KF - 1)
                        piece_end(last, f"{tag}_y{i}" if part == 2 else None)

            def squares_by_block(tag):
                o = begin("ss_" + tag, "dve")
                for k in range(KD):
                    pe.wait_ge(sem("sq_" + tag), k + 1)
                    last = mm(o[:, 0:L], ones[:], sq2[:, k, :], k == 0, k == KD - 1)
                end(last)

            pe.wait_ge(sem("ones"), 1)
            pe.wait_ge(sem("params"), 48)
            pe.wait_ge(sem("silu_c"), 2)
            modulation("ada", "w_ada", range(4), silu_c, 1)
            squares("n1", sq1, KD)
            pe.wait_ge(sem("h_n1"), 1)
            w = next_slab("w_idx", 0).rearrange("p (k n) -> p k n", k=KD)
            o = begin("ik", "act")
            for k in range(KD):
                last = mm(o[:, 0:L], w[:, k, 0:P], h_t[:, k, :], k == 0, k == KD - 1)
            end(last)
            o = begin("iw", "act")
            for t in range(NT):
                for k in range(KD):
                    last = mm(o[:, t * 8:t * 8 + 8], h_t[:, k, t * P:(t + 1) * P], w[:, k, P:P + 8], k == 0, k == KD - 1)
            end(last)
            release()
            by_feature("iq", "w_in", [0], h_t, "act")
            pe.wait_ge(*emptied("iq1"))
            for t in range(NT):
                for h in range(8):
                    r = 64 * (h % 2)
                    n = (t + 1) * P
                    o = begin(f"is{t}_{h}", "act")
                    end(mm(o[:, 0:n], iq_t[r:r + 64, h // 2, t * P:(t + 1) * P], ik_t[r:r + 64, 0:n], True, True))
            by_feature("q", "w_in", [1], h_t, "act")
            by_feature("k", "w_in", [2], h_t, "act")
            by_token("v", "w_in", [3], h_t, "act")
            for a, tag in ((0, "q"), (1, "k")):
                for i in range(2):
                    pe.wait_ge(*emptied(f"{tag}{i}"))
                    o = begin(f"{tag}ss{i}", "dve")
                    end(mm(o[:, 0:BANK], const("pair"), raw_sq[:, a, 2 * i:2 * i + 2, :].rearrange("p j t -> p (j t)"),
                           True, True))
            by_feature("cc", "w_in", [4], h_t, "act")
            by_feature("cx", "w_in", [5], h_t, "dve")
            by_feature("cb", "w_in", [6], h_t, "dve")
            modulation("ada", "w_ada", range(4, 12), silu_c, 1)
            squares("conv", sq1, KA)
            pe.wait_ge(sem("qk_ready"), 4)
            for t in range(NT):
                n = (t + 1) * P
                for h in range(HEADS):
                    r = 64 * (h % 2)
                    o = begin(f"at{t}_{h}", "dve")
                    end(mm(o[:, 0:n], q_t[r:r + 64, h // 2, t * P:(t + 1) * P], k_t[r:r + 64, h // 2, 0:n], True, True))
                pe.wait_ge(sem("probs"), t + 1)
                for i in range(2 * (t + 1)):
                    o = begin(f"pt{t}_{i}", "act")
                    for j in range(4):
                        h, s = divmod(4 * i + j, t + 1)
                        last = nc.tensor.transpose(o[:, j * P:(j + 1) * P], probs[:, h, s * P:(s + 1) * P], ident)
                    end(last)
            pe.wait_ge(*emptied("pt1_3"))
            for j in range(KA):
                o = begin(f"pv{j}", "act")
                for h in (2 * j, 2 * j + 1):
                    c = (h % 2) * L
                    last = mm(o[:, c:c + P], v_n[:, 0, j * P:(j + 1) * P], p_t0[:, h, :], True, True)
                    for s in range(2):
                        last = mm(o[:, c + P:c + L], v_n[:, s, j * P:(j + 1) * P], p_t1[:, h, s, :], s == 0, s == 1)
                end(last)
            squares("att", sq1, KA)
            pe.wait_ge(sem("y_mix"), 2)
            by_feature("wo", "w_out", range(2), y_mix, "dve")
            squares("n2", sq1, KD)
            pe.wait_ge(sem("h_n2"), 1)
            by_feature("pq", "peer_wq", range(4), h_t, "act")
            for t in range(NT):
                for i in range(2):
                    o = begin(f"ht{t}_{i}", "act")
                    for j in range(4):
                        last = nc.tensor.transpose(o[:, j * P:(j + 1) * P], h_t[:, 4 * i + j, t * P:(t + 1) * P], ident)
                    end(last)
            pe.wait_ge(*emptied("pq7"))
            w = next_slab("subkeys", 0).rearrange("p (h n) -> p h n", h=2 * PH)
            for t in range(NT):
                for i in range(4):
                    o = begin(f"ks{t}_{i}", "act")
                    for j in range(4):
                        hp = 4 * i + j
                        last = mm(o[:, j * P:(j + 1) * P], pq_t[:, hp, t * P:(t + 1) * P], w[:, hp, :], True, True)
                    end(last)
            release()

            modulation("ada2_", "w_ada_2", range(18), silu_c2, 2)
            squares("ctx1", hid, KD)
            pe.wait_ge(sem("h_ctx1"), 1)
            feed_forward("fc", 1, h_t)
            squares("ctx2", hid, KD)
            pe.wait_ge(sem("h_ctx2"), 1)
            by_token("kc", "w_in_2", range(2, 4), h_t, "act")
            by_token("vc", "w_in_2", range(4, 8), h_t, "act")

            for t in range(NT):
                pe.wait_ge(sem("experts"), t + 1)
                for i in range(2):
                    o = begin(f"yt{t}_{i}", "dve")
                    for j in range(4):
                        last = nc.tensor.transpose(o[:, j * P:(j + 1) * P],
                                                   y_of[t][:, (4 * i + j) * P:(4 * i + j + 1) * P], ident)
                    end(last)
            for h in range(RH):
                for a in range(2):
                    pe.wait_ge(sem("k_fade"), 2 * h + a + 1)
                    for b in range(2):
                        o = begin(f"st{h}_{a}_{b}", "act")
                        for t in range(NT):
                            last = mm(o[:, 0:DV], k_fade[(2 * h + a) % 4][:, t, b * P:(b + 1) * P],
                                      vc[:, t, h * DV:(h + 1) * DV], t == 0, t == 1)
                        end(last)
            squares_by_block("x1")
            split_feed_forward("f1", 0, 0)
            squares_by_block("x2")
            split_feature("gf", 4, h_hi_of, h_lo, "act", need=norm_need(1))
            split_feature("f", 4, h_hi_of, h_lo, "act")
            pe.wait_ge(*emptied("f3"))
            pe.wait_ge(sem("late"), 64)
            for t in range(NT):
                for g in range(FG):
                    o = begin(f"z{t}_{g}", "act")
                    for k in range(2):
                        last = mm(o[:, 0:BANK], f_t[:, 2 * g + k, t * P:(t + 1) * P],
                                  dft[:, k, :, :].rearrange("p a c -> p (a c)"), k == 0, k == 1)
                    end(last)
            pe.wait_ge(*emptied("z1_3"))
            for i in range(4):
                o = begin(f"mx{i}", "dve")
                for j in range(2):
                    n = 0
                    for t in range(NT):
                        for a in range(2):
                            last = mm(o[:, j * L:(j + 1) * L], dft_z[:, t, i, a, j * P:(j + 1) * P], dft[:, t, a, :],
                                      n == 0, n == 3)
                            n += 1
                end(last)
            split_feature("pf", 4, lambda k: mixed_hi[:, k, :], mixed_lo, "dve",
                          need={k: emptied(f"mx{k // 2}") for k in range(0, KD, 2)})
            split_feature("ga", 4, h_hi_of, h_lo, "act")
            split_feature("rq", 4, h_hi_of, h_lo, "dve")
            split_feature("rk", 4, h_hi_of, h_lo, "dve")
            split_token("rv", 4)
            split_feature("rg", 8, h_hi_of, h_lo, "act")
            for h in range(RH):
                pe.wait_ge(sem("q_faded"), h + 1)
                o = begin(f"sc{h}", "dve")
                for t in range(NT):
                    for b in range(2):
                        last = mm(o[:, t * L:(t + 1) * L], rk_t[:, 2 * h + b, t * P:(t + 1) * P], rq_t[:, 2 * h + b, :],
                                  b == 0, b == 1)
                end(last)
                for t in range(NT):
                    o = begin(f"o{h}_{t}", "dve")
                    n = 0
                    for a in range(2):
                        for b in range(2):
                            mm(o[:, 0:DV], q_faded[:, a, b, t * P:(t + 1) * P], state[:, h, a, b, :], n == 0, False)
                            n += 1
                    pe.wait_ge(*emptied(f"sc{h}"))
                    for s in range(NT):
                        last = mm(o[:, 0:DV], sc_t[:, s, t * P:(t + 1) * P], rv[:, s, h * DV:(h + 1) * DV],
                                  False, s == 1)
                    end(last)
                for t in range(NT):
                    pe.wait_ge(*emptied(f"o{h}_{t}"))
                    o = begin(f"ot{h}_{t}", "dve")
                    for j in range(4):
                        last = nc.tensor.transpose(o[:, j * P:(j + 1) * P], o_n[:, j * P:(j + 1) * P], ident)
                    end(last)
            split_feature("pr", 4, lambda k: rg_hi[:, k % 4 // 2, k // 4, k % 2, :], rg_lo, "dve", kb=16,
                          need={4 * h: (sem("rg_split"), h + 1) for h in range(RH)})
            split_feature("w2o", 4, lambda k: mixed_hi[:, k, :], m_lo, "dve",
                          need={2 * i: (sem("m_split"), i + 1) for i in range(4)})
            squares_by_block("x3")
            split_feed_forward("f2", 2, 1)
            squares_by_block("fin")
            assert used[0] == len(slabs)

        @block.sync
        def _(sp):
            for src, dst in (("params", prm), ("early", early), ("x", x_t)):
                d = dst[:] if src != "x" else x_t.rearrange("p k t -> p (k t)")
                sp.dma_start(d, dram[src]).then_inc(sem("params"), 16)
            for n, (name, i, words) in enumerate(slabs):
                if n == 8:
                    sp.dma_start(ctx_t.rearrange("p k t -> p (k t)"), dram["ctx"]).then_inc(sem("ctx_landed"), 16)
                slot, _, replaced = slots[n]
                if replaced is not None:
                    sp.wait_ge(group_done, slab_free[replaced])
                at = slot * SLAB
                sp.dma_start(ring[:, at:at + words], dram[name][i]).then_inc(landed[slot], 16)
                if n == second_at + SPLIT_RING - 1:
                    sp.wait_ge(sem("experts_added"), 1)
                    at = 0
                    for dst, w in ((late_decay, LATE_DECAY), (dft, LATE_DFT), (rope, LATE_ROPE), (late_xi, LATE_XI)):
                        s = "p m t i -> p (m t i)" if w == LATE_DECAY else (
                            "p k a c -> p (k a c)" if w == LATE_DFT else "p a t -> p (a t)")
                        sp.dma_start(dst.rearrange(s), dram["late"][:, at:at + w]).then_inc(sem("late"), 16)
                        at += w
            sp.wait_ge(sem("out_ready"), 1)
            sp.dma_start(out, h_t.rearrange("p k t -> p (k t)")).then_inc(sem("stored"), 16)
            sp.wait_ge(sem("stored"), 16)

        @block.gpsimd
        def _(pool):
            staged = sem("staged")
            for t in range(NT):
                pool.wait_ge(sem("ids"), t + 1)
                with pool.Fori(0, SLOTS // ROUND) as r:
                    for half in range(2):
                        n = ROUND // 2
                        pool.wait_ge(sem("row_free"), r * ROUND + (t * SLOTS + half * n + 1))
                        nc.gpsimd.tensor_copy(idx_stage[:, half * n:(half + 1) * n],
                                              ids[:, bass.ds(r * ROUND + (t * SLOTS + half * n), n)]).then_inc(staged, 1)
                        pool.wait_ge(staged, r * 2 + (t * 2 * SLOTS // ROUND + half + 1))
                        for s in range(n):
                            slot = half * n + s
                            pool.wait_ge(sem("row_free"), r * ROUND + (t * SLOTS + slot + 1))
                            pool.sem_inc(sem("row_turn"), 1)
                            nc.gpsimd.indirect_dma_start(
                                rows[slot % GBUF], None, dram["experts"],
                                bass.IndirectOffsetOnAxis(ap=idx_stage[:, slot:slot + 1], axis=0),
                            ).then_inc(row_landed[slot % GBUF], 16)

        @block.scalar
        def _(act):
            taken, roots = [0], [0]

            def root(ap):
                roots[0] += 1
                act.wait_ge(sem("root_in"), roots[0])
                nc.scalar.activation(ap, ap, ACT.Sqrt).then_inc(sem("root_out"), 1)

            hi_count = [0]

            def split_until(q):
                while hi_count[0] <= min(q, len(pieces) - 1):
                    i = hi_count[0]
                    hi_count[0] += 1
                    if i >= PIECES:
                        act.wait_ge(*piece_read[i - PIECES])
                    elif i == 0:
                        act.wait_ge(group_done, slab_free[last_in_split])
                    slot, loads, _ = slots[pieces[i][0]]
                    act.wait_ge(landed[slot], 16 * loads)
                    nc.scalar.activation(upper(i), whole(i, ring), ACT.Copy).then_inc(hi_made, 1)

            def ahead(name):
                split_until(piece_of[name] + PIECES - 1)

            def take(name):
                _, who, count = groups[index[name]]
                if name in piece_of:
                    ahead(name)
                taken[0] += 1
                assert who == "act" and count == taken[0], (name, who, count, taken[0])
                act.wait_ge(group_done, index[name] + 1)
                return psum[:, index[name] % BANKS, :]

            def drain(ins):
                ins.then_inc(drained["act"], 1)

            def flat(ap):
                return ap.rearrange("p a t -> p (a t)")

            def copy_out(name, dst, func=ACT.Copy, width=BANK, scale=1.0):
                drain(nc.scalar.activation(dst, take(name)[:, 0:width], func, scale=scale))

            def square(tag, dst, src, kb):
                nc.scalar.activation(flat(dst[:, 0:kb, :]), flat(src), ACT.Square).then_inc(sem("sq_" + tag), 1)

            def norm_hi(tag, m, shift, names):
                for k in range(KD):
                    if names:
                        name = names[k * len(names) // KD]
                        ahead(name)
                        act.wait_ge(*emptied(name))
                    nc.scalar.activation(sq2[:, k, :], x_t[:, k, :], ACT.Square).then_inc(sem("sq_" + tag), 1)
                root(rstd[:])
                if m is not None:
                    for k in range(KD):
                        act.wait_ge(sem("h_scaled"), KD * m + k + 1)
                        nc.scalar.activation(h_hi[:, k, :], h_t[:, k, :], ACT.Identity,
                                             bias=shift[:, k:k + 1]).then_inc(sem("h_hi"), 1)

            def decay_exp(n):
                h, a = divmod(n, 2)
                if n >= 2:
                    act.wait_ge(sem("decay_used"), n - 1)
                nc.scalar.activation(decay_tmp[:, a], late_decay[:, a].rearrange("p t i -> p (t i)"), ACT.Exp,
                                     scale=lg[:, 4 * a + h:4 * a + h + 1]).then_inc(sem("decay_exp"), 1)

            def split_ff_act(tag, f):
                for i in range(12):
                    if i < 11:
                        drain(nc.scalar.activation(flat(hid[:, 2 * i:2 * i + 2, :]), take(f"{tag}_a{i}"), ACT.Silu))
                    else:
                        ahead(f"{tag}_b10")
                    if f == 0 and i < 2 * RH:
                        decay_exp(i)
                    if i:
                        act.wait_ge(*emptied(f"{tag}_b{i - 1}"))
                        nc.scalar.activation(flat(hid_hi[:, 2 * i - 2:2 * i, :]), flat(hid[:, 2 * i - 2:2 * i, :]),
                                             ACT.Copy).then_inc(sem("hid_hi"), 1)

            def ff_act(tag):
                for i in range(11):
                    drain(nc.scalar.activation(flat(hid[:, 2 * i:2 * i + 2, :]), take(f"{tag}_a{i}"), ACT.Silu))
                    yield
                for i in range(8):
                    yield

            act.wait_ge(sem("params"), 48)
            nc.scalar.activation(silu_c, param("c"), ACT.Silu).then_inc(sem("silu_c"), 1)
            nc.scalar.activation(silu_c2, param("c2"), ACT.Silu).then_inc(sem("silu_c"), 1)
            square("n1", sq1, x_t, KD)
            for i in range(4):
                copy_out(f"ada{i}", mod1[:, 4 * i:4 * i + 4], width=4)
            root(rstd[:])
            act.wait_ge(sem("lg_abs"), 1)
            nc.scalar.activation(lg_e, lg_z, ACT.Exp, scale=-1.0).then_inc(sem("lg_exp"), 1)
            copy_out("ik", ik_t, width=L)
            copy_out("iw", iw.rearrange("p t h -> p (t h)"), width=16)
            for i in range(2):
                copy_out(f"iq{i}", flat(iq_t[:, 2 * i:2 * i + 2, :]))
            for t in range(NT):
                for h in range(8):
                    n = 8 * t + h
                    if n >= 4:
                        act.wait_ge(sem("relu_used"), n - 3)
                    copy_out(f"is{t}_{h}", relu[:, n % 4, 0:(t + 1) * P], ACT.Relu, (t + 1) * P)
            for a, tag in ((0, "q"), (1, "k")):
                for i in range(2):
                    o = take(f"{tag}{i}")
                    nc.scalar.activation(flat(raw[:, a, 2 * i:2 * i + 2, :]), o, ACT.Copy)
                    drain(nc.scalar.activation(flat(raw_sq[:, a, 2 * i:2 * i + 2, :]), o, ACT.Square))
            for t in range(NT):
                copy_out(f"v{t}", v_n[:, t, :])
            for i in range(2):
                copy_out(f"cc{i}", flat(gate_c[:, 2 * i:2 * i + 2, :]))
            for a in range(2):
                for i in range(2):
                    root(flat(raw_sq[:, a, 2 * i:2 * i + 2, :]))
            for i in range(4, 12):
                copy_out(f"ada{i}", mod1[:, 4 * i:4 * i + 4], width=4)
            act.wait_ge(sem("y_conv"), 1)
            square("conv", sq1, y_conv, KA)
            root(rstd[:])
            for t in range(NT):
                n = (t + 1) * P
                act.wait_ge(sem("shifted"), t + 1)
                nc.scalar.activation(probs[:, :, 0:n], probs[:, :, 0:n], ACT.Exp, scale=ATT_SCALE).then_inc(sem("exped"), 1)
                for i in range(2 * (t + 1)):
                    dst = p_t0[:, 4 * i:4 * i + 4, :] if t == 0 else p_t1[:, 2 * i:2 * i + 2, :, :]
                    s = "p h q -> p (h q)" if t == 0 else "p h s q -> p (h s q)"
                    copy_out(f"pt{t}_{i}", dst.rearrange(s))
            for j in range(KA):
                o = take(f"pv{j}")
                nc.scalar.activation(y_att[0:64, j, :], o[0:64, 0:L], ACT.Copy)
                drain(nc.scalar.activation(y_att[64:128, j, :], o[64:128, L:2 * L], ACT.Copy))
            act.wait_ge(sem("conv_mixed"), 1)
            act.wait_ge(drained["act"], taken[0])
            square("att", sq1, y_att, KA)
            root(rstd[:])
            act.wait_ge(*emptied("wo3"))
            square("n2", sq1, x_t, KD)
            root(rstd[:])
            for i in range(8):
                copy_out(f"pq{i}", flat(pq_t[:, 2 * i:2 * i + 2, :]))
            for t in range(NT):
                for i in range(2):
                    copy_out(f"ht{t}_{i}", h2[:, t, i * BANK:(i + 1) * BANK])
            for t in range(NT):
                for i in range(4):
                    copy_out(f"ks{t}_{i}", key_s[:, t, 4 * i:4 * i + 4, :].rearrange("p h n -> p (h n)"))

            def background():
                for i in range(28):
                    if i < 18:
                        copy_out(f"ada2_{i}", mod2[:, 8 * i:8 * i + 8], width=8)
                    yield
                act.wait_ge(sem("ctx_landed"), 16)
                act.wait_ge(sem("ids"), 2)
                square("ctx1", hid, ctx_t, KD)
                root(rstd[:])
                yield
                yield from ff_act("fc")
                act.wait_ge(*emptied("fc_y7"))
                square("ctx2", hid, ctx_t, KD)
                root(rstd[:])
                yield
                act.wait_ge(sem("h_ctx2"), 1)
                for i in range(12):
                    c, t = divmod(i, 2)
                    if c < 2:
                        copy_out(f"kc{i}", kc[:, t, c * BANK:(c + 1) * BANK])
                    else:
                        copy_out(f"vc{i - 4}", vc[:, t, (c - 2) * BANK:(c - 1) * BANK])
                    yield

            bg = background()
            for t in range(NT):
                act.wait_ge(sem("best"), t + 1)
                flat_best = best[:, t].rearrange("p h n -> p (h n)")
                nc.scalar.activation(flat_best, flat_best, ACT.Exp).then_inc(sem("best_exp"), 1)
                for b in range(SLOTS // BATCH):
                    n = t * (SLOTS // BATCH) + b
                    act.wait_ge(sem("dots"), BATCH * (n + 1))
                    nc.scalar.activation(acts[:, n % 8, :], dots[:, n % 8, :], ACT.Gelu_apprx_tanh).then_inc(sem("gelus"), 1)
                    if b % 2 == 1:
                        next(bg, None)
            for _ in bg:
                pass
            act.wait_ge(sem("lg"), 1)
            for a in range(2):
                for t in range(NT):
                    at = EARLY_AT["age"][0] + 2 * a + t
                    for h in range(RH):
                        c = (a * NT + t) * RH + h
                        last = nc.scalar.activation(fade[:, c:c + 1], early[:, at:at + 1], ACT.Exp,
                                                    scale=lg[:, 4 * a + h:4 * a + h + 1])
            last.then_inc(sem("fade"), 1)
            act.wait_ge(sem("experts_added"), 1)
            for h in range(RH):
                for a in range(2):
                    for b in range(2):
                        copy_out(f"st{h}_{a}_{b}", state[:, h, a, b, :])
            split_until(PIECES - 1)
            norm_hi("x1", 0, mod2_v[:, 0, :, 0], None)
            act.wait_ge(sem("late"), 64)
            split_ff_act("f1", 0)
            norm_hi("x2", 1, mod2_v[:, 3, :, 0], [f"f1_y{i}" for i in range(8)])
            for i in range(4):
                copy_out(f"gf{i}", flat(sig[:, 2 * i:2 * i + 2, :]), ACT.Sigmoid)
            for i in range(4):
                copy_out(f"f{i}", flat(f_t[:, 2 * i:2 * i + 2, :]))
            for t in range(NT):
                for g in range(FG):
                    o = take(f"z{t}_{g}")
                    nc.scalar.activation(dft_z[:, t, g, 0, :], o[:, 0:256], ACT.Copy)
                    drain(nc.scalar.activation(dft_z[:, t, g, 1, :], o[:, 256:512], ACT.Copy, scale=-1.0))
            for i in range(4):
                act.wait_ge(group_done, index[f"mx{i}"] + 1)
                nc.scalar.activation(flat(mixed_hi[:, 2 * i:2 * i + 2, :]), psum[:, index[f"mx{i}"] % BANKS, :],
                                     ACT.Copy).then_inc(sem("mixed_hi"), 1)
            ahead("pf3")
            act.wait_ge(*emptied("pf3"))
            for i in range(4):
                copy_out(f"ga{i}", flat(sig[:, 2 * i:2 * i + 2, :]), ACT.Sigmoid)
            for i in range(8):
                c, t = divmod(i, 2)
                copy_out(f"rv{i}", rv[:, t, c * BANK:(c + 1) * BANK])
            for i in range(8):
                copy_out(f"rg{i}", flat(rg_t[:, 2 * i:2 * i + 2, :]), ACT.Silu)
            for h in range(RH + 1):
                if h:
                    act.wait_ge(sem("q_faded"), h)
                if h < RH:
                    for a in range(2):
                        last = nc.scalar.activation(xi[:, a, :], late_xi[:, a, :], ACT.Exp,
                                                    scale=lg[:, 4 * a + h:4 * a + h + 1])
                    last.then_inc(sem("xi"), 1)
                if h:
                    for t in range(NT):
                        root(stat[:, 8:9])
                    act.wait_ge(sem("turned"), h)
                    nc.scalar.activation(rg_hi[:, :, h - 1].rearrange("p a j t -> p a (j t)"),
                                         rg_t[:, 4 * h - 4:4 * h, :].rearrange("p (a j) t -> p a (j t)", a=2),
                                         ACT.Copy).then_inc(sem("rg_hi"), 1)
            for i in range(4):
                ahead(f"pr{i}")
                act.wait_ge(sem("merged"), i + 1)
                nc.scalar.activation(flat(mixed_hi[:, 2 * i:2 * i + 2, :]), flat(m_t[:, 2 * i:2 * i + 2, :]),
                                     ACT.Copy).then_inc(sem("m_hi"), 1)
            norm_hi("x3", 2, mod2_v[:, 6, :, 0], [f"w2o{i}" for i in range(4)])
            split_ff_act("f2", 1)
            norm_hi("fin", None, None, [f"f2_y{i}" for i in range(8)])
            assert taken[0] == sum(g[1] == "act" for g in groups)

        @block.vector
        def _(v):
            taken, steps, roots = [0], {}, [0]
            chain = sem("dve_step")

            def step(ins, s=chain):
                ins.then_inc(s, 1)
                steps[s.name] = steps.get(s.name, 0) + 1
                v.wait_ge(s, steps[s.name])

            lo_count = [0]

            def split_until(q):
                while lo_count[0] <= min(q, len(pieces) - 1):
                    i = lo_count[0]
                    lo_count[0] += 1
                    v.wait_ge(hi_made, i + 1)
                    nc.vector.tensor_tensor(whole(i, ring_r), whole(i, ring), upper(i).bitcast(F32),
                                            ALU.subtract).then_inc(lo_made, 1)

            def ahead(name):
                split_until(piece_of[name] + PIECES - 1)

            def take(name):
                _, who, count = groups[index[name]]
                if name in piece_of:
                    ahead(name)
                taken[0] += 1
                assert who == "dve" and count == taken[0], (name, who, count, taken[0])
                v.wait_ge(group_done, index[name] + 1)
                return psum[:, index[name] % BANKS, :]

            def drain(ins):
                step(ins, drained["dve"])

            def flat(ap):
                return ap.rearrange("p a t -> p (a t)")

            TT, TS, STT = nc.vector.tensor_tensor, nc.vector.tensor_scalar, nc.vector.scalar_tensor_tensor

            def rooted(dst):
                roots[0] += 1
                step(nc.vector.reciprocal(dst, dst), sem("root_in"))
                v.wait_ge(sem("root_out"), roots[0])

            def root(name, dst, width, n):
                drain(TS(dst, take(name)[:, 0:width], 1.0 / n, EPS, ALU.mult, ALU.add))
                rooted(dst)

            def modulated(tag, src, dst, weight, scale, shift):
                step(STT(scale_of[tag], scale, 1.0, weight, ALU.add, ALU.mult))
                root("ss_" + tag, rstd[:], L, D)
                step(TT(dst, src, rstd[:].unsqueeze(1).to_broadcast([P, KD, L]), ALU.mult))
                for k in range(KD):
                    last = TS(dst[:, k, :], dst[:, k, :], scale_of[tag][:, k:k + 1], shift[:, k:k + 1], ALU.mult, ALU.add)
                    if k < KD - 1:
                        last.then_inc(chain, 1)
                        steps[chain.name] += 1
                step(last, sem("h_" + tag))

            def rest(dst, src, hi, s):
                step(TT(dst, src, hi.bitcast(F32), ALU.subtract), sem(s))

            def split_modulated(tag, m, weight, scale, shift):
                step(STT(scale_of[tag], scale, 1.0, weight, ALU.add, ALU.mult))
                root("ss_" + tag, rstd[:], L, D)
                for k in range(KD + 2):
                    if k < KD:
                        STT(h_t[:, k, :], x_t[:, k, :], scale_of[tag][:, k:k + 1], rstd[:], ALU.mult,
                            ALU.mult).then_inc(sem("h_scaled"), 1)
                    if k >= 2:
                        b = k - 2
                        v.wait_ge(sem("h_hi"), KD * m + b + 1)
                        STT(h_lo[:, b, :], h_t[:, b, :], shift[:, b:b + 1], h_hi[:, b, :].bitcast(F32), ALU.add,
                            ALU.subtract).then_inc(sem("h_split"), 1)

            def decay(n):
                h, a = divmod(n, 2)
                v.wait_ge(sem("decay_exp"), n + 1)
                mask = flat(late_decay[:, 2 + a])
                if a == 0:
                    step(TT(flat(decay_t[:, h]), decay_tmp[:, 0], mask, ALU.mult), sem("decay_used"))
                else:
                    step(TT(decay_tmp[:, 1], decay_tmp[:, 1], mask, ALU.mult))
                    step(TT(flat(decay_t[:, h]), flat(decay_t[:, h]), decay_tmp[:, 1], ALU.add), sem("decay_used"))

            def split_ff_dve(tag, f, gate):
                for i in range(12):
                    if i < 11:
                        o = take(f"{tag}_b{i}")
                        v.wait_ge(*emptied(f"{tag}_a{i}"))
                        hb = flat(hid[:, 2 * i:2 * i + 2, :])
                        drain(TT(hb, hb, o, ALU.mult))
                    if i:
                        v.wait_ge(sem("hid_hi"), 11 * f + i)
                        rest(flat(hid_lo[:, 2 * i - 2:2 * i, :]), flat(hid[:, 2 * i - 2:2 * i, :]),
                             flat(hid_hi[:, 2 * i - 2:2 * i, :]), "hid_split")
                    if f == 0 and i < 2 * RH:
                        decay(i)
                for i in range(8):
                    drain(STT(x_t[:, i, :], take(f"{tag}_y{i}")[:, 0:L], gate[:, i:i + 1], x_t[:, i, :],
                              ALU.mult, ALU.add))

            def mix(src, dst, k0, weight):
                for j in range(KA):
                    step(STT(dst[:, k0 + j, :], src[:, j, :], weight[:, j:j + 1], rstd[:], ALU.mult, ALU.mult),
                         sem("y_mix") if j == KA - 1 else chain)

            def residual(names, dst, gate, per):
                n = 0
                for name in names:
                    o = take(name)
                    for j in range(per):
                        ins = STT(dst[:, n, :], o[:, j * L:(j + 1) * L], gate[:, n:n + 1], dst[:, n, :], ALU.mult, ALU.add)
                        n += 1
                        if j < per - 1:
                            step(ins)
                    drain(ins)

            def ff_dve(tag, dst, gate):
                for i in range(11):
                    o = take(f"{tag}_b{i}")
                    v.wait_ge(*emptied(f"{tag}_a{i}"))
                    hb = flat(hid[:, 2 * i:2 * i + 2, :])
                    drain(TT(hb, hb, o, ALU.mult))
                    yield
                for i in range(8):
                    drain(STT(dst[:, i, :], take(f"{tag}_y{i}")[:, 0:L], gate[:, i:i + 1], dst[:, i, :],
                              ALU.mult, ALU.add))
                    yield

            step(nc.vector.memset(ones[:], 1.0), sem("ones"))
            v.wait_ge(sem("params"), 48)
            step(STT(lg_z, param("decay"), -1.0, param("decay"), ALU.mult, ALU.max), sem("lg_abs"))
            step(nc.vector.memset(padded[:, :, 0:2], 0.0))
            step(TS(flat(fill), const("causal"), 1.0, -FILL, ALU.subtract, ALU.mult))
            v.wait_ge(*emptied("ada3"))
            step(TT(mod1[:, 0:16], mod1[:, 0:16], param("b_ada")[:, 0:16], ALU.add))
            modulated("n1", x_t, h_t, param("norm1_w"), mod1[:, 8:16], mod1[:, 0:8])
            v.wait_ge(sem("lg_exp"), 1)
            step(TS(lg_z, lg_e, 2.0, None, ALU.add))
            step(nc.vector.reciprocal(lg_z, lg_z))
            step(TT(lg_z, lg_z, lg_e, ALU.mult))
            step(TT(lg_z2, lg_z, lg_z, ALU.mult))
            step(TS(lg_s, lg_z2, 1.0 / 17, None, ALU.mult))
            for odd in (15, 13, 11, 9, 7, 5, 3):
                step(STT(lg_s, lg_s, 1.0 / odd, lg_z2, ALU.add, ALU.mult))
            step(STT(lg_s, lg_s, 1.0, lg_z, ALU.add, ALU.mult))
            step(TS(lg_e, param("decay"), 0.0, None, ALU.min))
            step(STT(lg, lg_s, -2.0, lg_e, ALU.mult, ALU.add), sem("lg"))
            v.wait_ge(*emptied("iw"))
            for t in range(NT):
                n = (t + 1) * P
                if t == 0:
                    step(nc.vector.memset(idx[:, 0, P:L], 0.0))
                for h in range(8):
                    v.wait_ge(*emptied(f"is{t}_{h}"))
                    if h == 0:
                        ins = TS(idx[:, t, 0:n], relu[:, (8 * t + h) % 4, 0:n], iw[:, t, 0:1], None, ALU.mult)
                    else:
                        ins = STT(idx[:, t, 0:n], relu[:, (8 * t + h) % 4, 0:n], iw[:, t, h:h + 1], idx[:, t, 0:n],
                                  ALU.mult, ALU.add)
                    step(ins, sem("relu_used"))
            causal = const("causal")
            step(STT(flat(idx), flat(idx), IDX_SCALE, causal, ALU.mult, ALU.mult))
            step(TT(flat(idx), flat(idx), flat(fill), ALU.add))
            for t in range(NT):
                n = (t + 1) * P
                for _ in range(TOPK // 8):
                    step(nc.vector.max(max8, idx[:, t, 0:n]))
                    step(nc.vector.match_replace(idx[:, t, 0:n], max8, idx[:, t, 0:n], TAKEN))
            step(STT(flat(bias), flat(idx), TAKEN, causal, ALU.is_equal, ALU.mult))
            step(TS(flat(bias), flat(bias), 1.0, -MASKED, ALU.subtract, ALU.mult))
            for a, tag, dst in ((0, "q", q_t), (1, "k", k_t)):
                for i in range(2):
                    rs = flat(raw_sq[:, a, 2 * i:2 * i + 2, :])
                    root(f"{tag}ss{i}", rs, BANK, HD)
                    step(STT(flat(dst[:, 2 * i:2 * i + 2, :]), flat(raw[:, a, 2 * i:2 * i + 2, :]),
                             param(f"{tag}_norm_w")[:, 0:1], rs, ALU.mult, ALU.mult), sem("qk_ready"))
            for i in range(2):
                o = take(f"cx{i}").rearrange("p (j t) -> p j t", j=2)
                v.wait_ge(*emptied(f"cc{i}"))
                drain(TT(padded[:, 2 * i:2 * i + 2, 2:2 + L], gate_c[:, 2 * i:2 * i + 2, :], o, ALU.mult))
            cw, cb = param("conv_w"), param("conv_b")
            for j in range(KA):
                step(TS(y_conv[:, j, :], padded[:, j, 0:L], cw[:, j:j + 1], cb[:, j:j + 1], ALU.mult, ALU.add))
                for i in (1, 2):
                    step(STT(y_conv[:, j, :], padded[:, j, i:i + L], cw[:, 4 * i + j:4 * i + j + 1], y_conv[:, j, :],
                             ALU.mult, ALU.add))
            for i in range(2):
                o = take(f"cb{i}")
                yc = flat(y_conv[:, 2 * i:2 * i + 2, :])
                drain(TT(yc, yc, o, ALU.mult))
            v.wait_ge(*emptied("ada11"))
            step(TT(mod1[:, 16:48], mod1[:, 16:48], param("b_ada")[:, 16:48], ALU.add), sem("y_conv"))
            root("ss_conv", rstd[:], L, ATT)
            mix(y_conv, y_mix, KA, param("conv_out_norm_w"))
            step(nc.vector.memset(stat[:, 0:1], 0.0), sem("conv_mixed"))
            for t in range(NT):
                n = (t + 1) * P
                pr = probs[:, :, 0:n]
                if t:
                    v.wait_ge(*emptied("pt0_1"))
                for h in range(HEADS):
                    drain(TT(probs[:, h, 0:n], take(f"at{t}_{h}")[:, 0:n], bias[:, t, 0:n], ALU.add))
                step(nc.vector.tensor_reduce(mxs, pr, AX_X, ALU.max))
                step(TT(pr, pr, mxs.unsqueeze(2).to_broadcast([P, HEADS, n]), ALU.subtract), sem("shifted"))
                v.wait_ge(sem("exped"), t + 1)
                step(nc.vector.tensor_reduce(mxs, pr, AX_X, ALU.add))
                step(nc.vector.reciprocal(mxs, mxs))
                step(TT(pr, pr, mxs.unsqueeze(2).to_broadcast([P, HEADS, n]), ALU.mult), sem("probs"))
            root("ss_att", rstd[:], L, ATT)
            mix(y_att, y_mix, 0, param("attn_out_norm_w"))
            residual([f"wo{i}" for i in range(4)], x_t, mod1[:, 16:24], 2)
            modulated("n2", x_t, h_t, param("norm2_w"), mod1[:, 32:40], mod1[:, 24:32])

            def top16(values, out_v, out_i):
                step(nc.vector.max(out_v[:, 0:8], values))
                step(nc.vector.max_index(out_i[:, 0:8], out_v[:, 0:8], values))
                step(nc.vector.match_replace(values, out_v[:, 0:8], values, FILL))
                step(nc.vector.max(out_v[:, 8:16], values))
                step(nc.vector.max_index(out_i[:, 8:16], out_v[:, 8:16], values))

            def choose_experts(t):
                fv = found[:].rearrange("p (h n) -> p h n", h=2 * PH)
                for hp in range(2 * PH):
                    v.wait_ge(*emptied(f"ks{t}_{hp // 4}"))
                    top16(key_s[:, t, hp, :], top_v[:, hp, :], fv[:, hp, :])
                    yield
                step(nc.vector.tensor_copy(flat(top_i), found[:]))
                tv = top_v.rearrange("p (h a) n -> p h a n", a=2)
                ti = top_i.rearrange("p (h a) n -> p h a n", a=2)
                wide = [P, PH, PSEL, PSEL]
                step(TT(combo.rearrange("p h (i j) -> p h i j", i=PSEL),
                        tv[:, :, 0, :].unsqueeze(3).to_broadcast(wide), tv[:, :, 1, :].unsqueeze(2).to_broadcast(wide),
                        ALU.add))
                yield
                pl = place[:].rearrange("p (h n) -> p h n", h=PH)
                for h in range(PH):
                    top16(combo[:, h, :], best[:, t, h, :], pl[:, h, :])
                    yield
                hi = half_i.rearrange("p (a n) -> p a n", a=2)
                hid_ = half_id.rearrange("p (a n) -> p a n", a=2)
                spare = found[:, 0:SLOTS]
                step(TS(spare, place[:], 4, None, ALU.logical_shift_right))
                step(nc.vector.tensor_copy(hi[:, 0, :], spare))
                step(TS(spare, place[:], 15, None, ALU.bitwise_and))
                step(nc.vector.tensor_copy(hi[:, 1, :], spare))
                hot = pick.rearrange("p k t -> p (k t)").rearrange("p (s n) -> p s n", n=PSEL)
                hot4 = pick.rearrange("p k t -> p (k t)").rearrange("p (h s n) -> p h s n", h=PH, s=PSEL)
                for a in range(2):
                    step(TT(hot, hi[:, a, :].unsqueeze(2).to_broadcast([P, SLOTS, PSEL]),
                            const("iota16").unsqueeze(1).to_broadcast([P, SLOTS, PSEL]), ALU.is_equal))
                    step(TT(hot4, hot4, ti[:, :, a, :].unsqueeze(2).to_broadcast(wide), ALU.mult))
                    step(nc.vector.tensor_reduce(hid_[:, a, :], hot, AX_X, ALU.add))
                    yield
                step(STT(id_f, hid_[:, 0, :], float(PK), hid_[:, 1, :], ALU.mult, ALU.add))
                step(nc.vector.tensor_copy(ids[:, t * SLOTS:(t + 1) * SLOTS], id_f), sem("ids"))
                bt = best[:, t]
                step(nc.vector.tensor_copy(hsum[:, 0:8], bt[:, :, 0]))
                step(TT(bt, bt, hsum[:, 0:8].unsqueeze(2).to_broadcast([P, PH, PSEL]), ALU.subtract), sem("best"))
                yield

            def gates(t):
                v.wait_ge(sem("best_exp"), t + 1)
                step(nc.vector.tensor_reduce(hsum[:, 0:8], best[:, t], AX_X, ALU.add))
                step(nc.vector.reciprocal(hsum[:, 0:8], hsum[:, 0:8]))
                step(TT(best[:, t], best[:, t], hsum[:, 0:8].unsqueeze(2).to_broadcast([P, PH, PSEL]), ALU.mult))

            def background():
                yield from choose_experts(1)
                v.wait_ge(*emptied("ada2_17"))
                b2 = param("b_ada_2").unsqueeze(2).to_broadcast([P, 72, 2])
                m2 = mod2[:].rearrange("p (j s) -> p j s", s=2)
                step(TT(m2, m2, b2, ALU.add))
                for key, row, s in (("ctx1", 2, 1), ("x1", 2, 0), ("x3", 8, 0)):
                    step(TS(half_gate[key], mod2_v[:, row, :, s], 0.5, None, ALU.mult))
                v.wait_ge(sem("ctx_landed"), 16)
                modulated("ctx1", ctx_t, h_t, param("norm_ffn1_2"), mod2_v[:, 1, :, 1], mod2_v[:, 0, :, 1])
                yield
                yield from ff_dve("fc", ctx_t, half_gate["ctx1"])
                modulated("ctx2", ctx_t, h_t, param("norm_mix_2"), mod2_v[:, 4, :, 1], mod2_v[:, 3, :, 1])
                yield

            for _ in choose_experts(0):
                pass
            v.wait_ge(*emptied("ks1_3"))
            v.sem_inc(sem("row_free"), GBUF)
            bg = background()
            per_tile = SLOTS // BATCH

            def dot_batch(n):
                for s in range(BATCH):
                    g = n * BATCH + s
                    v.wait_ge(row_landed[g % GBUF], 16 * (g // GBUF + 1))
                    u = rows[g % GBUF][:, 0:D]
                    step(nc.vector.tensor_tensor_reduce(u, u, h2[:, n // per_tile, :], 1.0, 0.0, ALU.mult, ALU.add,
                                                        dots[:, n % 8, s:s + 1]), sem("dots"))

            def sum_batch(n):
                t, b = divmod(n, per_tile)
                v.wait_ge(sem("gelus"), n + 1)
                gate = flat(best[:, t])[:, b * BATCH:(b + 1) * BATCH]
                step(TT(weights[:, n % 8, :], acts[:, n % 8, :], gate, ALU.mult))
                for s in range(BATCH):
                    g = n * BATCH + s
                    STT(y_of[t], rows[g % GBUF][:, D:2 * D], weights[:, n % 8, s:s + 1], y_of[t],
                        ALU.mult, ALU.add).then_inc(sem("row_free"), 1)
                    v.wait_ge(sem("row_free"), GBUF + g + 1)

            for t in range(NT):
                gates(t)
                step(nc.vector.memset(y_of[t], 0.0))
                dot_batch(t * per_tile)
                for b in range(per_tile):
                    n = t * per_tile + b
                    if b + 1 < per_tile:
                        dot_batch(n + 1)
                    sum_batch(n)
                    if b % 2 == 1:
                        next(bg, None)
                step(nc.vector.memset(stat[:, 0:1], 0.0), sem("experts"))
            for _ in bg:
                pass
            for t in range(NT):
                for i in range(2):
                    o = take(f"yt{t}_{i}")
                    for j in range(4):
                        k = 4 * i + j
                        xs = x_t[:, k, t * P:(t + 1) * P]
                        ins = STT(xs, o[:, j * P:(j + 1) * P], mod1[:, 40 + k:41 + k], xs, ALU.mult, ALU.add)
                        if j < 3:
                            step(ins)
                    drain(ins)
            step(nc.vector.memset(stat[:, 0:1], 0.0), sem("experts_added"))
            v.wait_ge(*emptied("kc3"))
            v.wait_ge(*emptied("vc7"))
            v.wait_ge(sem("fade"), 1)
            for h in range(RH):
                for a in range(2):
                    n = 2 * h + a
                    if n >= 4:
                        v.wait_ge(*emptied(f"st{(n - 4) // 2}_{(n - 4) % 2}_1"))
                    for t in range(NT):
                        c = (a * NT + t) * RH + h
                        step(TS(k_fade[n % 4][:, t, :], kc[:, t, h * DK:(h + 1) * DK], fade[:, c:c + 1], None, ALU.mult),
                             sem("k_fade") if t == NT - 1 else chain)
            v.wait_ge(*emptied(f"st{RH - 1}_1_1"))
            split_until(PIECES - 1)
            split_modulated("x1", 0, param("norm_ffn1_2"), mod2_v[:, 1, :, 0], mod2_v[:, 0, :, 0])
            v.wait_ge(sem("late"), 64)
            split_ff_dve("f1", 0, half_gate["x1"])
            split_modulated("x2", 1, param("norm_mix_2"), mod2_v[:, 4, :, 0], mod2_v[:, 3, :, 0])
            ahead("f3")
            for i in range(4):
                o = take(f"mx{i}")
                v.wait_ge(sem("mixed_hi"), i + 1)
                drain(TT(flat(mixed_lo[:, 2 * i:2 * i + 2, :]), o, flat(mixed_hi[:, 2 * i:2 * i + 2, :]).bitcast(F32),
                         ALU.subtract))
            v.wait_ge(*emptied("gf3"))
            for i in range(4):
                drain(TT(flat(m_t[:, 2 * i:2 * i + 2, :]), flat(sig[:, 2 * i:2 * i + 2, :]), take(f"pf{i}"), ALU.mult))
            cos = rope[:, 0, :].unsqueeze(1).to_broadcast([P, 2, L])
            sin = rope[:, 1, :].unsqueeze(1).to_broadcast([P, 2, L])
            for tag, dst, scale in (("rq", rq_t, DK ** -0.5), ("rk", rk_t, 1.0)):
                for h in range(RH):
                    o = take(f"{tag}{h}").rearrange("p (b t) -> p b t", b=2)
                    d = dst[:, 2 * h:2 * h + 2, :]
                    step(STT(d, o, scale, cos, ALU.mult, ALU.mult))
                    drain(STT(rope_tmp, o, scale, sin, ALU.mult, ALU.mult))
                    step(TT(d[:, 0, :], d[:, 0, :], rope_tmp[:, 1, :], ALU.subtract))
                    step(TT(d[:, 1, :], d[:, 1, :], rope_tmp[:, 0, :], ALU.add))
            ahead("rg7")
            v.wait_ge(*emptied("rv7"))
            v.wait_ge(*emptied("rg7"))
            def split_gated(h):
                v.wait_ge(sem("rg_hi"), h + 1)
                blocks = slice(4 * h, 4 * h + 4)
                rest(rg_lo[:, blocks, :].rearrange("p (a j) t -> p a (j t)", a=2),
                     rg_t[:, blocks, :].rearrange("p (a j) t -> p a (j t)", a=2),
                     rg_hi[:, :, h].rearrange("p a j t -> p a (j t)"), "rg_split")

            for h in range(RH):
                v.wait_ge(sem("xi"), h + 1)
                for a in range(2):
                    step(TT(q_faded[:, a], rq_t[:, 2 * h:2 * h + 2, :], xi[:, a, :].unsqueeze(1).to_broadcast([P, 2, L]),
                            ALU.mult), sem("q_faded") if a else chain)
                drain(TT(flat(sc_t), take(f"sc{h}"), flat(decay_t[:, h]), ALU.mult))
                for t in range(NT):
                    o = take(f"o{h}_{t}")
                    step(nc.vector.bn_stats(stat[:, 0:6], o))
                    step(nc.vector.bn_aggr(stat[:, 6:8], stat[:, 0:6]))
                    step(TS(stat[:, 8:9], stat[:, 7:8], EPS, None, ALU.add))
                    rooted(stat[:, 8:9])
                    if t:
                        v.wait_ge(group_done, index[f"ot{h}_0"] + 1)
                    drain(TS(o_n, o, stat[:, 6:7], stat[:, 8:9], ALU.subtract, ALU.mult))
                if h:
                    split_gated(h - 1)
                for t in range(NT):
                    o = take(f"ot{h}_{t}")
                    for j in range(4):
                        k = 4 * h + j
                        g = rg_t[:, k, t * P:(t + 1) * P]
                        ins = STT(g, o[:, j * P:(j + 1) * P], param("ret_gn_w_2")[:, k:k + 1], g, ALU.mult, ALU.mult)
                        if j < 3:
                            step(ins)
                    drain(ins)
                step(nc.vector.memset(stat[:, 9:10], 0.0), sem("turned"))
            split_gated(RH - 1)
            v.wait_ge(*emptied("ga3"))

            def split_merged(i):
                v.wait_ge(sem("m_hi"), i + 1)
                two = slice(2 * i, 2 * i + 2)
                rest(flat(m_lo[:, two, :]), flat(m_t[:, two, :]), flat(mixed_hi[:, two, :]), "m_split")

            for i in range(4):
                s = flat(sig[:, 2 * i:2 * i + 2, :])
                m = flat(m_t[:, 2 * i:2 * i + 2, :])
                drain(TT(s, s, take(f"pr{i}"), ALU.mult))
                step(TT(m, m, s, ALU.add), sem("merged"))
                if i:
                    split_merged(i - 1)
            split_merged(3)
            residual([f"w2o{i}" for i in range(4)], x_t, mod2_v[:, 5, :, 0], 2)
            split_modulated("x3", 2, param("norm_ffn2_2"), mod2_v[:, 7, :, 0], mod2_v[:, 6, :, 0])
            split_ff_dve("f2", 1, half_gate["x3"])
            root("ss_fin", rstd[:], L, D)
            for k in range(KD):
                step(STT(h_t[:, k, :], x_t[:, k, :], param("norm_final_2")[:, k:k + 1], rstd[:], ALU.mult, ALU.mult),
                     sem("out_ready") if k == KD - 1 else chain)
            assert taken[0] == sum(g[1] == "dve" for g in groups)




def _tiles(w, width):
    k, n = w.shape
    return np.ascontiguousarray(w.reshape(k // P, P, n // width, width).transpose(2, 1, 0, 3)).reshape(
        n // width, P, k // P * width)


def _columns(vec):
    return np.asarray(vec).reshape(-1, P).T


def _feature_major(x):
    return np.ascontiguousarray(np.asarray(x).reshape(L, KD, P).transpose(2, 1, 0)).reshape(P, KD * L)


def _ffn_pairs(w13):
    w = np.asarray(w13)[0]
    w = w.reshape(D, 2, FF // 256, 256).transpose(0, 2, 1, 3).reshape(D, 2 * FF)
    return _tiles(w, 512)


def _pairs_apart(w):
    return w.reshape(D, RH, DK // 2, 2).transpose(0, 1, 3, 2).reshape(D, RH * DK)


def kernel(**inputs):
    import concourse.bacc as bacc
    from concourse.bass_utils import run_bass_kernel_spmd

    a = {k: np.asarray(v) for k, v in inputs.items()}
    early, late = shape_constants()
    w_in = a["w_in"]
    w_in_2 = a["w_in_2"][0]
    order = [3072, 0, 512, 1024, 2048, 2560, 1536]
    ik, iw = w_in[:, 3584:3648], w_in[:, 3648:3656]
    parts = {
        "c": _columns(a["c"]),
        "c2": np.stack([_columns(a["c_2"]), _columns(a["c_ctx_2"])], 2).reshape(P, 16),
        "b_ada": _columns(a["b_ada"]), "b_ada_2": _columns(a["b_ada_2"]),
        "q_norm_w": np.tile(a["q_norm_w"], 2)[:, None], "k_norm_w": np.tile(a["k_norm_w"], 2)[:, None],
        "conv_w": a["conv_w"].reshape(3, KA, P).transpose(2, 0, 1).reshape(P, 12),
        "decay": np.broadcast_to(np.concatenate([a["decay_fwd_2"][0], a["decay_bwd_2"][0]]), (P, 8)),
    }
    params = np.concatenate([parts[n] if n in parts else _columns(a[n]) for n, _ in PARAMS], 1)
    arrays = {
        "params": params, "early": early, "late": late,
        "x": _feature_major(a["x"][0]), "ctx": _feature_major(a["ctx_2"][0]),
        "w_ada": _tiles(a["w_ada"], 512),
        "w_idx": _tiles(np.concatenate([ik, ik, iw], 1), 136),
        "w_in": np.concatenate([_tiles(w_in[:, o:o + 512], 512) for o in order]),
        "w_out": _tiles(a["w_out"], 512), "peer_wq": _tiles(a["peer_wq"], 512),
        "subkeys": a["peer_subkeys"].reshape(2 * PH, PK, P).transpose(2, 0, 1).reshape(1, P, 2 * PH * PK),
        "experts": np.concatenate([a["peer_u"], a["peer_v"]], 1),
        "w_ada_2": _tiles(a["w_ada_2"][0], 512),
        "w13_ffn1": _ffn_pairs(a["w13_ffn1_2"]), "w2_ffn1": _tiles(a["w2_ffn1_2"][0], P),
        "w13_ffn2": _ffn_pairs(a["w13_ffn2_2"]), "w2_ffn2": _tiles(a["w2_ffn2_2"][0], P),
        "w_in_2": _tiles(np.concatenate([_pairs_apart(w_in_2[:, 0:1024]), _pairs_apart(w_in_2[:, 1024:2048]),
                                         w_in_2[:, 2048:]], 1), 512),
        "p_ret": _tiles(a["p_ret_2"][0], 256), "p_four": _tiles(a["p_four_2"][0], 512),
        "w_out_2": _tiles(a["w_out_2"][0], 512),
    }
    nc = bacc.Bacc("TRN2", target_bir_lowering=False, num_devices=1)
    feeds, dram = {}, {}
    for name, array in arrays.items():
        feeds["in_" + name] = np.ascontiguousarray(array)
        dram[name] = nc.dram_tensor("in_" + name, array.shape, F32, kind="ExternalInput").ap()
    out = nc.dram_tensor("out_x", (P, KD * L), F32, kind="ExternalOutput").ap()
    program(nc, dram, out)
    got = run_bass_kernel_spmd(nc, [feeds], core_ids=[0]).results[0]["out_x"]
    return np.ascontiguousarray(np.asarray(got).reshape(P, KD, L).transpose(2, 1, 0)).reshape(1, L, D)
```

```python
from contextlib import ExitStack

import numpy as np

import concourse.bass as bass
from concourse import mybir

ALU = mybir.AluOpType
ACT = mybir.ActivationFunctionType
F32 = mybir.dt.float32
F32R = mybir.dt.float32r
U32 = mybir.dt.uint32
AX_X = mybir.AxisListType.X

P = 128
D = 1024
KD = D // P
L = 256
NT = L // P
EPS = 1e-6
BANKS = 8
BANK = 512

HEADS, HD = 8, 64
ATT = HEADS * HD
KA = ATT // P
TOPK = L // 4
PH, PK, PSEL = 8, 128, 16
SLOTS = PH * PSEL
ATT_SCALE = HD ** -0.5
IDX_SCALE = (64 ** -0.5) * (8 ** -0.5)
FILL, TAKEN = -3.0e38, -3.2e38
MASKED = -1.0e30

RH, DK, DV = 4, 256, 512
FF = 2816
KF = FF // P
FG = 4
MOD_CTX = 10
MOD_LATE = 8
LATE_LOAD = (0, 1, 1, 2, 4, 6, 8, 10)
LATE_TURN = (0, 1, 3, 4, 7, 9, 11, 13)
RING = 4
SLAB = 4096
SPLIT_RING = 3
PIECES = 4
PIECE = SLAB // PIECES
GBUF = 8
ROW = 2 * D
BATCH = 2
CHOICE_STEPS = 5 * (PH // 2) + 1
ROUND = 16

PARAMS = [("c", 8), ("c2", 16), ("b_ada", 48), ("b_ada_2", 72), ("norm1_w", 8), ("norm2_w", 8), ("q_norm_w", 1),
          ("k_norm_w", 1), ("conv_w", 12), ("conv_b", 4), ("attn_out_norm_w", 4), ("conv_out_norm_w", 4),
          ("norm_ffn1_2", 8), ("norm_mix_2", 8), ("ret_gn_w_2", 16), ("norm_ffn2_2", 8), ("norm_final_2", 8),
          ("decay", 8)]
EARLY = [("ident", P), ("pair", P), ("causal", NT * L), ("iota16", PSEL), ("age", 2 * NT)]
LATE_DECAY = 2 * NT * L * 2
LATE_DFT = 2 * 2 * 256
LATE_ROPE = 2 * L
LATE_XI = 2 * L


def offsets(table):
    at, out = 0, {}
    for name, width in table:
        out[name] = (at, width)
        at += width
    return out, at


PARAM_AT, PARAM_W = offsets(PARAMS)
EARLY_AT, EARLY_W = offsets(EARLY)


def shape_constants():
    tok = np.arange(L)
    causal = (tok[None, :] <= tok[:, None]).astype(np.float32).reshape(NT, P, L).transpose(1, 0, 2)
    pair = (np.arange(P)[:, None] // HD == np.arange(P)[None, :] // HD).astype(np.float32)
    age = np.stack([L - 1 - tok.reshape(NT, P), tok.reshape(NT, P)]).transpose(2, 0, 1).astype(np.float32)
    iota16 = np.broadcast_to(np.arange(PSEL, dtype=np.float32), (P, PSEL))
    early = np.concatenate([np.eye(P, dtype=np.float32), pair, causal.reshape(P, -1), iota16, age.reshape(P, -1)], 1)
    diff = (tok[None, :] - tok[:, None]).astype(np.float32)
    decay = np.stack([np.maximum(diff, 0), np.maximum(-diff, 0), diff >= 0, diff <= 0]).astype(np.float32)
    decay = decay.reshape(4, NT, P, L).transpose(2, 0, 1, 3).reshape(P, -1)
    ang = 2 * np.pi * (np.outer(np.arange(256), np.arange(256)) % 256) / 256
    dft = (np.concatenate([np.cos(ang), np.sin(ang)], 1) / 16).astype(np.float32)
    dft = dft.reshape(2, P, 512).transpose(1, 0, 2).reshape(P, -1)
    inv = (np.float32(10000.0) ** (-np.arange(64, dtype=np.float32) / 64)).astype(np.float32)
    row, col = (tok // 64).astype(np.float32), (tok % 64).astype(np.float32)
    turn = np.concatenate([inv[:, None] * row[None, :], inv[:, None] * col[None, :]], 0).astype(np.float32)
    rope = np.concatenate([np.cos(turn), np.sin(turn)], 1).astype(np.float32)
    xi = np.broadcast_to(np.concatenate([tok + 1, L - tok]).astype(np.float32), (P, 2 * L))
    late = np.concatenate([decay, dft, rope, xi], 1)
    return np.ascontiguousarray(early), np.ascontiguousarray(late)


def slab_order():
    ada = [("w_ada", i, SLAB) for i in range(12)]
    ffn = lambda n: [(f"w13_ffn{n}", i, SLAB) for i in range(11)] + [(f"w2_ffn{n}", i, KF * P) for i in range(8)]
    w_in_2 = {"q": (0, 2), "k": (2, 4), "v": (4, 8), "g": (8, 12), "f": (12, 14), "ga": (14, 16), "gf": (16, 18)}
    proj = lambda n: [("w_in_2", i, SLAB) for i in range(*w_in_2[n])]
    w_in = lambda i: [("w_in", i, SLAB)]
    out_proj = [("w_out", i, SLAB) for i in range(2)]
    first = (ada[:4] + w_in(0) + [("w_idx", 0, KD * 136)] + w_in(1) + w_in(2) + w_in(4) + w_in(5) + w_in(6) + w_in(3)
             + ada[4:9] + out_proj + ada[9:10] + [("peer_wq", i, SLAB) for i in range(4)] + ada[10:])
    context = [("w_ada_2", i, SLAB) for i in range(MOD_CTX)] + ffn(1) + proj("k") + proj("v")
    ffn_x = []
    for step, slab in enumerate(ffn(1)):
        ffn_x += [("w_ada_2", MOD_CTX + j, SLAB) for j in range(MOD_LATE) if LATE_LOAD[j] == step]
        ffn_x.append(slab)
    second = (ffn_x + proj("gf") + proj("f") + [("p_four", i, SLAB) for i in range(2)] + proj("ga") + proj("q")
              + proj("k") + proj("v") + proj("g") + [("p_ret", i, SLAB) for i in range(4)]
              + [("w_out_2", i, SLAB) for i in range(2)] + ffn(2))
    return first + context + second, len(first) + len(context)


def cuts(name, i):
    if name.startswith("w2_ffn"):
        return [(0, 8, 0, P), (8, 16, 0, P), (16, KF, 0, P)]
    if name == "p_ret":
        return [(8 * b, 8 * b + 8, c * P, (c + 1) * P) for c in range(2) for b in range(2)]
    if (name, i) == ("w_in", 3) or (name == "w_in_2" and 4 <= i < 8):
        return [(2 * q, 2 * q + 2, 0, 4 * P) for q in range(4)]
    return [(0, KD, c * P, (c + 1) * P) for c in range(4)]


def slots_of(slabs, second_at):
    plan, users = [], {}
    for n in range(len(slabs)):
        slot = n % RING if n < second_at else (n - second_at) % SPLIT_RING
        users.setdefault(slot, []).append(n)
        plan.append((slot, len(users[slot]), users[slot][-2] if len(users[slot]) > 1 else None))
    return plan, [n for n in users[SPLIT_RING] if n < second_at][-1]


def program(nc, dram, out):
    slabs, second_at = slab_order()
    slots, last_in_split = slots_of(slabs, second_at)
    late_mod = [n for n in range(second_at, len(slabs)) if slabs[n][0] == "w_ada_2"]
    split = [n for n in range(len(slabs)) if (n >= second_at and n not in late_mod) or slabs[n][0] in ("w_in", "w_out", "peer_wq")]
    pieces = [(n,) + cut for n in split for cut in cuts(*slabs[n][:2])]
    first_out = sum(slabs[p[0]][0] == "w_in" for p in pieces)
    first_pieces = sum(p[0] < second_at for p in pieces)
    with ExitStack() as ctx:
        def sb(name, width, dt=F32):
            return ctx.enter_context(nc.sbuf_tensor(name, [P, width], dt))

        def twin(name, width):
            plain = sb(name, width)
            return plain, nc.alloc_sbuf_tensor_at(name + "_r", [P, width], F32R, offset=nc.sbuf_base - 4 * width)

        sems = {}

        def sem(name):
            if name not in sems:
                sems[name] = ctx.enter_context(nc.semaphore(name))
            return sems[name]

        psum = ctx.enter_context(nc.psum_tensor("psum", [P, BANKS, BANK], F32))
        ring, ring_r = twin("ring", RING * SLAB)
        x_t = sb("x_t", KD * L)[:].rearrange("p (k t) -> p k t", k=KD)
        h_words, h_words_r = twin("h_t", KD * L)
        h_t, h_lo = (t[:].rearrange("p (k t) -> p k t", k=KD) for t in (h_words, h_words_r))
        prm = sb("prm", PARAM_W)
        early = sb("early", EARLY_W)
        ones = sb("ones", P)
        mod1 = sb("mod1", 48)
        mod2 = sb("mod2", 144)
        mod2_v = mod2[:].rearrange("p (m k s) -> p m k s", m=9, s=2)
        cols = sb("cols", 160)
        rstd = sb("rstd", L)
        arena, arena_r = twin("arena", 27648)
        upper_1 = nc.alloc_sbuf_tensor_at("upper_1", [P, PIECES * PIECE], F32R, offset=nc.sbuf_base - 4 * 27648)
        small, small_r = twin("small", 2600)
        ids = sb("ids", NT * SLOTS, U32)
        idx_stage = sb("idx_stage", ROUND, U32)
        found = sb("found", 2 * PH * PSEL, U32)
        place = sb("place", SLOTS, U32)
        spare = sb("spare", 2 * PSEL, U32)

        def param(name):
            at, w = PARAM_AT[name]
            return prm[:, at:at + w]

        def const(name):
            at, w = EARLY_AT[name]
            return early[:, at:at + w]

        ident = const("ident")

        silu_c, silu_c2 = cols[:, 0:8], cols[:, 8:24]
        scale_of = {}
        for i, key in enumerate(("n1", "n2", "ctx1", "ctx2", "x1", "x2", "x3")):
            scale_of[key] = cols[:, 24 + 8 * i:32 + 8 * i]
        half_gate = {"ctx1": cols[:, 80:88], "x1": cols[:, 88:96], "x3": cols[:, 96:104]}
        lg = cols[:, 104:112]
        lg_e, lg_z, lg_z2, lg_s = (cols[:, 112 + 8 * i:120 + 8 * i] for i in range(4))
        fade = cols[:, 144:160]

        ctx_t = arena[:, 0:2048].rearrange("p (k t) -> p k t", k=KD)
        h2 = arena[:, 2048:4096].rearrange("p (t d) -> p t d", t=NT)
        y_acc = arena[:, 4096:5120]
        y_of = [y_acc, h2[:, 0, :]]
        F0, G0 = 5120, 11264
        iq_t = arena[:, G0:G0 + 1024].rearrange("p (j t) -> p j t", j=4)
        ik_t = arena[:, G0 + 1024:G0 + 1280]
        idx = arena[:, G0 + 1280:G0 + 1792].rearrange("p (t s) -> p t s", t=NT)
        fill = arena[:, G0 + 1792:G0 + 2304].rearrange("p (t s) -> p t s", t=NT)
        bias = arena[:, G0 + 2304:G0 + 2816].rearrange("p (t s) -> p t s", t=NT)
        relu = arena[:, G0 + 2816:G0 + 3840].rearrange("p (b s) -> p b s", b=4)
        q_t = arena[:, G0 + 3840:G0 + 4864].rearrange("p (j t) -> p j t", j=KA)
        k_t = arena[:, G0 + 4864:G0 + 5888].rearrange("p (j t) -> p j t", j=KA)
        raw = arena[:, G0 + 5888:G0 + 7936].rearrange("p (a j t) -> p a j t", a=2, j=KA)
        raw_sq = arena[:, G0 + 7936:G0 + 9984].rearrange("p (a j t) -> p a j t", a=2, j=KA)
        y_mix = arena[:, G0 + 5888:G0 + 7936].rearrange("p (k t) -> p k t", k=KD)
        v_n = arena[:, G0 + 9984:G0 + 11008].rearrange("p (t d) -> p t d", t=NT)
        padded = arena[:, G0 + 11008:G0 + 12040].rearrange("p (j t) -> p j t", j=KA)
        y_conv = arena[:, G0 + 12040:G0 + 13064].rearrange("p (j t) -> p j t", j=KA)
        sq1 = arena[:, G0 + 13064:G0 + 15112].rearrange("p (k t) -> p k t", k=KD)
        gate_c = arena[:, 4096:5120].rearrange("p (j t) -> p j t", j=KA)
        p_t0 = arena[:, F0:F0 + 1024].rearrange("p (h q) -> p h q", h=HEADS)
        p_t1 = arena[:, F0 + 1024:F0 + 3072].rearrange("p (h s q) -> p h s q", h=HEADS, s=2)
        probs = [arena[:, G0 + 7936:G0 + 8960].rearrange("p (h s) -> p h s", h=HEADS),
                 arena[:, F0 + 3072:F0 + 5120].rearrange("p (h s) -> p h s", h=HEADS)]
        subkeys = arena[:, G0 + 9984:G0 + 12032].rearrange("p (h n) -> p h n", h=2 * PH)
        mod_row = small[0:1, 1536:2560].rearrange("p (a n) -> p a n", a=2)
        y_att = arena[:, F0 + 5120:F0 + 6144].rearrange("p (j t) -> p j t", j=KA)
        pq_t = arena[:, G0:G0 + 4096].rearrange("p (h t) -> p h t", h=2 * PH)
        key_s = arena[:, F0:F0 + 4096].rearrange("p (t h n) -> p t h n", t=NT, h=2 * PH)
        combo = arena[:, F0 + 4096:F0 + 6144].rearrange("p (h n) -> p h n", h=PH)
        pick = [y_acc[:, 0:2 * PSEL * PSEL], h_words[:, 0:2 * PSEL * PSEL]]
        rows = [arena[:, G0 + i * ROW:G0 + (i + 1) * ROW] for i in range(GBUF)]
        top_v = small[:, 0:256].rearrange("p (h n) -> p h n", h=2 * PH)
        top_i = small[:, 256:512].rearrange("p (h n) -> p h n", h=2 * PH)
        best = small[:, 512:768].rearrange("p (t h n) -> p t h n", t=NT, h=PH)
        half_i = small[:, 768:1024]
        half_id = small[:, 1024:1280]
        id_f = small[:, 1280:1408]
        hsum = small[:, 1408:1424]
        dots = small[:, 1424:1424 + 16].rearrange("p (b n) -> p b n", b=8)
        acts = small[:, 1440:1456].rearrange("p (b n) -> p b n", b=8)
        weights = small[:, 1456:1472].rearrange("p (b n) -> p b n", b=8)
        max8 = small[:, 1472:1480]
        stat = small[:, 2568:2584]
        mxs = small[:, 1496:1504]
        iw = small[:, 1504:1520].rearrange("p (t h) -> p t h", t=NT)
        xi = small[:, 1536:2048].rearrange("p (a t) -> p a t", a=2)
        rope_tmp = small[:, 2048:2560].rearrange("p (b t) -> p b t", b=2)
        hid = arena[:, F0:F0 + KF * L].rearrange("p (k t) -> p k t", k=KF)
        kc = arena[:, F0:F0 + 2048].rearrange("p (t n) -> p t n", t=NT)
        vc = arena[:, F0 + 2048:F0 + 6144].rearrange("p (t n) -> p t n", t=NT)
        k_fade = [arena[:, G0 + 2048 + i * 512:G0 + 2560 + i * 512].rearrange("p (t n) -> p t n", t=NT) for i in range(4)]
        state = arena[:, G0 + 8192:G0 + 16384].rearrange("p (h a b v) -> p h a b v", h=RH, a=2, b=2)
        late_decay = arena[:, 2048:4096].rearrange("p (m t i) -> p m t i", m=4, t=NT)
        decay_t = arena[:, 0:2048].rearrange("p (h t i) -> p h t i", h=RH, t=NT)
        sq2 = small[:, 0:2048].rearrange("p (k t) -> p k t", k=KD)
        sig = arena[:, 2048:4096].rearrange("p (k t) -> p k t", k=KD)
        rope = arena[:, 4096:4608].rearrange("p (a t) -> p a t", a=2)
        late_xi = arena[:, 4608:5120].rearrange("p (a t) -> p a t", a=2)
        f_t = arena[:, F0:F0 + 2048].rearrange("p (k t) -> p k t", k=KD)
        m_t = arena[:, F0 + 4096:F0 + 6144].rearrange("p (k t) -> p k t", k=KD)
        dft_z = arena[:, G0:G0 + 4096].rearrange("p (t g a c) -> p t g a c", t=NT, g=FG, a=2)
        decay_tmp = arena[:, G0 + 5632:G0 + 6656].rearrange("p (a i) -> p a i", a=2)
        dft = arena[:, G0 + 6656:G0 + 7680].rearrange("p (k a c) -> p k a c", k=2, a=2)
        rq_t = arena[:, G0:G0 + 2048].rearrange("p (k t) -> p k t", k=KD)
        rk_t = arena[:, G0 + 2048:G0 + 4096].rearrange("p (k t) -> p k t", k=KD)
        rv = arena[:, F0:F0 + 4096].rearrange("p (t n) -> p t n", t=NT)
        rg_t = arena[:, G0 + 4096:G0 + 8192].rearrange("p (k t) -> p k t", k=16)
        pair_of = lambda ap: ap.rearrange("p (a k t) -> p a k t", a=2, k=2)
        q_faded = [pair_of(h_words[:, 0:1024]), pair_of(small[:, 512:1536])]
        sc_t = [h_words[:, 1024:1536].rearrange("p (s t) -> p s t", s=NT),
                small[:, 2048:2560].rearrange("p (s t) -> p s t", s=NT)]
        o_n = [h_words[:, 1536:2048], small[:, 0:512]]

        h_hi_1 = arena_r[:, F0:F0 + 2048].rearrange("p (k t) -> p k t", k=KD)
        h_lo_1 = arena_r[:, F0 + 2048:F0 + 4096].rearrange("p (k t) -> p k t", k=KD)
        h_hi_2 = arena_r[:, G0 + 4096:G0 + 6144].rearrange("p (k t) -> p k t", k=KD)
        h_lo_2 = arena_r[:, G0 + 6144:G0 + 8192].rearrange("p (k t) -> p k t", k=KD)
        y_mix_lo = arena_r[:, G0 + 5888:G0 + 7936].rearrange("p (k t) -> p k t", k=KD)
        h_hi = small_r[:, 0:2048].rearrange("p (k t) -> p k t", k=KD)
        hid_lo = arena_r[:, F0:F0 + KF * L].rearrange("p (k t) -> p k t", k=KF)
        hid_hi = arena_r[:, G0:G0 + KF * L].rearrange("p (k t) -> p k t", k=KF)
        mixed_lo = arena_r[:, F0 + 2048:F0 + 4096].rearrange("p (k t) -> p k t", k=KD)
        mixed_hi = arena_r[:, F0:F0 + 2048].rearrange("p (k t) -> p k t", k=KD)
        m_lo = arena_r[:, F0 + 4096:F0 + 6144].rearrange("p (k t) -> p k t", k=KD)
        rg_lo = arena_r[:, G0 + 4096:G0 + 8192].rearrange("p (k t) -> p k t", k=16)
        rg_hi = arena_r[:, G0:G0 + 4096].rearrange("p (a h j t) -> p a h j t", a=2, h=RH, j=2)

        def whole(q, ring_of):
            n, k0, k1, c0, c1 = pieces[q]
            width = 512 if cuts(*slabs[n][:2])[-1][3] == 4 * P else slabs[n][2] // cuts(*slabs[n][:2])[-1][1]
            at = slots[n][0] * SLAB
            return ring_of[:, at:at + slabs[n][2]].rearrange("p (k n) -> p k n", n=width)[:, k0:k1, c0:c1]

        def upper(q):
            n, k0, k1, c0, c1 = pieces[q]
            home, at = (upper_1, 0) if q < first_pieces else (ring_r, SPLIT_RING * SLAB)
            at += (q % PIECES) * PIECE
            return home[:, at:at + (k1 - k0) * (c1 - c0)].rearrange("p (k n) -> p k n", n=c1 - c0)

        group_done = sem("group_done")
        drained = {"act": sem("act_drained"), "dve": sem("dve_drained")}
        landed = [sem(f"slab_landed{i}") for i in range(RING)]
        row_landed = [sem(f"row_landed{i}") for i in range(GBUF)]

        groups, index, turn = [], {}, {"act": 0, "dve": 0}
        def phase_end(q):
            return next(end for end in (first_out, first_pieces, len(pieces)) if q < end)

        piece_read = []
        piece_of = {}
        hi_made, lo_made, piece_done = sem("hi_made"), sem("lo_made"), sem("piece_done")
        slab_free = {n: (sem("late_mod"), j + 1) for j, n in enumerate(late_mod)}
        late_sum = [small[:, 2048:2560], arena[:, G0 + 7680:G0 + 8192]]

        def emptied(name):
            _, who, count = groups[index[name]]
            return drained[who], count

        block = ctx.enter_context(nc.Block())

        @block.tensor
        def _(pe):
            def begin(name, who):
                i = len(groups)
                if i >= BANKS:
                    pe.wait_ge(drained[groups[i - BANKS][1]], groups[i - BANKS][2])
                count = 1 + sum(g[1] == who for g in groups)
                groups.append((name, who, count))
                index[name] = i
                return psum[:, i % BANKS, :]

            def end(ins):
                ins.then_inc(group_done, 1)

            used = [0]

            def next_slab(name, i):
                n = used[0]
                assert slabs[n][:2] == (name, i), (slabs[n], name, i)
                used[0] += 1
                pe.wait_ge(landed[slots[n][0]], 16 * slots[n][1])
                at = slots[n][0] * SLAB
                return ring[:, at:at + slabs[n][2]]

            def release():
                slab_free[used[0] - 1] = (group_done, len(groups))
                while used[0] in late_mod:
                    used[0] += 1

            def mm(o, a, b, first, last):
                return nc.tensor.matmul(o, a, b, start=first, stop=last)

            def by_token(tag, array, ids_, src, who):
                n = 0
                for i in ids_:
                    w = next_slab(array, i).rearrange("p (k n) -> p k n", k=KD)
                    for t in range(NT):
                        o = begin(f"{tag}{n}", who)
                        n += 1
                        for k in range(KD):
                            last = mm(o[:, 0:BANK], src[:, k, t * P:(t + 1) * P], w[:, k, :], k == 0, k == KD - 1)
                        end(last)
                    release()

            def squares(tag, sq, kb):
                pe.wait_ge(sem("sq_" + tag), 1)
                o = begin("ss_" + tag, "dve")
                for k in range(kb):
                    last = mm(o[:, 0:L], ones[:], sq[:, k, :], k == 0, k == kb - 1)
                end(last)

            def modulation(tag, array, ids_, src, width):
                for i in ids_:
                    w = next_slab(array, i).rearrange("p (k n) -> p k n", k=KD)
                    o = begin(f"{tag}{i}", "act")
                    for j in range(4):
                        for k in range(KD):
                            last = mm(o[:, j * width:(j + 1) * width], w[:, k, j * P:(j + 1) * P],
                                      src[:, k * width:(k + 1) * width], k == 0, k == KD - 1)
                    end(last)
                    release()

            def ada_row(i):
                w = next_slab("w_ada", i).rearrange("p (k n) -> p k n", k=KD)
                o = begin(f"ada_row{i}", "act")
                for k in range(KD):
                    last = mm(o[0:1, 0:BANK], silu_c[:, k:k + 1], w[:, k, :], k == 0, k == KD - 1)
                end(last)
                release()

            def ada_turn(i):
                pe.wait_ge(*emptied(f"ada_row{i}"))
                o = begin(f"ada{i}", "act")
                for j in range(4):
                    last = nc.tensor.transpose(o[:, j:j + 1], mod_row[:, i % 2, j * P:(j + 1) * P], ident[0:1, 0:1])
                end(last)

            def feed_forward(tag, n, src):
                for i in range(11):
                    w = next_slab(f"w13_ffn{n}", i).rearrange("p (k n) -> p k n", k=KD)
                    for half, who in ((0, "act"), (1, "dve")):
                        o = begin(f"{tag}_{'ab'[half]}{i}", who)
                        for j in range(2):
                            c = half * 256 + j * P
                            for k in range(KD):
                                last = mm(o[:, j * L:(j + 1) * L], w[:, k, c:c + P], src[:, k, :], k == 0, k == KD - 1)
                        end(last)
                    release()
                pe.wait_ge(*emptied(f"{tag}_b10"))
                for i in range(8):
                    w = next_slab(f"w2_ffn{n}", i).rearrange("p (k n) -> p k n", k=KF)
                    o = begin(f"{tag}_y{i}", "dve")
                    for k in range(KF):
                        last = mm(o[:, 0:L], w[:, k, :], hid[:, k, :], k == 0, k == KF - 1)
                    end(last)
                    release()

            def next_piece():
                q = len(piece_read)
                pe.wait_ge(lo_made, q + 1)
                return pieces[q][1:], upper(q), whole(q, ring_r)

            mid = [0]

            def piece_end(ins, name=None):
                if name:
                    end(ins)
                    piece_of[name] = len(piece_read)
                    piece_read.append((group_done, len(groups)))
                else:
                    mid[0] += 1
                    ins.then_inc(piece_done, 1)
                    piece_read.append((piece_done, mid[0]))
                n = pieces[len(piece_read) - 1][0]
                if len(piece_read) == len(pieces) or pieces[len(piece_read)][0] != n:
                    assert used[0] == n
                    used[0] += 1
                    release()

            def three(o, w_hi, w_lo, a_hi, a_lo, first, last):
                mm(o, w_hi, a_hi, first, False)
                mm(o, w_hi, a_lo, False, False)
                return mm(o, w_lo, a_hi, False, last)

            def split_feature(tag, count, hi, lo, who, kb=KD, need=None, start=0):
                need = need or {}
                for n in range(start, start + count):
                    o = begin(f"{tag}{n}", who)
                    for j in range(2):
                        for part in range(kb // KD):
                            (k0, k1, _, _), w_hi, w_lo = next_piece()
                            for k in range(k0, k1):
                                if k in need:
                                    pe.wait_ge(*need.pop(k))
                                last = three(o[:, j * L:(j + 1) * L], w_hi[:, k - k0, :], w_lo[:, k - k0, :],
                                             hi(k), lo[:, k, :], k == 0, k == kb - 1)
                            ends = j == 1 and part == kb // KD - 1
                            piece_end(last, f"{tag}{n}" if ends else None)

            def split_token(tag, count, h_hi, h_lo):
                for i in range(count):
                    o = [begin(f"{tag}{NT * i + t}", "act") for t in range(NT)]
                    for part in range(4):
                        (k0, k1, _, _), w_hi, w_lo = next_piece()
                        for t in range(NT):
                            ts = slice(t * P, (t + 1) * P)
                            for k in range(k0, k1):
                                mm(o[t], h_hi[:, k, ts], w_hi[:, k - k0, :], k == 0, False)
                                mm(o[t], h_lo[:, k, ts], w_hi[:, k - k0, :], False, False)
                                last = mm(o[t], h_hi[:, k, ts], w_lo[:, k - k0, :], False, k == KD - 1)
                            if part == 3 and t < NT - 1:
                                end(last)
                        piece_end(last, f"{tag}{NT * i + NT - 1}" if part == 3 else None)
                    piece_of[f"{tag}{NT * i}"] = piece_of[f"{tag}{NT * i + 1}"]

            def norm_need(m):
                return {k: (sem("h_split"), KD * m + k + 1) for k in range(KD)}

            def h_hi_of(k):
                return h_hi[:, k, :]

            def late_modulation(f, step):
                if f == 0 and step in LATE_TURN:
                    j = LATE_TURN.index(step)
                    pe.wait_ge(sem("late_mod"), j + 1)
                    o = begin(f"late_mod{j}", "act")
                    for b in range(4):
                        last = mm(o[:, b:b + 1], late_sum[j % 2][:, b * P:(b + 1) * P], ones[:, 0:1], True, True)
                    end(last)

            def split_feed_forward(tag, m, f):
                need = norm_need(m)
                for i in range(11):
                    late_modulation(f, i)
                    for half, who in ((0, "act"), (1, "dve")):
                        name = f"{tag}_{'ab'[half]}{i}"
                        o = begin(name, who)
                        for j in range(2):
                            _, w_hi, w_lo = next_piece()
                            for k in range(KD):
                                if k in need:
                                    pe.wait_ge(*need.pop(k))
                                last = three(o[:, j * L:(j + 1) * L], w_hi[:, k, :], w_lo[:, k, :], h_hi[:, k, :],
                                             h_lo[:, k, :], k == 0, k == KD - 1)
                            piece_end(last, name if j else None)
                for i in range(8):
                    late_modulation(f, 11 + i)
                    o = begin(f"{tag}_y{i}", "dve")
                    for part in range(3):
                        (k0, k1, _, _), w_hi, w_lo = next_piece()
                        if i == 0:
                            pe.wait_ge(sem("hid_split"), 11 * f + k1 // 2)
                        for k in range(k0, k1):
                            last = three(o[:, 0:L], w_hi[:, k - k0, :], w_lo[:, k - k0, :], hid_hi[:, k, :],
                                         hid_lo[:, k, :], k == 0, k == KF - 1)
                        piece_end(last, f"{tag}_y{i}" if part == 2 else None)

            def squares_by_block(tag, sq=sq2):
                o = begin("ss_" + tag, "dve")
                for k in range(KD):
                    pe.wait_ge(sem("sq_" + tag), k + 1)
                    last = mm(o[:, 0:L], ones[:], sq[:, k, :], k == 0, k == KD - 1)
                end(last)

            pe.wait_ge(sem("ones"), 1)
            pe.wait_ge(sem("silu_c"), 2)
            for i in range(4):
                ada_row(i)
                if i == 1:
                    pe.wait_ge(sem("early_landed"), 16)
                if i:
                    ada_turn(i - 1)
            ada_turn(3)
            squares("n1", sq1, KD)
            h1_hi = lambda k: h_hi_1[:, k, :]
            split_feature("iq", 2, h1_hi, h_lo_1, "act", need=norm_need(0))
            pe.wait_ge(sem("h_n1"), 1)
            w = next_slab("w_idx", 0).rearrange("p (k n) -> p k n", k=KD)
            o = begin("ik", "act")
            for k in range(KD):
                last = mm(o[:, 0:L], w[:, k, 0:P], h_t[:, k, :], k == 0, k == KD - 1)
            end(last)
            o = begin("iw", "act")
            for t in range(NT):
                for k in range(KD):
                    last = mm(o[:, t * 8:t * 8 + 8], h_t[:, k, t * P:(t + 1) * P], w[:, k, P:P + 8], k == 0, k == KD - 1)
            end(last)
            release()
            pe.wait_ge(*emptied("ik"))
            for t in range(NT):
                for h in range(8):
                    r = 64 * (h % 2)
                    n = (t + 1) * P
                    o = begin(f"is{t}_{h}", "act")
                    end(mm(o[:, 0:n], iq_t[r:r + 64, h // 2, t * P:(t + 1) * P], ik_t[r:r + 64, 0:n], True, True))
            split_feature("q", 2, h1_hi, h_lo_1, "act")
            split_feature("k", 2, h1_hi, h_lo_1, "act")
            for a, tag in ((0, "q"), (1, "k")):
                for i in range(2):
                    pe.wait_ge(*emptied(f"{tag}{i}"))
                    o = begin(f"{tag}ss{i}", "dve")
                    end(mm(o[:, 0:BANK], const("pair"), raw_sq[:, a, 2 * i:2 * i + 2, :].rearrange("p j t -> p (j t)"),
                           True, True))
            split_feature("cc", 2, h1_hi, h_lo_1, "act")
            split_feature("cx", 2, h1_hi, h_lo_1, "dve")
            split_feature("cb", 2, h1_hi, h_lo_1, "dve")
            split_token("v", 1, h_hi_1, h_lo_1)
            pe.wait_ge(sem("qk_ready"), 4)
            for t in range(NT):
                n = (t + 1) * P
                for i in range(2 * (t + 1)):
                    per = 4 // (t + 1)
                    o = begin(f"at{t}_{i}", "dve")
                    for j in range(per):
                        h = 4 * (i // 2) + i % 2 + 2 * j
                        r = 64 * (h % 2)
                        last = mm(o[:, j * n:(j + 1) * n], q_t[r:r + 64, h // 2, t * P:(t + 1) * P],
                                  k_t[r:r + 64, h // 2, 0:n], True, True)
                    end(last)
            ada_row(4)
            squares("conv", sq1, KA)
            for t in range(NT):
                pe.wait_ge(sem("probs"), t + 1)
                for i in range(2 * (t + 1)):
                    o = begin(f"pt{t}_{i}", "act")
                    for j in range(4):
                        h, s = divmod(4 * i + j, t + 1)
                        last = nc.tensor.transpose(o[:, j * P:(j + 1) * P], probs[t][:, h, s * P:(s + 1) * P], ident)
                    end(last)
                if t == 0:
                    ada_row(5)
                    ada_turn(4)
            pe.wait_ge(*emptied("pt1_3"))
            for j in range(KA):
                o = begin(f"pv{j}", "act")
                for h in (2 * j, 2 * j + 1):
                    c = (h % 2) * L
                    last = mm(o[:, c:c + P], v_n[:, 0, j * P:(j + 1) * P], p_t0[:, h, :], True, True)
                    for s in range(2):
                        last = mm(o[:, c + P:c + L], v_n[:, s, j * P:(j + 1) * P], p_t1[:, h, s, :], s == 0, s == 1)
                end(last)
            ada_turn(5)
            ada_row(6)
            squares("att", sq1, KA)
            ada_row(7)
            ada_turn(6)
            ada_row(8)
            ada_turn(7)
            split_feature("wo", 4, lambda k: h_hi_1[:, k, :], y_mix_lo, "dve",
                          need={k: (sem("y_split"), (k + 2) if k < KA else 1) for k in range(KD)})
            squares_by_block("n2", sq1)
            ada_row(9)
            ada_turn(8)
            ada_turn(9)
            need = norm_need(1)
            for i in range(4):
                split_feature("pq", 2, lambda k: h_hi_2[:, k, :], h_lo_2, "act", need=need, start=2 * i)
                need = None
                if i == 0:
                    pe.wait_ge(sem("subkeys"), 16)
                pe.wait_ge(*emptied(f"pq{2 * i + 1}"))
                for t in range(NT):
                    o = begin(f"ks{t}_{i}", "act")
                    for j in range(4):
                        hp = 4 * i + j
                        last = mm(o[:, j * P:(j + 1) * P], pq_t[:, hp, t * P:(t + 1) * P], subkeys[:, hp, :], True, True)
                    end(last)
            pe.wait_ge(sem("h_n2"), 1)
            for t in range(NT):
                for i in range(2):
                    o = begin(f"ht{t}_{i}", "act")
                    for j in range(4):
                        last = nc.tensor.transpose(o[:, j * P:(j + 1) * P], h_t[:, 4 * i + j, t * P:(t + 1) * P], ident)
                    end(last)
            for i in (10, 11):
                ada_row(i)
                ada_turn(i)

            modulation("ada2_", "w_ada_2", range(MOD_CTX), silu_c2, 2)
            squares("ctx1", hid, KD)
            pe.wait_ge(sem("h_ctx1"), 1)
            feed_forward("fc", 1, h_t)
            squares("ctx2", hid, KD)
            pe.wait_ge(sem("h_ctx2"), 1)
            by_token("kc", "w_in_2", range(2, 4), h_t, "act")
            by_token("vc", "w_in_2", range(4, 8), h_t, "act")

            for t in range(NT):
                pe.wait_ge(sem("experts"), t + 1)
                for i in range(2):
                    o = begin(f"yt{t}_{i}", "dve")
                    for j in range(4):
                        last = nc.tensor.transpose(o[:, j * P:(j + 1) * P],
                                                   y_of[t][:, (4 * i + j) * P:(4 * i + j + 1) * P], ident)
                    end(last)
            squares_by_block("x1")
            for h in range(RH):
                for a in range(2):
                    pe.wait_ge(sem("k_fade"), 2 * h + a + 1)
                    for b in range(2):
                        o = begin(f"st{h}_{a}_{b}", "act")
                        for t in range(NT):
                            last = mm(o[:, 0:DV], k_fade[(2 * h + a) % 4][:, t, b * P:(b + 1) * P],
                                      vc[:, t, h * DV:(h + 1) * DV], t == 0, t == 1)
                        end(last)
            split_feed_forward("f1", 2, 0)
            squares_by_block("x2")
            split_feature("gf", 4, h_hi_of, h_lo, "act", need=norm_need(3))
            split_feature("f", 4, h_hi_of, h_lo, "act")
            pe.wait_ge(*emptied("f3"))
            pe.wait_ge(sem("late"), 64)
            for t in range(NT):
                for g in range(FG):
                    o = begin(f"z{t}_{g}", "act")
                    for k in range(2):
                        last = mm(o[:, 0:BANK], f_t[:, 2 * g + k, t * P:(t + 1) * P],
                                  dft[:, k, :, :].rearrange("p a c -> p (a c)"), k == 0, k == 1)
                    end(last)
            pe.wait_ge(*emptied("z1_3"))
            for i in range(4):
                o = begin(f"mx{i}", "dve")
                for j in range(2):
                    n = 0
                    for t in range(NT):
                        for a in range(2):
                            last = mm(o[:, j * L:(j + 1) * L], dft_z[:, t, i, a, j * P:(j + 1) * P], dft[:, t, a, :],
                                      n == 0, n == 3)
                            n += 1
                end(last)
            split_feature("pf", 4, lambda k: mixed_hi[:, k, :], mixed_lo, "dve",
                          need={k: emptied(f"mx{k // 2}") for k in range(0, KD, 2)})
            split_feature("ga", 4, h_hi_of, h_lo, "act")
            split_feature("rq", 4, h_hi_of, h_lo, "dve")
            split_feature("rk", 4, h_hi_of, h_lo, "dve")
            split_token("rv", 4, h_hi, h_lo)
            split_feature("rg", 8, h_hi_of, h_lo, "act")
            def scores(h):
                o = begin(f"sc{h}", "dve")
                for t in range(NT):
                    for b in range(2):
                        last = mm(o[:, t * L:(t + 1) * L], rk_t[:, 2 * h + b, t * P:(t + 1) * P], rq_t[:, 2 * h + b, :],
                                  b == 0, b == 1)
                end(last)

            scores(0)
            for h in range(RH):
                pe.wait_ge(sem("q_faded"), h + 1)
                for t in range(NT):
                    o = begin(f"o{h}_{t}", "dve")
                    n = 0
                    for a in range(2):
                        for b in range(2):
                            mm(o[:, 0:DV], q_faded[h % 2][:, a, b, t * P:(t + 1) * P], state[:, h, a, b, :], n == 0, False)
                            n += 1
                    pe.wait_ge(*emptied(f"sc{h}"))
                    for s in range(NT):
                        last = mm(o[:, 0:DV], sc_t[h % 2][:, s, t * P:(t + 1) * P], rv[:, s, h * DV:(h + 1) * DV],
                                  False, s == 1)
                    end(last)
                if h + 1 < RH:
                    scores(h + 1)
                for t in range(NT):
                    pe.wait_ge(*emptied(f"o{h}_{t}"))
                    o = begin(f"ot{h}_{t}", "dve")
                    for j in range(4):
                        last = nc.tensor.transpose(o[:, j * P:(j + 1) * P], o_n[t][:, j * P:(j + 1) * P], ident)
                    end(last)
            split_feature("pr", 4, lambda k: rg_hi[:, k % 4 // 2, k // 4, k % 2, :], rg_lo, "dve", kb=16,
                          need={4 * h: (sem("rg_split"), h + 1) for h in range(RH)})
            split_feature("w2o", 4, lambda k: mixed_hi[:, k, :], m_lo, "dve",
                          need={2 * i: (sem("m_split"), i + 1) for i in range(4)})
            squares_by_block("x3")
            split_feed_forward("f2", 4, 1)
            squares_by_block("fin")
            assert used[0] == len(slabs)

        @block.sync
        def _(sp):
            sp.dma_start(prm[:], dram["params"]).then_inc(sem("params"), 16)
            for n, (name, i, words) in enumerate(slabs):
                slot, _, replaced = slots[n]
                if slabs[n][:2] == ("peer_wq", 1):
                    sp.wait_ge(sem("y_mix"), 2 * KA)
                    sp.dma_start(subkeys.rearrange("p h n -> p (h n)"), dram["subkeys"][0]).then_inc(sem("subkeys"), 16)
                if replaced is not None and slabs[replaced][:2] == ("peer_wq", 3):
                    sp.wait_ge(*slab_free[replaced])
                    sp.dma_start(ctx_t.rearrange("p k t -> p (k t)"), dram["ctx"]).then_inc(sem("ctx_landed"), 16)
                if replaced is not None:
                    sp.wait_ge(*slab_free[replaced])
                at = slot * SLAB
                sp.dma_start(ring[:, at:at + words], dram[name][i]).then_inc(landed[slot], 16)
                if n == 1:
                    sp.dma_start(x_t.rearrange("p k t -> p (k t)"), dram["x"]).then_inc(sem("x_landed"), 16)
                    sp.dma_start(early[:], dram["early"]).then_inc(sem("early_landed"), 16)
                if n == second_at + SPLIT_RING - 1:
                    sp.wait_ge(sem("experts_added"), 1)
                    at = 0
                    for dst, w in ((late_decay, LATE_DECAY), (dft, LATE_DFT), (rope, LATE_ROPE), (late_xi, LATE_XI)):
                        s = "p m t i -> p (m t i)" if w == LATE_DECAY else (
                            "p k a c -> p (k a c)" if w == LATE_DFT else "p a t -> p (a t)")
                        sp.dma_start(dst.rearrange(s), dram["late"][:, at:at + w]).then_inc(sem("late"), 16)
                        at += w
            sp.wait_ge(sem("out_ready"), 1)
            sp.dma_start(out, h_t.rearrange("p k t -> p (k t)")).then_inc(sem("stored"), 16)
            sp.wait_ge(sem("stored"), 16)

        @block.gpsimd
        def _(pool):
            for i in range(first_pieces):
                pool.wait_ge(hi_made, i + 1)
                nc.gpsimd.tensor_tensor(whole(i, ring_r), whole(i, ring), upper(i).bitcast(F32),
                                        ALU.subtract).then_inc(lo_made, 1)
            staged = sem("staged")
            for t in range(NT):
                pool.wait_ge(sem("ids"), t + 1)
                with pool.Fori(0, SLOTS // ROUND) as r:
                    for half in range(2):
                        n = ROUND // 2
                        pool.wait_ge(sem("row_free"), r * ROUND + (t * SLOTS + half * n + 1))
                        nc.gpsimd.tensor_copy(idx_stage[:, half * n:(half + 1) * n],
                                              ids[:, bass.ds(r * ROUND + (t * SLOTS + half * n), n)]).then_inc(staged, 1)
                        pool.wait_ge(staged, r * 2 + (t * 2 * SLOTS // ROUND + half + 1))
                        for s in range(n):
                            slot = half * n + s
                            pool.wait_ge(sem("row_free"), r * ROUND + (t * SLOTS + slot + 1))
                            pool.sem_inc(sem("row_turn"), 1)
                            nc.gpsimd.indirect_dma_start(
                                rows[slot % GBUF], None, dram["experts"],
                                bass.IndirectOffsetOnAxis(ap=idx_stage[:, slot:slot + 1], axis=0),
                            ).then_inc(row_landed[slot % GBUF], 16)

            summed = sem("late_summed")
            for j, n in enumerate(late_mod):
                slot, loads, _ = slots[n]
                w = ring[:, slot * SLAB:(slot + 1) * SLAB].rearrange("p (k n) -> p k n", k=KD)
                acc = late_sum[j % 2]
                pool.wait_ge(landed[slot], 16 * loads)
                if j >= 2:
                    pool.wait_ge(group_done, index[f"late_mod{j - 2}"] + 1)
                c = silu_c2.rearrange("p (k s) -> p k s", s=2)[:, :, 0:1].to_broadcast([P, KD, SLAB // KD])
                nc.gpsimd.tensor_tensor(w, w, c, ALU.mult).then_inc(summed, 1)
                pool.wait_ge(summed, 3 * j + 1)
                nc.gpsimd.tensor_tensor(w[:, 0:4, :], w[:, 0:4, :], w[:, 4:8, :], ALU.add).then_inc(summed, 1)
                pool.wait_ge(summed, 3 * j + 2)
                nc.gpsimd.tensor_tensor(w[:, 0:2, :], w[:, 0:2, :], w[:, 2:4, :], ALU.add).then_inc(summed, 1)
                pool.wait_ge(summed, 3 * j + 3)
                if j == 0:
                    pool.wait_ge(sem("experts_added"), 1)
                nc.gpsimd.tensor_tensor(acc, w[:, 0, :], w[:, 1, :], ALU.add).then_inc(sem("late_mod"), 1)

        @block.scalar
        def _(act):
            taken, roots = [0], [0]

            def root(ap):
                roots[0] += 1
                act.wait_ge(sem("root_in"), roots[0])
                nc.scalar.activation(ap, ap, ACT.Sqrt).then_inc(sem("root_out"), 1)

            hi_count = [0]

            def split_until(q):
                while hi_count[0] <= q:
                    i = hi_count[0]
                    hi_count[0] += 1
                    if i >= PIECES:
                        act.wait_ge(*piece_read[i - PIECES])
                    if i == first_pieces:
                        act.wait_ge(*slab_free[last_in_split])
                    slot, loads, _ = slots[pieces[i][0]]
                    act.wait_ge(landed[slot], 16 * loads)
                    nc.scalar.activation(upper(i), whole(i, ring), ACT.Copy).then_inc(hi_made, 1)

            def ahead(name):
                q = piece_of[name]
                split_until(min(q + PIECES, phase_end(q)) - 1)

            def take(name):
                _, who, count = groups[index[name]]
                if name in piece_of:
                    ahead(name)
                taken[0] += 1
                assert who == "act" and count == taken[0], (name, who, count, taken[0])
                act.wait_ge(group_done, index[name] + 1)
                return psum[:, index[name] % BANKS, :]

            def drain(ins):
                ins.then_inc(drained["act"], 1)

            def flat(ap):
                return ap.rearrange("p a t -> p (a t)")

            def copy_out(name, dst, func=ACT.Copy, width=BANK, scale=1.0):
                drain(nc.scalar.activation(dst, take(name)[:, 0:width], func, scale=scale))

            def square(tag, dst, src, kb):
                nc.scalar.activation(flat(dst[:, 0:kb, :]), flat(src), ACT.Square).then_inc(sem("sq_" + tag), 1)

            def normed_hi(m, shift, hi):
                for k in range(KD):
                    act.wait_ge(sem("h_scaled"), KD * m + k + 1)
                    nc.scalar.activation(hi[:, k, :], h_t[:, k, :], ACT.Identity,
                                         bias=shift[:, k:k + 1]).then_inc(sem("h_hi"), 1)

            def ada_row(i):
                if i >= 2:
                    act.wait_ge(group_done, index[f"ada{i - 2}"] + 1)
                drain(nc.scalar.activation(mod_row[:, i % 2, :], take(f"ada_row{i}")[0:1, :], ACT.Copy))

            def ada_turned(i):
                copy_out(f"ada{i}", mod1[:, 4 * i:4 * i + 4], width=4)

            def norm_hi(tag, m, shift, names, sq=sq2, hi=h_hi, between=None):
                for k in range(KD):
                    if tag == "x2":
                        late_modulation(11 + k)
                    if names:
                        name = names[k * len(names) // KD]
                        ahead(name)
                        act.wait_ge(*emptied(name))
                    nc.scalar.activation(sq[:, k, :], x_t[:, k, :], ACT.Square).then_inc(sem("sq_" + tag), 1)
                root(rstd[:])
                if between:
                    between()
                if m is not None:
                    normed_hi(m, shift, hi)

            def decay_exp(n):
                h, a = divmod(n, 2)
                if n >= 2:
                    act.wait_ge(sem("decay_used"), n - 1)
                nc.scalar.activation(decay_tmp[:, a], late_decay[:, a].rearrange("p t i -> p (t i)"), ACT.Exp,
                                     scale=lg[:, 4 * a + h:4 * a + h + 1]).then_inc(sem("decay_exp"), 1)

            def late_modulation(step):
                if step in LATE_TURN:
                    j = LATE_TURN.index(step)
                    c = 4 * (MOD_CTX + j)
                    copy_out(f"late_mod{j}", mod2[:].rearrange("p (j s) -> p j s", s=2)[:, c:c + 4, 0], width=4)

            def split_ff_act(tag, f):
                for i in range(12):
                    if f == 0 and i < 11:
                        late_modulation(i)
                    if i < 11:
                        drain(nc.scalar.activation(flat(hid[:, 2 * i:2 * i + 2, :]), take(f"{tag}_a{i}"), ACT.Silu))
                    else:
                        ahead(f"{tag}_b10")
                    if f == 0 and i < 2 * RH:
                        decay_exp(i)
                    if i:
                        act.wait_ge(*emptied(f"{tag}_b{i - 1}"))
                        nc.scalar.activation(flat(hid_hi[:, 2 * i - 2:2 * i, :]), flat(hid[:, 2 * i - 2:2 * i, :]),
                                             ACT.Copy).then_inc(sem("hid_hi"), 1)

            def ff_act(tag):
                for i in range(11):
                    drain(nc.scalar.activation(flat(hid[:, 2 * i:2 * i + 2, :]), take(f"{tag}_a{i}"), ACT.Silu))
                    yield
                for i in range(8):
                    yield

            act.wait_ge(sem("params"), 16)
            nc.scalar.activation(silu_c, param("c"), ACT.Silu).then_inc(sem("silu_c"), 1)
            nc.scalar.activation(silu_c2, param("c2"), ACT.Silu).then_inc(sem("silu_c"), 1)
            act.wait_ge(sem("x_landed"), 16)
            square("n1", sq1, x_t, KD)
            act.wait_ge(sem("lg_abs"), 1)
            nc.scalar.activation(lg_e, lg_z, ACT.Exp, scale=-1.0).then_inc(sem("lg_exp"), 1)
            for i in range(4):
                ada_row(i)
                if i:
                    ada_turned(i - 1)
                if i == 2:
                    split_until(PIECES - 1)
            ada_turned(3)
            root(rstd[:])
            normed_hi(0, mod1[:, 0:8], h_hi_1)
            for i in range(2):
                copy_out(f"iq{i}", flat(iq_t[:, 2 * i:2 * i + 2, :]))
            copy_out("ik", ik_t, width=L)
            copy_out("iw", iw.rearrange("p t h -> p (t h)"), width=16)
            for t in range(NT):
                for h in range(8):
                    n = 8 * t + h
                    if n >= 4:
                        act.wait_ge(sem("relu_used"), n - 3)
                    copy_out(f"is{t}_{h}", relu[:, n % 4, 0:(t + 1) * P], ACT.Relu, (t + 1) * P)
            for a, tag in ((0, "q"), (1, "k")):
                for i in range(2):
                    o = take(f"{tag}{i}")
                    nc.scalar.activation(flat(raw[:, a, 2 * i:2 * i + 2, :]), o, ACT.Copy)
                    drain(nc.scalar.activation(flat(raw_sq[:, a, 2 * i:2 * i + 2, :]), o, ACT.Square))
            for i in range(2):
                copy_out(f"cc{i}", flat(gate_c[:, 2 * i:2 * i + 2, :]))
            for a in range(2):
                for i in range(2):
                    root(flat(raw_sq[:, a, 2 * i:2 * i + 2, :]))
                    ahead(f"{('cx', 'cb')[a]}{i}")
            for t in range(NT):
                copy_out(f"v{t}", v_n[:, t, :])
            act.wait_ge(sem("y_conv"), 1)
            square("conv", sq1, y_conv, KA)
            for t in range(NT):
                act.wait_ge(sem("shifted"), t + 1)
                nc.scalar.activation(probs[t], probs[t], ACT.Exp, scale=ATT_SCALE).then_inc(sem("exped"), 1)
            ada_row(4)
            root(rstd[:])
            for t in range(NT):
                for i in range(2 * (t + 1)):
                    dst = p_t0[:, 4 * i:4 * i + 4, :] if t == 0 else p_t1[:, 2 * i:2 * i + 2, :, :]
                    s = "p h q -> p (h q)" if t == 0 else "p h s q -> p (h s q)"
                    copy_out(f"pt{t}_{i}", dst.rearrange(s))
                if t == 0:
                    ada_row(5)
                    ada_turned(4)
            for j in range(KA):
                o = take(f"pv{j}")
                nc.scalar.activation(y_att[0:64, j, :], o[0:64, 0:L], ACT.Copy)
                drain(nc.scalar.activation(y_att[64:128, j, :], o[64:128, L:2 * L], ACT.Copy))
            ada_turned(5)
            act.wait_ge(sem("y_mix"), KA)
            act.wait_ge(drained["act"], taken[0])
            square("att", sq1, y_att, KA)
            nc.scalar.activation(flat(h_hi_1[:, KA:KD, :]), flat(y_mix[:, KA:KD, :]), ACT.Copy).then_inc(sem("y_hi"), 1)
            ada_row(6)
            root(rstd[:])
            for j in range(KA):
                act.wait_ge(sem("y_mix"), KA + j + 1)
                nc.scalar.activation(h_hi_1[:, j, :], y_mix[:, j, :], ACT.Copy).then_inc(sem("y_hi"), 1)
            split_until(first_out + PIECES - 1)
            ada_row(7)
            ada_turned(6)
            ada_row(8)
            ada_turned(7)

            def last_modulation():
                ada_row(9)
                ada_turned(8)
                ada_turned(9)

            norm_hi("n2", 1, mod1[:, 24:32], [f"wo{i}" for i in range(4)], sq1, h_hi_2, last_modulation)
            for i in range(4):
                for n in (2 * i, 2 * i + 1):
                    copy_out(f"pq{n}", flat(pq_t[:, 2 * n:2 * n + 2, :]))
                for t in range(NT):
                    copy_out(f"ks{t}_{i}", key_s[:, t, 4 * i:4 * i + 4, :].rearrange("p h n -> p (h n)"))
            for t in range(NT):
                for i in range(2):
                    copy_out(f"ht{t}_{i}", h2[:, t, i * BANK:(i + 1) * BANK])
            for i in (10, 11):
                ada_row(i)
                ada_turned(i)

            def background():
                for i in range(CHOICE_STEPS):
                    if i < MOD_CTX:
                        copy_out(f"ada2_{i}", mod2[:, 8 * i:8 * i + 8], width=8)
                    yield
                act.wait_ge(sem("ctx_landed"), 16)
                act.wait_ge(sem("ids"), 2)
                square("ctx1", hid, ctx_t, KD)
                root(rstd[:])
                yield
                yield from ff_act("fc")
                act.wait_ge(*emptied("fc_y7"))
                square("ctx2", hid, ctx_t, KD)
                root(rstd[:])
                yield
                act.wait_ge(sem("h_ctx2"), 1)
                for i in range(12):
                    c, t = divmod(i, 2)
                    if c < 2:
                        copy_out(f"kc{i}", kc[:, t, c * BANK:(c + 1) * BANK])
                    else:
                        copy_out(f"vc{i - 4}", vc[:, t, (c - 2) * BANK:(c - 1) * BANK])
                    yield

            bg = background()
            for t in range(NT):
                act.wait_ge(sem("best"), t + 1)
                flat_best = best[:, t].rearrange("p h n -> p (h n)")
                nc.scalar.activation(flat_best, flat_best, ACT.Exp).then_inc(sem("best_exp"), 1)
                for b in range(SLOTS // BATCH):
                    n = t * (SLOTS // BATCH) + b
                    act.wait_ge(sem("dots"), BATCH * (n + 1))
                    nc.scalar.activation(acts[:, n % 8, :], dots[:, n % 8, :], ACT.Gelu_apprx_tanh).then_inc(sem("gelus"), 1)
                    if b % 2 == 1:
                        next(bg, None)
            for _ in bg:
                pass
            act.wait_ge(sem("lg"), 1)
            for a in range(2):
                for t in range(NT):
                    at = EARLY_AT["age"][0] + 2 * a + t
                    for h in range(RH):
                        c = (a * NT + t) * RH + h
                        last = nc.scalar.activation(fade[:, c:c + 1], early[:, at:at + 1], ACT.Exp,
                                                    scale=lg[:, 4 * a + h:4 * a + h + 1])
            last.then_inc(sem("fade"), 1)
            act.wait_ge(sem("experts_added"), 1)
            norm_hi("x1", 2, mod2_v[:, 0, :, 0], None)
            for h in range(RH):
                for a in range(2):
                    for b in range(2):
                        copy_out(f"st{h}_{a}_{b}", state[:, h, a, b, :])
                    if h == RH - 1:
                        split_until(first_pieces + PIECES // 2 * (a + 1) - 1)
            act.wait_ge(sem("late"), 64)
            split_ff_act("f1", 0)
            norm_hi("x2", 3, mod2_v[:, 3, :, 0], [f"f1_y{i}" for i in range(8)])
            for i in range(4):
                copy_out(f"gf{i}", flat(sig[:, 2 * i:2 * i + 2, :]), ACT.Sigmoid)
            for i in range(4):
                copy_out(f"f{i}", flat(f_t[:, 2 * i:2 * i + 2, :]))
            for t in range(NT):
                for g in range(FG):
                    o = take(f"z{t}_{g}")
                    nc.scalar.activation(dft_z[:, t, g, 0, :], o[:, 0:256], ACT.Copy)
                    drain(nc.scalar.activation(dft_z[:, t, g, 1, :], o[:, 256:512], ACT.Copy, scale=-1.0))
            for i in range(4):
                act.wait_ge(group_done, index[f"mx{i}"] + 1)
                nc.scalar.activation(flat(mixed_hi[:, 2 * i:2 * i + 2, :]), psum[:, index[f"mx{i}"] % BANKS, :],
                                     ACT.Copy).then_inc(sem("mixed_hi"), 1)
            ahead("pf3")
            act.wait_ge(*emptied("pf3"))
            for i in range(4):
                copy_out(f"ga{i}", flat(sig[:, 2 * i:2 * i + 2, :]), ACT.Sigmoid)
            for i in range(8):
                c, t = divmod(i, 2)
                copy_out(f"rv{i}", rv[:, t, c * BANK:(c + 1) * BANK])
            for i in range(8):
                copy_out(f"rg{i}", flat(rg_t[:, 2 * i:2 * i + 2, :]), ACT.Silu)
            def xi_of(h):
                if h:
                    act.wait_ge(sem("q_faded"), h)
                for a in range(2):
                    last = nc.scalar.activation(xi[:, a, :], late_xi[:, a, :], ACT.Exp,
                                                scale=lg[:, 4 * a + h:4 * a + h + 1])
                last.then_inc(sem("xi"), 1)

            xi_of(0)
            xi_of(1)
            for h in range(RH):
                if h + 2 < RH:
                    xi_of(h + 2)
                for t in range(NT):
                    root(stat[:, 8:9])
                act.wait_ge(sem("turned"), h + 1)
                nc.scalar.activation(rg_hi[:, :, h].rearrange("p a j t -> p a (j t)"),
                                     rg_t[:, 4 * h:4 * h + 4, :].rearrange("p (a j) t -> p a (j t)", a=2),
                                     ACT.Copy).then_inc(sem("rg_hi"), 1)
            for i in range(4):
                ahead(f"pr{i}")
                act.wait_ge(sem("merged"), i + 1)
                nc.scalar.activation(flat(mixed_hi[:, 2 * i:2 * i + 2, :]), flat(m_t[:, 2 * i:2 * i + 2, :]),
                                     ACT.Copy).then_inc(sem("m_hi"), 1)
            norm_hi("x3", 4, mod2_v[:, 6, :, 0], [f"w2o{i}" for i in range(4)])
            split_ff_act("f2", 1)
            norm_hi("fin", None, None, [f"f2_y{i}" for i in range(8)])
            assert taken[0] == sum(g[1] == "act" for g in groups)

        @block.vector
        def _(v):
            taken, steps, roots = [0], {}, [0]
            chain = sem("dve_step")

            def step(ins, s=chain):
                ins.then_inc(s, 1)
                steps[s.name] = steps.get(s.name, 0) + 1
                v.wait_ge(s, steps[s.name])

            lo_count = [first_pieces]

            def split_until(q):
                while lo_count[0] <= q:
                    i = lo_count[0]
                    lo_count[0] += 1
                    v.wait_ge(hi_made, i + 1)
                    nc.vector.tensor_tensor(whole(i, ring_r), whole(i, ring), upper(i).bitcast(F32),
                                            ALU.subtract).then_inc(lo_made, 1)

            def ahead(name):
                q = piece_of[name]
                split_until(min(q + PIECES, phase_end(q)) - 1)

            def take(name):
                _, who, count = groups[index[name]]
                if name in piece_of:
                    ahead(name)
                taken[0] += 1
                assert who == "dve" and count == taken[0], (name, who, count, taken[0])
                v.wait_ge(group_done, index[name] + 1)
                return psum[:, index[name] % BANKS, :]

            def drain(ins):
                step(ins, drained["dve"])

            def flat(ap):
                return ap.rearrange("p a t -> p (a t)")

            TT, TS, STT = nc.vector.tensor_tensor, nc.vector.tensor_scalar, nc.vector.scalar_tensor_tensor

            def rooted(dst):
                roots[0] += 1
                step(nc.vector.reciprocal(dst, dst), sem("root_in"))
                v.wait_ge(sem("root_out"), roots[0])

            def root(name, dst, width, n):
                drain(TS(dst, take(name)[:, 0:width], 1.0 / n, EPS, ALU.mult, ALU.add))
                rooted(dst)

            def modulated(tag, src, dst, weight, scale, shift):
                step(STT(scale_of[tag], scale, 1.0, weight, ALU.add, ALU.mult))
                root("ss_" + tag, rstd[:], L, D)
                step(TT(dst, src, rstd[:].unsqueeze(1).to_broadcast([P, KD, L]), ALU.mult))
                for k in range(KD):
                    last = TS(dst[:, k, :], dst[:, k, :], scale_of[tag][:, k:k + 1], shift[:, k:k + 1], ALU.mult, ALU.add)
                    if k < KD - 1:
                        last.then_inc(chain, 1)
                        steps[chain.name] += 1
                step(last, sem("h_" + tag))

            def rest(dst, src, hi, s):
                step(TT(dst, src, hi.bitcast(F32), ALU.subtract), sem(s))

            def split_modulated(tag, m, weight, scale, shift, hi=h_hi, lo=h_lo, late=None):
                if late:
                    root("ss_" + tag, rstd[:], L, D)
                    late()
                step(STT(scale_of[tag], scale, 1.0, weight, ALU.add, ALU.mult))
                if not late:
                    root("ss_" + tag, rstd[:], L, D)
                for k in range(KD + 2):
                    if k < KD:
                        STT(h_t[:, k, :], x_t[:, k, :], scale_of[tag][:, k:k + 1], rstd[:], ALU.mult,
                            ALU.mult).then_inc(sem("h_scaled"), 1)
                    if k >= 2:
                        b = k - 2
                        v.wait_ge(sem("h_hi"), KD * m + b + 1)
                        STT(lo[:, b, :], h_t[:, b, :], shift[:, b:b + 1], hi[:, b, :].bitcast(F32), ALU.add,
                            ALU.subtract).then_inc(sem("h_split"), 1)
                if lo is not h_lo:
                    v.wait_ge(sem("h_split"), KD * (m + 1))
                    for k in range(KD):
                        TS(h_t[:, k, :], h_t[:, k, :], shift[:, k:k + 1], None, ALU.add).then_inc(sem("h_whole"), 1)
                    v.wait_ge(sem("h_whole"), KD * (m + 1))
                    step(nc.vector.memset(stat[:, 0:1], 0.0), sem("h_" + tag))

            def decay(n):
                h, a = divmod(n, 2)
                v.wait_ge(sem("decay_exp"), n + 1)
                mask = flat(late_decay[:, 2 + a])
                if a == 0:
                    step(TT(flat(decay_t[:, h]), decay_tmp[:, 0], mask, ALU.mult), sem("decay_used"))
                else:
                    step(TT(decay_tmp[:, 1], decay_tmp[:, 1], mask, ALU.mult))
                    step(TT(flat(decay_t[:, h]), flat(decay_t[:, h]), decay_tmp[:, 1], ALU.add), sem("decay_used"))

            def split_ff_dve(tag, f, gate):
                for i in range(12):
                    if i < 11:
                        o = take(f"{tag}_b{i}")
                        v.wait_ge(*emptied(f"{tag}_a{i}"))
                        hb = flat(hid[:, 2 * i:2 * i + 2, :])
                        drain(TT(hb, hb, o, ALU.mult))
                    if i:
                        v.wait_ge(sem("hid_hi"), 11 * f + i)
                        rest(flat(hid_lo[:, 2 * i - 2:2 * i, :]), flat(hid[:, 2 * i - 2:2 * i, :]),
                             flat(hid_hi[:, 2 * i - 2:2 * i, :]), "hid_split")
                    if f == 0 and i < 2 * RH:
                        decay(i)
                for i in range(8):
                    drain(STT(x_t[:, i, :], take(f"{tag}_y{i}")[:, 0:L], gate[:, i:i + 1], x_t[:, i, :],
                              ALU.mult, ALU.add))

            def mix(src, dst, k0, weight):
                for j in range(KA):
                    step(STT(dst[:, k0 + j, :], src[:, j, :], weight[:, j:j + 1], rstd[:], ALU.mult, ALU.mult),
                         sem("y_mix"))

            def residual(names, dst, gate, per):
                n = 0
                for name in names:
                    o = take(name)
                    for j in range(per):
                        ins = STT(dst[:, n, :], o[:, j * L:(j + 1) * L], gate[:, n:n + 1], dst[:, n, :], ALU.mult, ALU.add)
                        n += 1
                        if j < per - 1:
                            step(ins)
                    drain(ins)

            def ff_dve(tag, dst, gate):
                for i in range(11):
                    o = take(f"{tag}_b{i}")
                    v.wait_ge(*emptied(f"{tag}_a{i}"))
                    hb = flat(hid[:, 2 * i:2 * i + 2, :])
                    drain(TT(hb, hb, o, ALU.mult))
                    yield
                for i in range(8):
                    drain(STT(dst[:, i, :], take(f"{tag}_y{i}")[:, 0:L], gate[:, i:i + 1], dst[:, i, :],
                              ALU.mult, ALU.add))
                    yield

            step(nc.vector.memset(ones[:], 1.0), sem("ones"))
            v.wait_ge(sem("params"), 16)
            step(STT(lg_z, param("decay"), -1.0, param("decay"), ALU.mult, ALU.max), sem("lg_abs"))
            step(nc.vector.memset(padded[:, :, 0:2], 0.0))
            v.wait_ge(sem("early_landed"), 16)
            v.wait_ge(sem("x_landed"), 16)
            step(TS(flat(fill), const("causal"), 1.0, -FILL, ALU.subtract, ALU.mult))
            v.wait_ge(sem("lg_exp"), 1)
            step(TS(lg_z, lg_e, 2.0, None, ALU.add))
            step(nc.vector.reciprocal(lg_z, lg_z))
            step(TT(lg_z, lg_z, lg_e, ALU.mult))
            step(TT(lg_z2, lg_z, lg_z, ALU.mult))
            step(TS(lg_s, lg_z2, 1.0 / 17, None, ALU.mult))
            for odd in (15, 13, 11, 9, 7, 5, 3):
                step(STT(lg_s, lg_s, 1.0 / odd, lg_z2, ALU.add, ALU.mult))
            step(STT(lg_s, lg_s, 1.0, lg_z, ALU.add, ALU.mult))
            step(TS(lg_e, param("decay"), 0.0, None, ALU.min))
            step(STT(lg, lg_s, -2.0, lg_e, ALU.mult, ALU.add), sem("lg"))
            v.wait_ge(*emptied("ada3"))
            step(TT(mod1[:, 0:16], mod1[:, 0:16], param("b_ada")[:, 0:16], ALU.add))
            split_modulated("n1", 0, param("norm1_w"), mod1[:, 8:16], mod1[:, 0:8], h_hi_1, h_lo_1)
            v.wait_ge(*emptied("iw"))
            for t in range(NT):
                n = (t + 1) * P
                if t == 0:
                    step(nc.vector.memset(idx[:, 0, P:L], 0.0))
                for h in range(8):
                    v.wait_ge(*emptied(f"is{t}_{h}"))
                    if h == 0:
                        ins = TS(idx[:, t, 0:n], relu[:, (8 * t + h) % 4, 0:n], iw[:, t, 0:1], None, ALU.mult)
                    else:
                        ins = STT(idx[:, t, 0:n], relu[:, (8 * t + h) % 4, 0:n], iw[:, t, h:h + 1], idx[:, t, 0:n],
                                  ALU.mult, ALU.add)
                    step(ins, sem("relu_used"))
            causal = const("causal")
            step(STT(flat(idx), flat(idx), IDX_SCALE, causal, ALU.mult, ALU.mult))
            step(TT(flat(idx), flat(idx), flat(fill), ALU.add))
            for t in range(NT):
                n = (t + 1) * P
                for _ in range(TOPK // 8):
                    step(nc.vector.max(max8, idx[:, t, 0:n]))
                    step(nc.vector.match_replace(idx[:, t, 0:n], max8, idx[:, t, 0:n], TAKEN))
            step(STT(flat(bias), flat(idx), TAKEN, causal, ALU.is_equal, ALU.mult))
            step(TS(flat(bias), flat(bias), 1.0, -MASKED, ALU.subtract, ALU.mult))
            for a, tag, dst in ((0, "q", q_t), (1, "k", k_t)):
                for i in range(2):
                    rs = flat(raw_sq[:, a, 2 * i:2 * i + 2, :])
                    root(f"{tag}ss{i}", rs, BANK, HD)
                    step(STT(flat(dst[:, 2 * i:2 * i + 2, :]), flat(raw[:, a, 2 * i:2 * i + 2, :]),
                             param(f"{tag}_norm_w")[:, 0:1], rs, ALU.mult, ALU.mult), sem("qk_ready"))
            for i in range(2):
                o = take(f"cx{i}").rearrange("p (j t) -> p j t", j=2)
                v.wait_ge(*emptied(f"cc{i}"))
                drain(TT(padded[:, 2 * i:2 * i + 2, 2:2 + L], gate_c[:, 2 * i:2 * i + 2, :], o, ALU.mult))
            cw, cb = param("conv_w"), param("conv_b")
            for j in range(KA):
                step(TS(y_conv[:, j, :], padded[:, j, 0:L], cw[:, j:j + 1], cb[:, j:j + 1], ALU.mult, ALU.add))
                for i in (1, 2):
                    step(STT(y_conv[:, j, :], padded[:, j, i:i + L], cw[:, 4 * i + j:4 * i + j + 1], y_conv[:, j, :],
                             ALU.mult, ALU.add))
            for i in range(2):
                o = take(f"cb{i}")
                yc = flat(y_conv[:, 2 * i:2 * i + 2, :])
                drain(TT(yc, yc, o, ALU.mult))
            step(nc.vector.memset(stat[:, 0:1], 0.0), sem("y_conv"))

            def logits(t):
                n, per = (t + 1) * P, 4 // (t + 1)
                for i in range(2 * (t + 1)):
                    o = take(f"at{t}_{i}").rearrange("p (h s) -> p h s", h=per)
                    first = 4 * (i // 2) + i % 2
                    drain(TT(probs[t][:, first:first + 2 * per - 1:2, :], o,
                             bias[:, t, 0:n].unsqueeze(1).to_broadcast([P, per, n]), ALU.add))
                step(nc.vector.tensor_reduce(mxs, probs[t], AX_X, ALU.max))
                step(TT(probs[t], probs[t], mxs.unsqueeze(2).to_broadcast([P, HEADS, n]), ALU.subtract), sem("shifted"))

            def normalise(t):
                v.wait_ge(sem("exped"), t + 1)
                step(nc.vector.tensor_reduce(mxs, probs[t], AX_X, ALU.add))
                step(nc.vector.reciprocal(mxs, mxs))
                step(TT(probs[t], probs[t], mxs.unsqueeze(2).to_broadcast([P, HEADS, (t + 1) * P]), ALU.mult),
                     sem("probs"))

            logits(0)
            logits(1)
            normalise(0)
            root("ss_conv", rstd[:], L, ATT)
            mix(y_conv, y_mix, KA, param("conv_out_norm_w"))
            normalise(1)
            v.wait_ge(sem("y_hi"), 1)
            rest(flat(y_mix_lo[:, KA:KD, :]), flat(y_mix[:, KA:KD, :]), flat(h_hi_1[:, KA:KD, :]), "y_split")
            root("ss_att", rstd[:], L, ATT)
            mix(y_att, y_mix, 0, param("attn_out_norm_w"))
            for j in range(KA):
                v.wait_ge(sem("y_hi"), j + 2)
                rest(y_mix_lo[:, j, :], y_mix[:, j, :], h_hi_1[:, j, :], "y_split")
            v.wait_ge(*emptied("ada5"))
            step(TT(mod1[:, 16:24], mod1[:, 16:24], param("b_ada")[:, 16:24], ALU.add))
            residual([f"wo{i}" for i in range(4)], x_t, mod1[:, 16:24], 2)

            def late_modulation():
                v.wait_ge(*emptied("ada9"))
                step(TT(mod1[:, 24:40], mod1[:, 24:40], param("b_ada")[:, 24:40], ALU.add))

            split_modulated("n2", 1, param("norm2_w"), mod1[:, 32:40], mod1[:, 24:32], h_hi_2, h_lo_2, late_modulation)

            def top16(rows_of):
                stages = (lambda a, o, i: nc.vector.max(o[:, 0:8], a),
                          lambda a, o, i: nc.vector.max_index(i[:, 0:8], o[:, 0:8], a),
                          lambda a, o, i: nc.vector.match_replace(a, o[:, 0:8], a, FILL),
                          lambda a, o, i: nc.vector.max(o[:, 8:16], a),
                          lambda a, o, i: nc.vector.max_index(i[:, 8:16], o[:, 8:16], a))
                mark = {}
                for n, stage in enumerate(stages):
                    for r, row in enumerate(rows_of):
                        if n:
                            v.wait_ge(chain, mark[r])
                        stage(*row).then_inc(chain, 1)
                        steps[chain.name] = mark[r] = steps.get(chain.name, 0) + 1
                v.wait_ge(chain, steps[chain.name])

            def choose_experts(t):
                fv = found[:].rearrange("p (h n) -> p h n", h=2 * PH)
                pl = place[:].rearrange("p (h n) -> p h n", h=PH)
                tv = top_v.rearrange("p (h a) n -> p h a n", a=2)
                ti = top_i.rearrange("p (h a) n -> p h a n", a=2)
                hi = half_i.rearrange("p (a n) -> p a n", a=2)
                hid_ = half_id.rearrange("p (a n) -> p a n", a=2)
                two = [P, 2, PSEL, PSEL]
                for g in range(PH // 2):
                    v.wait_ge(*emptied(f"ks{t}_{g}"))
                    for hp in (4 * g, 4 * g + 2):
                        top16([(key_s[:, t, n, :], top_v[:, n, :], fv[:, n, :]) for n in (hp, hp + 1)])
                        yield
                    hs = slice(2 * g, 2 * g + 2)
                    step(TT(combo[:, hs].rearrange("p h (i j) -> p h i j", i=PSEL),
                            tv[:, hs, 0, :].unsqueeze(3).to_broadcast(two), tv[:, hs, 1, :].unsqueeze(2).to_broadcast(two),
                            ALU.add))
                    yield
                    top16([(combo[:, h, :], best[:, t, h, :], pl[:, h, :]) for h in (2 * g, 2 * g + 1)])
                    yield
                    heads, some = slice(4 * g, 4 * g + 4), slice(2 * g * PSEL, (2 * g + 2) * PSEL)
                    step(nc.vector.tensor_copy(top_i[:, heads, :], fv[:, heads, :]))
                    step(TS(spare[:], place[:, some], 4, None, ALU.logical_shift_right))
                    step(nc.vector.tensor_copy(hi[:, 0, some], spare[:]))
                    step(TS(spare[:], place[:, some], 15, None, ALU.bitwise_and))
                    step(nc.vector.tensor_copy(hi[:, 1, some], spare[:]))
                    hot = pick[t].rearrange("p (s n) -> p s n", n=PSEL)
                    hot4 = pick[t].rearrange("p (h s n) -> p h s n", h=2, s=PSEL)
                    if t:
                        v.wait_ge(*emptied("ht1_1"))
                    for a in range(2):
                        step(TT(hot, hi[:, a, some].unsqueeze(2).to_broadcast([P, 2 * PSEL, PSEL]),
                                const("iota16").unsqueeze(1).to_broadcast([P, 2 * PSEL, PSEL]), ALU.is_equal))
                        step(TT(hot4, hot4, ti[:, hs, a, :].unsqueeze(2).to_broadcast(two), ALU.mult))
                        step(nc.vector.tensor_reduce(hid_[:, a, some], hot, AX_X, ALU.add))
                    yield
                step(STT(id_f, hid_[:, 0, :], float(PK), hid_[:, 1, :], ALU.mult, ALU.add))
                step(nc.vector.tensor_copy(ids[:, t * SLOTS:(t + 1) * SLOTS], id_f), sem("ids"))
                bt = best[:, t]
                step(nc.vector.tensor_copy(hsum[:, 0:8], bt[:, :, 0]))
                step(TT(bt, bt, hsum[:, 0:8].unsqueeze(2).to_broadcast([P, PH, PSEL]), ALU.subtract), sem("best"))
                yield

            def gates(t):
                v.wait_ge(sem("best_exp"), t + 1)
                step(nc.vector.tensor_reduce(hsum[:, 0:8], best[:, t], AX_X, ALU.add))
                step(nc.vector.reciprocal(hsum[:, 0:8], hsum[:, 0:8]))
                step(TT(best[:, t], best[:, t], hsum[:, 0:8].unsqueeze(2).to_broadcast([P, PH, PSEL]), ALU.mult))

            def background():
                v.wait_ge(*emptied("ada11"))
                step(TT(mod1[:, 40:48], mod1[:, 40:48], param("b_ada")[:, 40:48], ALU.add))
                yield from choose_experts(1)
                v.wait_ge(*emptied(f"ada2_{MOD_CTX - 1}"))
                m2 = mod2[:].rearrange("p (j s) -> p j s", s=2)[:, 0:4 * MOD_CTX, :]
                step(TT(m2, m2, param("b_ada_2")[:, 0:4 * MOD_CTX].unsqueeze(2).to_broadcast([P, 4 * MOD_CTX, 2]), ALU.add))
                for key, row, s in (("ctx1", 2, 1), ("x1", 2, 0)):
                    step(TS(half_gate[key], mod2_v[:, row, :, s], 0.5, None, ALU.mult))
                v.wait_ge(sem("ctx_landed"), 16)
                modulated("ctx1", ctx_t, h_t, param("norm_ffn1_2"), mod2_v[:, 1, :, 1], mod2_v[:, 0, :, 1])
                yield
                yield from ff_dve("fc", ctx_t, half_gate["ctx1"])
                modulated("ctx2", ctx_t, h_t, param("norm_mix_2"), mod2_v[:, 4, :, 1], mod2_v[:, 3, :, 1])
                yield

            for _ in choose_experts(0):
                pass
            v.wait_ge(*emptied("ks1_3"))
            v.sem_inc(sem("row_free"), GBUF)
            bg = background()
            per_tile = SLOTS // BATCH

            def dot_batch(n):
                for s in range(BATCH):
                    g = n * BATCH + s
                    v.wait_ge(row_landed[g % GBUF], 16 * (g // GBUF + 1))
                    u = rows[g % GBUF][:, 0:D]
                    step(nc.vector.tensor_tensor_reduce(u, u, h2[:, n // per_tile, :], 1.0, 0.0, ALU.mult, ALU.add,
                                                        dots[:, n % 8, s:s + 1]), sem("dots"))

            def sum_batch(n):
                t, b = divmod(n, per_tile)
                v.wait_ge(sem("gelus"), n + 1)
                gate = flat(best[:, t])[:, b * BATCH:(b + 1) * BATCH]
                step(TT(weights[:, n % 8, :], acts[:, n % 8, :], gate, ALU.mult))
                for s in range(BATCH):
                    g = n * BATCH + s
                    STT(y_of[t], rows[g % GBUF][:, D:2 * D], weights[:, n % 8, s:s + 1], y_of[t],
                        ALU.mult, ALU.add).then_inc(sem("row_free"), 1)
                    v.wait_ge(sem("row_free"), GBUF + g + 1)

            for t in range(NT):
                gates(t)
                step(nc.vector.memset(y_of[t], 0.0))
                dot_batch(t * per_tile)
                for b in range(per_tile):
                    n = t * per_tile + b
                    if b + 1 < per_tile:
                        dot_batch(n + 1)
                    sum_batch(n)
                    if b % 2 == 1:
                        next(bg, None)
                step(nc.vector.memset(stat[:, 0:1], 0.0), sem("experts"))
            for _ in bg:
                pass
            for t in range(NT):
                for i in range(2):
                    o = take(f"yt{t}_{i}")
                    for j in range(4):
                        k = 4 * i + j
                        xs = x_t[:, k, t * P:(t + 1) * P]
                        ins = STT(xs, o[:, j * P:(j + 1) * P], mod1[:, 40 + k:41 + k], xs, ALU.mult, ALU.add)
                        if j < 3:
                            step(ins)
                    drain(ins)
            step(nc.vector.memset(stat[:, 0:1], 0.0), sem("experts_added"))
            v.wait_ge(*emptied("kc3"))
            v.wait_ge(*emptied("vc7"))
            v.wait_ge(sem("fade"), 1)
            def fade_keys(n):
                h, a = divmod(n, 2)
                if n >= 4:
                    v.wait_ge(*emptied(f"st{(n - 4) // 2}_{(n - 4) % 2}_1"))
                for t in range(NT):
                    c = (a * NT + t) * RH + h
                    step(TS(k_fade[n % 4][:, t, :], kc[:, t, h * DK:(h + 1) * DK], fade[:, c:c + 1], None, ALU.mult),
                         sem("k_fade") if t == NT - 1 else chain)

            for n in range(4):
                fade_keys(n)
            split_modulated("x1", 2, param("norm_ffn1_2"), mod2_v[:, 1, :, 0], mod2_v[:, 0, :, 0])
            for n in range(4, 2 * RH):
                fade_keys(n)
            split_until(first_pieces + PIECES - 1)
            v.wait_ge(sem("late"), 64)
            split_ff_dve("f1", 0, half_gate["x1"])
            split_modulated("x2", 3, param("norm_mix_2"), mod2_v[:, 4, :, 0], mod2_v[:, 3, :, 0])
            v.wait_ge(*emptied(f"late_mod{MOD_LATE - 1}"))
            late_cols = mod2[:].rearrange("p (j s) -> p j s", s=2)[:, 4 * MOD_CTX:72, 0]
            step(TT(late_cols, late_cols, param("b_ada_2")[:, 4 * MOD_CTX:72], ALU.add))
            step(TS(half_gate["x3"], mod2_v[:, 8, :, 0], 0.5, None, ALU.mult))
            ahead("f3")
            for i in range(4):
                o = take(f"mx{i}")
                v.wait_ge(sem("mixed_hi"), i + 1)
                drain(TT(flat(mixed_lo[:, 2 * i:2 * i + 2, :]), o, flat(mixed_hi[:, 2 * i:2 * i + 2, :]).bitcast(F32),
                         ALU.subtract))
            v.wait_ge(*emptied("gf3"))
            for i in range(4):
                drain(TT(flat(m_t[:, 2 * i:2 * i + 2, :]), flat(sig[:, 2 * i:2 * i + 2, :]), take(f"pf{i}"), ALU.mult))
            cos = rope[:, 0, :].unsqueeze(1).to_broadcast([P, 2, L])
            sin = rope[:, 1, :].unsqueeze(1).to_broadcast([P, 2, L])
            for tag, dst, scale in (("rq", rq_t, DK ** -0.5), ("rk", rk_t, 1.0)):
                for h in range(RH):
                    o = take(f"{tag}{h}").rearrange("p (b t) -> p b t", b=2)
                    d = dst[:, 2 * h:2 * h + 2, :]
                    step(STT(d, o, scale, cos, ALU.mult, ALU.mult))
                    drain(STT(rope_tmp, o, scale, sin, ALU.mult, ALU.mult))
                    step(TT(d[:, 0, :], d[:, 0, :], rope_tmp[:, 1, :], ALU.subtract))
                    step(TT(d[:, 1, :], d[:, 1, :], rope_tmp[:, 0, :], ALU.add))
            ahead("rg7")
            v.wait_ge(*emptied("rv7"))
            v.wait_ge(*emptied("rg7"))
            def split_gated(h):
                v.wait_ge(sem("rg_hi"), h + 1)
                blocks = slice(4 * h, 4 * h + 4)
                rest(rg_lo[:, blocks, :].rearrange("p (a j) t -> p a (j t)", a=2),
                     rg_t[:, blocks, :].rearrange("p (a j) t -> p a (j t)", a=2),
                     rg_hi[:, :, h].rearrange("p a j t -> p a (j t)"), "rg_split")

            def fade_queries(h):
                v.wait_ge(sem("xi"), h + 1)
                for a in range(2):
                    step(TT(q_faded[h % 2][:, a], rq_t[:, 2 * h:2 * h + 2, :],
                            xi[:, a, :].unsqueeze(1).to_broadcast([P, 2, L]), ALU.mult), sem("q_faded") if a else chain)

            def decay_scores(h):
                drain(TT(flat(sc_t[h % 2]), take(f"sc{h}"), flat(decay_t[:, h]), ALU.mult))

            fade_queries(0)
            decay_scores(0)
            for h in range(RH):
                if h + 1 < RH:
                    fade_queries(h + 1)
                for t in range(NT):
                    o = take(f"o{h}_{t}")
                    step(nc.vector.bn_stats(stat[:, 0:6], o))
                    step(nc.vector.bn_aggr(stat[:, 6:8], stat[:, 0:6]))
                    step(TS(stat[:, 8:9], stat[:, 7:8], EPS, None, ALU.add))
                    rooted(stat[:, 8:9])
                    drain(TS(o_n[t], o, stat[:, 6:7], stat[:, 8:9], ALU.subtract, ALU.mult))
                if h + 1 < RH:
                    decay_scores(h + 1)
                if h:
                    split_gated(h - 1)
                for t in range(NT):
                    o = take(f"ot{h}_{t}")
                    for j in range(4):
                        k = 4 * h + j
                        g = rg_t[:, k, t * P:(t + 1) * P]
                        ins = STT(g, o[:, j * P:(j + 1) * P], param("ret_gn_w_2")[:, k:k + 1], g, ALU.mult, ALU.mult)
                        if j < 3:
                            step(ins)
                    drain(ins)
                step(nc.vector.memset(stat[:, 9:10], 0.0), sem("turned"))
            split_gated(RH - 1)
            v.wait_ge(*emptied("ga3"))

            def split_merged(i):
                v.wait_ge(sem("m_hi"), i + 1)
                two = slice(2 * i, 2 * i + 2)
                rest(flat(m_lo[:, two, :]), flat(m_t[:, two, :]), flat(mixed_hi[:, two, :]), "m_split")

            for i in range(4):
                s = flat(sig[:, 2 * i:2 * i + 2, :])
                m = flat(m_t[:, 2 * i:2 * i + 2, :])
                drain(TT(s, s, take(f"pr{i}"), ALU.mult))
                step(TT(m, m, s, ALU.add), sem("merged"))
                if i:
                    split_merged(i - 1)
            split_merged(3)
            residual([f"w2o{i}" for i in range(4)], x_t, mod2_v[:, 5, :, 0], 2)
            split_modulated("x3", 4, param("norm_ffn2_2"), mod2_v[:, 7, :, 0], mod2_v[:, 6, :, 0])
            split_ff_dve("f2", 1, half_gate["x3"])
            root("ss_fin", rstd[:], L, D)
            for k in range(KD):
                step(STT(h_t[:, k, :], x_t[:, k, :], param("norm_final_2")[:, k:k + 1], rstd[:], ALU.mult, ALU.mult),
                     sem("out_ready") if k == KD - 1 else chain)
            assert taken[0] == sum(g[1] == "dve" for g in groups)




def _tiles(w, width):
    k, n = w.shape
    return np.ascontiguousarray(w.reshape(k // P, P, n // width, width).transpose(2, 1, 0, 3)).reshape(
        n // width, P, k // P * width)


def _columns(vec):
    return np.asarray(vec).reshape(-1, P).T


def _feature_major(x):
    return np.ascontiguousarray(np.asarray(x).reshape(L, KD, P).transpose(2, 1, 0)).reshape(P, KD * L)


def _ffn_pairs(w13):
    w = np.asarray(w13)[0]
    w = w.reshape(D, 2, FF // 256, 256).transpose(0, 2, 1, 3).reshape(D, 2 * FF)
    return _tiles(w, 512)


def _pairs_apart(w):
    return w.reshape(D, RH, DK // 2, 2).transpose(0, 1, 3, 2).reshape(D, RH * DK)


def kernel(**inputs):
    import concourse.bacc as bacc
    from concourse.bass_utils import run_bass_kernel_spmd

    a = {k: np.asarray(v) for k, v in inputs.items()}
    early, late = shape_constants()
    w_in = a["w_in"]
    w_in_2 = a["w_in_2"][0]
    order = [3072, 0, 512, 1024, 2048, 2560, 1536]
    ik, iw = w_in[:, 3584:3648], w_in[:, 3648:3656]
    parts = {
        "c": _columns(a["c"]),
        "c2": np.stack([_columns(a["c_2"]), _columns(a["c_ctx_2"])], 2).reshape(P, 16),
        "b_ada": _columns(a["b_ada"]), "b_ada_2": _columns(a["b_ada_2"]),
        "q_norm_w": np.tile(a["q_norm_w"], 2)[:, None], "k_norm_w": np.tile(a["k_norm_w"], 2)[:, None],
        "conv_w": a["conv_w"].reshape(3, KA, P).transpose(2, 0, 1).reshape(P, 12),
        "decay": np.broadcast_to(np.concatenate([a["decay_fwd_2"][0], a["decay_bwd_2"][0]]), (P, 8)),
    }
    params = np.concatenate([parts[n] if n in parts else _columns(a[n]) for n, _ in PARAMS], 1)
    arrays = {
        "params": params, "early": early, "late": late,
        "x": _feature_major(a["x"][0]), "ctx": _feature_major(a["ctx_2"][0]),
        "w_ada": _tiles(a["w_ada"], 512),
        "w_idx": _tiles(np.concatenate([ik, ik, iw], 1), 136),
        "w_in": np.concatenate([_tiles(w_in[:, o:o + 512], 512) for o in order]),
        "w_out": _tiles(a["w_out"], 512), "peer_wq": _tiles(a["peer_wq"], 512),
        "subkeys": a["peer_subkeys"].reshape(2 * PH, PK, P).transpose(2, 0, 1).reshape(1, P, 2 * PH * PK),
        "experts": np.concatenate([a["peer_u"], a["peer_v"]], 1),
        "w_ada_2": _tiles(a["w_ada_2"][0], 512),
        "w13_ffn1": _ffn_pairs(a["w13_ffn1_2"]), "w2_ffn1": _tiles(a["w2_ffn1_2"][0], P),
        "w13_ffn2": _ffn_pairs(a["w13_ffn2_2"]), "w2_ffn2": _tiles(a["w2_ffn2_2"][0], P),
        "w_in_2": _tiles(np.concatenate([_pairs_apart(w_in_2[:, 0:1024]), _pairs_apart(w_in_2[:, 1024:2048]),
                                         w_in_2[:, 2048:]], 1), 512),
        "p_ret": _tiles(a["p_ret_2"][0], 256), "p_four": _tiles(a["p_four_2"][0], 512),
        "w_out_2": _tiles(a["w_out_2"][0], 512),
    }
    nc = bacc.Bacc("TRN2", target_bir_lowering=False, num_devices=1)
    feeds, dram = {}, {}
    for name, array in arrays.items():
        feeds["in_" + name] = np.ascontiguousarray(array)
        dram[name] = nc.dram_tensor("in_" + name, array.shape, F32, kind="ExternalInput").ap()
    out = nc.dram_tensor("out_x", (P, KD * L), F32, kind="ExternalOutput").ap()
    program(nc, dram, out)
    got = run_bass_kernel_spmd(nc, [feeds], core_ids=[0]).results[0]["out_x"]
    return np.ascontiguousarray(np.asarray(got).reshape(P, KD, L).transpose(2, 1, 0)).reshape(1, L, D)
```
